# Optimizing a Trainium2 kernel written in Bass

```python
import math
import jax
import jax.numpy as jnp
from jax import lax
import numpy as np

"""One inference step (prompt group + sample group, shared weights) of a 2-layer hybrid decoder trunk.

Per layer:  h = RMSNorm(x)
            z = h @ w_in   (one combined projection, columns partitioned among all mixers + merge gates)
            A = S5 diagonal complex SSM (24 groups x 16 ch, 64 complex states per group) + GLU
            B = native sparse attention: compressed blocks / gathered top-k selected blocks / sliding window,
                each branch with its own K/V, ALiBi distance penalty, per-head sigmoid branch gates
            C = short gated conv: B * conv3(C * xin)
            x = x + W_o( sum_b sigmoid(gate_b) * P_b(branch_b) )
            x = x + HierMoE(RMSNorm(x))   (top-1 expert group, then top-2 experts inside it)
Final RMSNorm.

Inputs:
  x_prompt   (BATCH, SEQ, D_MODEL)              positions 0..SEQ-1
  x_sample   (DEC_BATCH, DEC_SEQ, D_MODEL)      positions PAST_LEN..PAST_LEN+DEC_SEQ-1
  cache_kv   (DEPTH, N_POOL, PAGE_SIZE, 4, KV_HEADS, HEAD_DIM)  paged rows [k_cmp, v_cmp, k_slc, v_slc]
  page_table (DEC_BATCH, PAST_LEN // PAGE_SIZE) int32  logical -> physical page
  cache_win  (DEPTH, DEC_BATCH, min(WINDOW, PAST_LEN), 2, KV_HEADS, HEAD_DIM)  last window rows [k_win, v_win]
  state_ssm  (DEPTH, DEC_BATCH, SSM_GROUPS, SSM_STATE, 2)  S5 complex state (re, im)
  state_conv (DEPTH, DEC_BATCH, CONV_WIDTH - 1, CONV_DIM)  last conv-input rows
  then the weights (leading DEPTH axis, except norm_final_g).
Output tuple:
  y_prompt    (BATCH, SEQ, D_MODEL)
  y_sample    (DEC_BATCH, DEC_SEQ, D_MODEL)
  kv_prompt   (DEPTH, BATCH, SEQ, 4, KV_HEADS, HEAD_DIM)          new paged-cache rows
  kv_sample   (DEPTH, DEC_BATCH, DEC_SEQ, 4, KV_HEADS, HEAD_DIM)
  win_prompt  (DEPTH, BATCH, min(WINDOW, SEQ), 2, KV_HEADS, HEAD_DIM)      window buffer after the prompt
  win_sample  (DEPTH, DEC_BATCH, min(WINDOW, min(WINDOW, PAST_LEN) + DEC_SEQ), 2, KV_HEADS, HEAD_DIM)
  ssm_prompt  (DEPTH, BATCH, SSM_GROUPS, SSM_STATE, 2)
  ssm_sample  (DEPTH, DEC_BATCH, SSM_GROUPS, SSM_STATE, 2)
  conv_prompt (DEPTH, BATCH, CONV_WIDTH - 1, CONV_DIM)
  conv_sample (DEPTH, DEC_BATCH, CONV_WIDTH - 1, CONV_DIM)
"""

D_MODEL = 1024
BATCH = 1
SEQ = 512
DEPTH = 1
DEC_BATCH = 8
DEC_SEQ = 1
PAST_LEN = 4096
PAGE_SIZE = 128

SSM_GROUP_CH = 16
SSM_GROUPS = 24
SSM_DIM = SSM_GROUPS * SSM_GROUP_CH
SSM_STATE = 64
N_HEADS = 8
HEAD_DIM = 64
KV_HEADS = 2
ATTN_DIM = N_HEADS * HEAD_DIM
KV_DIM = KV_HEADS * HEAD_DIM
CMP_BLOCK = 32
CMP_HIDDEN = 64
SEL_BLOCK = 64
N_SELECT = 8
WINDOW = 512
QUERY_BLOCK = 128
FORCE_BONUS = 1e4
CONV_DIM = 384
CONV_WIDTH = 3
N_EXPERT_GROUPS = 4
EXPERTS_PER_GROUP = 4
N_EXPERTS = N_EXPERT_GROUPS * EXPERTS_PER_GROUP
TOP_K = 2
D_FF_EXPERT = 256
RMS_EPS = 1e-6
N_IN = SSM_DIM + ATTN_DIM + 6 * KV_DIM + 3 * N_HEADS + 3 * CONV_DIM + 3 * D_MODEL

kernel_name = "hybrid_s5_nsa_shortconv_hiermoe_step"

def rms_norm(x, g):
    x32 = x.astype(jnp.float32)
    y = x32 * lax.rsqrt(jnp.mean(x32 * x32, axis=-1, keepdims=True) + RMS_EPS)
    return (y * g.astype(jnp.float32)).astype(x.dtype)

def masked_softmax(s, mask):
    s = jnp.where(mask, s, -jnp.inf)
    m = jnp.max(s, axis=-1, keepdims=True)
    m = jnp.where(jnp.isfinite(m), m, 0.0)
    e = jnp.where(mask, jnp.exp(s - m), 0.0)
    return e / jnp.maximum(jnp.sum(e, axis=-1, keepdims=True), 1.0)

def alibi_slopes():
    return 2.0 ** (-8.0 * jnp.arange(1, N_HEADS + 1, dtype=jnp.float32) / N_HEADS)

def complex_affine_combine(e1, e2):
    ar1, ai1, br1, bi1 = e1
    ar2, ai2, br2, bi2 = e2
    return (ar1 * ar2 - ai1 * ai2,
            ar1 * ai2 + ai1 * ar2,
            ar2 * br1 - ai2 * bi1 + br2,
            ar2 * bi1 + ai2 * br1 + bi2)

def s5_branch(u, h0, a_re, a_im, log_dt, b_re, b_im, c_re, c_im, d_skip, w_glu, b_glu):
    f32 = jnp.float32
    bsz, seq = u.shape[:2]
    u32 = u.astype(f32)
    ug = u32.reshape(bsz, seq, SSM_GROUPS, SSM_GROUP_CH)
    ar = a_re.astype(f32)
    ai = a_im.astype(f32)
    dt = jnp.exp(log_dt.astype(f32))[:, None]
    mag = jnp.exp(ar * dt)
    abar_re = mag * jnp.cos(ai * dt)
    abar_im = mag * jnp.sin(ai * dt)
    den = ar * ar + ai * ai
    coef_re = ((abar_re - 1.0) * ar + abar_im * ai) / den
    coef_im = (abar_im * ar - (abar_re - 1.0) * ai) / den
    br = b_re.astype(f32)
    bi = b_im.astype(f32)
    bbar_re = coef_re[..., None] * br - coef_im[..., None] * bi
    bbar_im = coef_re[..., None] * bi + coef_im[..., None] * br
    bu_re = jnp.einsum('blgc,gpc->blgp', ug, bbar_re)
    bu_im = jnp.einsum('blgc,gpc->blgp', ug, bbar_im)
    h0r = h0[..., 0].astype(f32)
    h0i = h0[..., 1].astype(f32)
    bu_re = bu_re.at[:, 0].add(abar_re * h0r - abar_im * h0i)
    bu_im = bu_im.at[:, 0].add(abar_re * h0i + abar_im * h0r)
    a_r = jnp.broadcast_to(abar_re, bu_re.shape)
    a_i = jnp.broadcast_to(abar_im, bu_im.shape)
    _, _, hr, hi = lax.associative_scan(complex_affine_combine, (a_r, a_i, bu_re, bu_im), axis=1)
    y = (jnp.einsum('blgp,gcp->blgc', hr, c_re.astype(f32))
         - jnp.einsum('blgp,gcp->blgc', hi, c_im.astype(f32)))
    y = y.reshape(bsz, seq, SSM_DIM) + d_skip.astype(f32) * u32
    g = jax.nn.gelu(y)
    out = g * jax.nn.sigmoid(g @ w_glu.astype(f32) + b_glu.astype(f32))
    h_last = jnp.stack([hr[:, -1], hi[:, -1]], axis=-1)
    return out.astype(u.dtype), h_last.astype(h0.dtype)

def compress_blocks(k, pe, w1, w2):
    bsz, lk, kvh, hd = k.shape
    nc = lk // CMP_BLOCK
    blocks = k.reshape(bsz, nc, CMP_BLOCK, kvh, hd) + pe[None, None, :, None, :]
    flat = blocks.transpose(0, 1, 3, 2, 4).reshape(bsz, nc, kvh, CMP_BLOCK * hd)
    return jax.nn.gelu(flat @ w1) @ w2

def nsa_branch(q, gate_logits, kv_all, win_all, pos0, p0_win, cmp_pe, cmp_w1, cmp_w2):
    f32 = jnp.float32
    bsz, seq = q.shape[:2]
    grp = N_HEADS // KV_HEADS
    scale = HEAD_DIM ** -0.5
    qpos = pos0 + jnp.arange(seq, dtype=jnp.int32)
    slopes = alibi_slopes().reshape(KV_HEADS, grp)
    q5 = q.reshape(bsz, seq, KV_HEADS, grp, HEAD_DIM)

    pad = (-kv_all.shape[1]) % SEL_BLOCK
    kv = jnp.pad(kv_all, ((0, 0), (0, pad), (0, 0), (0, 0), (0, 0)))
    k_cmp, v_cmp, k_slc, v_slc = kv[:, :, 0], kv[:, :, 1], kv[:, :, 2], kv[:, :, 3]

    kc = compress_blocks(k_cmp, cmp_pe[0], cmp_w1[0], cmp_w2[0])
    vc = compress_blocks(v_cmp, cmp_pe[1], cmp_w1[1], cmp_w2[1])
    n_cmp = kc.shape[1]
    n_sel_blocks = n_cmp // (SEL_BLOCK // CMP_BLOCK)
    cend = (jnp.arange(n_cmp, dtype=jnp.int32) + 1) * CMP_BLOCK - 1
    dist_c = qpos[:, None] - cend[None, :]
    s = (jnp.einsum('blgmd,bcgd->blgmc', q5, kc).astype(f32) * scale
         - slopes[None, None, :, :, None] * dist_c.astype(f32)[None, :, None, None, :])
    p_cmp = masked_softmax(s, (dist_c >= 0)[None, :, None, None, :])
    o_cmp = jnp.einsum('blgmc,bcgd->blgmd', p_cmp.astype(vc.dtype), vc)

    imp = p_cmp.sum(axis=3).reshape(bsz, seq, KV_HEADS, n_sel_blocks, -1).sum(-1)
    blk = jnp.arange(n_sel_blocks, dtype=jnp.int32)[None, :]
    cur = (qpos // SEL_BLOCK)[:, None]
    forced = ((blk == 0) | (blk == cur) | (blk == cur - 1)).astype(f32)
    causal_blk = blk * SEL_BLOCK <= qpos[:, None]
    score = jnp.where(causal_blk[None, :, None, :], imp + FORCE_BONUS * forced[None, :, None, :], -jnp.inf)
    n_sel = min(N_SELECT, n_sel_blocks)
    _, sel_idx = lax.top_k(score, n_sel)

    ks_t = k_slc.reshape(bsz, n_sel_blocks, SEL_BLOCK, KV_HEADS, HEAD_DIM).transpose(0, 3, 1, 2, 4)
    vs_t = v_slc.reshape(bsz, n_sel_blocks, SEL_BLOCK, KV_HEADS, HEAD_DIM).transpose(0, 3, 1, 2, 4)
    win_pad = jnp.pad(win_all, ((0, 0), (WINDOW, 0), (0, 0), (0, 0), (0, 0)))
    kw, vw = win_pad[:, :, 0], win_pad[:, :, 1]

    qb = QUERY_BLOCK if seq % QUERY_BLOCK == 0 else seq
    nb = seq // qb
    q_blocks = q5.reshape(bsz, nb, qb, KV_HEADS, grp, HEAD_DIM).swapaxes(0, 1)
    idx_blocks = sel_idx.reshape(bsz, nb, qb, KV_HEADS, n_sel).swapaxes(0, 1)
    pos_blocks = qpos.reshape(nb, qb)
    b_ix = jnp.arange(bsz)[:, None, None, None]
    g_ix = jnp.arange(KV_HEADS)[None, None, :, None]
    n_keys_sel = n_sel * SEL_BLOCK

    def block_fn(args):
        qblk, iblk, pblk = args
        kg = ks_t[b_ix, g_ix, iblk].reshape(bsz, qb, KV_HEADS, n_keys_sel, HEAD_DIM)
        vg = vs_t[b_ix, g_ix, iblk].reshape(bsz, qb, KV_HEADS, n_keys_sel, HEAD_DIM)
        kpos = (iblk[..., None] * SEL_BLOCK + jnp.arange(SEL_BLOCK, dtype=jnp.int32)).reshape(bsz, qb, KV_HEADS, n_keys_sel)
        d_s = pblk[None, :, None, None] - kpos
        s1 = (jnp.einsum('bqgmd,bqgkd->bqgmk', qblk, kg).astype(f32) * scale
              - slopes[None, None, :, :, None] * d_s.astype(f32)[:, :, :, None, :])
        p1 = masked_softmax(s1, (d_s >= 0)[:, :, :, None, :])
        o_slc = jnp.einsum('bqgmk,bqgkd->bqgmd', p1.astype(vg.dtype), vg)
        start = pblk[0] - p0_win
        kwb = lax.dynamic_slice_in_dim(kw, start, qb + WINDOW, axis=1)
        vwb = lax.dynamic_slice_in_dim(vw, start, qb + WINDOW, axis=1)
        kpos_w = pblk[0] - WINDOW + jnp.arange(qb + WINDOW, dtype=jnp.int32)
        d_w = pblk[:, None] - kpos_w[None, :]
        mask_w = (kpos_w[None, :] >= p0_win) & (d_w >= 0) & (d_w < WINDOW)
        s2 = (jnp.einsum('bqgmd,bkgd->bqgmk', qblk, kwb).astype(f32) * scale
              - slopes[None, None, :, :, None] * d_w.astype(f32)[None, :, None, None, :])
        p2 = masked_softmax(s2, mask_w[None, :, None, None, :])
        o_win = jnp.einsum('bqgmk,bkgd->bqgmd', p2.astype(vwb.dtype), vwb)
        return o_slc, o_win

    o_slc, o_win = lax.map(block_fn, (q_blocks, idx_blocks, pos_blocks))
    o_slc = o_slc.swapaxes(0, 1).reshape(bsz, seq, KV_HEADS, grp, HEAD_DIM)
    o_win = o_win.swapaxes(0, 1).reshape(bsz, seq, KV_HEADS, grp, HEAD_DIM)
    gates = jax.nn.sigmoid(gate_logits.astype(f32)).reshape(bsz, seq, 3, KV_HEADS, grp)[..., None]
    o = gates[:, :, 0] * o_cmp + gates[:, :, 1] * o_slc + gates[:, :, 2] * o_win
    return o.reshape(bsz, seq, ATTN_DIM).astype(q.dtype)

def short_conv_branch(gate_b, gate_c, x_in, conv_prev, conv_w):
    seq = x_in.shape[1]
    u = gate_c * x_in
    up = jnp.concatenate([conv_prev.astype(u.dtype), u], axis=1)
    y = sum(conv_w[j] * up[:, j:j + seq] for j in range(CONV_WIDTH))
    return gate_b * y, up[:, -(CONV_WIDTH - 1):]

def token_mixers(h, pos0, kv_past, win_past, ssm_h0, conv_prev, w_in, a_re, a_im, log_dt,
                 b_re, b_im, c_re, c_im, d_skip, w_glu, b_glu, cmp_pe, cmp_w1, cmp_w2, conv_w,
                 w_br_ssm, w_br_attn, w_br_conv, w_out):
    bsz, seq, _ = h.shape
    sizes = (SSM_DIM, ATTN_DIM, 4 * KV_DIM, 2 * KV_DIM, 3 * N_HEADS, CONV_DIM, CONV_DIM, CONV_DIM, 3 * D_MODEL)
    cuts = [int(c) for c in np.cumsum(sizes)[:-1]]
    z = h @ w_in
    u_ssm, q, kv_paged, kv_win, nsa_gates, conv_b, conv_c, conv_x, merge = jnp.split(z, cuts, axis=-1)

    y_ssm, h_last = s5_branch(u_ssm, ssm_h0, a_re, a_im, log_dt, b_re, b_im, c_re, c_im, d_skip, w_glu, b_glu)

    kv_new = kv_paged.reshape(bsz, seq, 4, KV_HEADS, HEAD_DIM)
    win_new = kv_win.reshape(bsz, seq, 2, KV_HEADS, HEAD_DIM)
    kv_all = jnp.concatenate([kv_past.astype(h.dtype), kv_new], axis=1)
    win_all = jnp.concatenate([win_past.astype(h.dtype), win_new], axis=1)
    y_attn = nsa_branch(q.reshape(bsz, seq, N_HEADS, HEAD_DIM), nsa_gates, kv_all, win_all,
                        pos0, pos0 - win_past.shape[1], cmp_pe, cmp_w1, cmp_w2)

    y_conv, conv_last = short_conv_branch(conv_b, conv_c, conv_x, conv_prev, conv_w)

    g = jax.nn.sigmoid(merge.astype(jnp.float32)).astype(h.dtype)
    g_ssm, g_attn, g_conv = jnp.split(g, 3, axis=-1)
    merged = g_ssm * (y_ssm @ w_br_ssm) + g_attn * (y_attn @ w_br_attn) + g_conv * (y_conv @ w_br_conv)
    win_state = win_all[:, -min(WINDOW, win_all.shape[1]):]
    return merged @ w_out, kv_new, win_state, h_last, conv_last

def hier_moe(h, w_rg, b_rg, w_re, b_re, w_gate, w_up, w_down):
    f32 = jnp.float32
    bsz, seq, dm = h.shape
    t = h.reshape(-1, dm)
    n_tok = t.shape[0]
    lg = (t @ w_rg).astype(f32) + b_rg.astype(f32)
    pg = jax.nn.softmax(lg, axis=-1)
    gsel = jnp.argmax(lg, axis=-1)
    gw = jnp.max(pg, axis=-1)
    le = ((t @ w_re).astype(f32) + b_re.astype(f32)).reshape(n_tok, N_EXPERT_GROUPS, EXPERTS_PER_GROUP)
    le_sel = le[jnp.arange(n_tok), gsel]
    pe = jax.nn.softmax(le_sel, axis=-1)
    top_v, top_i = lax.top_k(pe, TOP_K)
    wts = top_v / jnp.sum(top_v, axis=-1, keepdims=True) * gw[:, None]
    eid = gsel[:, None] * EXPERTS_PER_GROUP + top_i
    comb = jnp.sum(jax.nn.one_hot(eid, N_EXPERTS, dtype=f32) * wts[..., None], axis=1)
    hg = jnp.einsum('nd,edf->nef', t, w_gate)
    hu = jnp.einsum('nd,edf->nef', t, w_up)
    act = jax.nn.silu(hg) * hu * comb[:, :, None].astype(t.dtype)
    y = jnp.einsum('nef,efd->nd', act, w_down)
    return y.reshape(bsz, seq, dm)

def setup_inputs(seed: int = 0) -> dict:
    key = jax.random.key(seed)
    ks = iter(jax.random.split(key, 48))
    f32 = jnp.float32

    def nrm(shape, scale):
        return scale * jax.random.normal(next(ks), shape, f32)

    n_pages = PAST_LEN // PAGE_SIZE
    n_used = DEC_BATCH * n_pages
    n_pool = n_used + max(1, n_used // 4)
    win_buf = min(WINDOW, PAST_LEN)
    n_idx = jnp.arange(SSM_STATE, dtype=f32)
    return {
        'x_prompt': nrm((BATCH, SEQ, D_MODEL), 1.0),
        'x_sample': nrm((DEC_BATCH, DEC_SEQ, D_MODEL), 1.0),
        'cache_kv': nrm((DEPTH, n_pool, PAGE_SIZE, 4, KV_HEADS, HEAD_DIM), 1.0),
        'page_table': jax.random.permutation(next(ks), n_pool)[:n_used].reshape(DEC_BATCH, n_pages).astype(jnp.int32),
        'cache_win': nrm((DEPTH, DEC_BATCH, win_buf, 2, KV_HEADS, HEAD_DIM), 1.0),
        'state_ssm': nrm((DEPTH, DEC_BATCH, SSM_GROUPS, SSM_STATE, 2), 0.5),
        'state_conv': nrm((DEPTH, DEC_BATCH, CONV_WIDTH - 1, CONV_DIM), 1.0),
        'norm_attn_g': 1.0 + nrm((DEPTH, D_MODEL), 0.01),
        'w_in': nrm((DEPTH, D_MODEL, N_IN), D_MODEL ** -0.5),
        'ssm_a_re': -0.5 + nrm((DEPTH, SSM_GROUPS, SSM_STATE), 0.01),
        'ssm_a_im': math.pi * n_idx + nrm((DEPTH, SSM_GROUPS, SSM_STATE), 0.01),
        'ssm_log_dt': jax.random.uniform(next(ks), (DEPTH, SSM_GROUPS), f32, math.log(1e-3), math.log(1e-1)),
        'ssm_b_re': nrm((DEPTH, SSM_GROUPS, SSM_STATE, SSM_GROUP_CH), (2 * SSM_GROUP_CH) ** -0.5),
        'ssm_b_im': nrm((DEPTH, SSM_GROUPS, SSM_STATE, SSM_GROUP_CH), (2 * SSM_GROUP_CH) ** -0.5),
        'ssm_c_re': nrm((DEPTH, SSM_GROUPS, SSM_GROUP_CH, SSM_STATE), SSM_STATE ** -0.5),
        'ssm_c_im': nrm((DEPTH, SSM_GROUPS, SSM_GROUP_CH, SSM_STATE), SSM_STATE ** -0.5),
        'ssm_d': nrm((DEPTH, SSM_DIM), 1.0),
        'ssm_w_glu': nrm((DEPTH, SSM_DIM, SSM_DIM), SSM_DIM ** -0.5),
        'ssm_b_glu': nrm((DEPTH, SSM_DIM), 0.01),
        'cmp_pe': nrm((DEPTH, 2, CMP_BLOCK, HEAD_DIM), 0.02),
        'cmp_w1': nrm((DEPTH, 2, CMP_BLOCK * HEAD_DIM, CMP_HIDDEN), (CMP_BLOCK * HEAD_DIM) ** -0.5),
        'cmp_w2': nrm((DEPTH, 2, CMP_HIDDEN, HEAD_DIM), CMP_HIDDEN ** -0.5),
        'conv_w': nrm((DEPTH, CONV_WIDTH, CONV_DIM), CONV_WIDTH ** -0.5),
        'w_br_ssm': nrm((DEPTH, SSM_DIM, D_MODEL), SSM_DIM ** -0.5),
        'w_br_attn': nrm((DEPTH, ATTN_DIM, D_MODEL), ATTN_DIM ** -0.5),
        'w_br_conv': nrm((DEPTH, CONV_DIM, D_MODEL), CONV_DIM ** -0.5),
        'w_out': nrm((DEPTH, D_MODEL, D_MODEL), D_MODEL ** -0.5),
        'norm_ffn_g': 1.0 + nrm((DEPTH, D_MODEL), 0.01),
        'w_router_group': nrm((DEPTH, D_MODEL, N_EXPERT_GROUPS), D_MODEL ** -0.5),
        'b_router_group': nrm((DEPTH, N_EXPERT_GROUPS), 0.01),
        'w_router_expert': nrm((DEPTH, D_MODEL, N_EXPERTS), D_MODEL ** -0.5),
        'b_router_expert': nrm((DEPTH, N_EXPERTS), 0.01),
        'moe_w_gate': nrm((DEPTH, N_EXPERTS, D_MODEL, D_FF_EXPERT), D_MODEL ** -0.5),
        'moe_w_up': nrm((DEPTH, N_EXPERTS, D_MODEL, D_FF_EXPERT), D_MODEL ** -0.5),
        'moe_w_down': nrm((DEPTH, N_EXPERTS, D_FF_EXPERT, D_MODEL), D_FF_EXPERT ** -0.5),
        'norm_final_g': 1.0 + nrm((D_MODEL,), 0.01),
    }

def reference(x_prompt, x_sample, cache_kv, page_table, cache_win, state_ssm, state_conv,
              norm_attn_g, w_in, ssm_a_re, ssm_a_im, ssm_log_dt, ssm_b_re, ssm_b_im, ssm_c_re, ssm_c_im,
              ssm_d, ssm_w_glu, ssm_b_glu, cmp_pe, cmp_w1, cmp_w2, conv_w, w_br_ssm, w_br_attn, w_br_conv,
              w_out, norm_ffn_g, w_router_group, b_router_group, w_router_expert, b_router_expert,
              moe_w_gate, moe_w_up, moe_w_down, norm_final_g):

    def run(x, pos0, kv_past_of, win_past, ssm_h0, conv_prev):
        kv_rows, win_rows, ssm_rows, conv_rows = [], [], [], []
        for l in range(DEPTH):
            h = rms_norm(x, norm_attn_g[l])
            mix, kv_new, win_state, h_last, conv_last = token_mixers(
                h, pos0, kv_past_of(l), win_past[l], ssm_h0[l], conv_prev[l], w_in[l],
                ssm_a_re[l], ssm_a_im[l], ssm_log_dt[l], ssm_b_re[l], ssm_b_im[l], ssm_c_re[l], ssm_c_im[l],
                ssm_d[l], ssm_w_glu[l], ssm_b_glu[l], cmp_pe[l], cmp_w1[l], cmp_w2[l], conv_w[l],
                w_br_ssm[l], w_br_attn[l], w_br_conv[l], w_out[l])
            x = x + mix
            x = x + hier_moe(rms_norm(x, norm_ffn_g[l]), w_router_group[l], b_router_group[l],
                             w_router_expert[l], b_router_expert[l], moe_w_gate[l], moe_w_up[l], moe_w_down[l])
            kv_rows.append(kv_new)
            win_rows.append(win_state)
            ssm_rows.append(h_last)
            conv_rows.append(conv_last)
        return (rms_norm(x, norm_final_g), jnp.stack(kv_rows), jnp.stack(win_rows),
                jnp.stack(ssm_rows), jnp.stack(conv_rows))

    bp = x_prompt.shape[0]
    dt = x_prompt.dtype
    y_prompt, kv_prompt, win_prompt, ssm_prompt, conv_prompt = run(
        x_prompt, 0,
        lambda l: jnp.zeros((bp, 0, 4, KV_HEADS, HEAD_DIM), dt),
        jnp.zeros((DEPTH, bp, 0, 2, KV_HEADS, HEAD_DIM), dt),
        jnp.zeros((DEPTH, bp, SSM_GROUPS, SSM_STATE, 2), dt),
        jnp.zeros((DEPTH, bp, CONV_WIDTH - 1, CONV_DIM), dt))

    bs = x_sample.shape[0]
    past_len = page_table.shape[1] * PAGE_SIZE
    y_sample, kv_sample, win_sample, ssm_sample, conv_sample = run(
        x_sample, past_len,
        lambda l: cache_kv[l][page_table].reshape(bs, past_len, 4, KV_HEADS, HEAD_DIM),
        cache_win, state_ssm, state_conv)

    return (y_prompt, y_sample, kv_prompt, kv_sample, win_prompt, win_sample,
            ssm_prompt, ssm_sample, conv_prompt, conv_sample)


_drawn_inputs = setup_inputs


def setup_inputs(seed=0):
    import zlib

    import numpy as np

    out = dict(_drawn_inputs(seed))
    spreads = {}
    factors = {'norm_attn_g': 3.571,
     'ssm_a_re': 15.737,
     'ssm_b_glu': 64.0,
     'cmp_pe': 47.464,
     'norm_ffn_g': 25.224,
     'b_router_group': 15.562,
     'b_router_expert': 44.36,
     'norm_final_g': 34.695}
    for name, (base, spread) in spreads.items():
        noise = np.random.default_rng([zlib.crc32(name.encode()), seed]).standard_normal(out[name].shape)
        drawn = base * np.exp(spread * noise) if base else spread * noise
        out[name] = jnp.asarray(drawn.astype(out[name].dtype))
    for name, factor in factors.items():
        out[name] = (out[name] * factor).astype(out[name].dtype)
    return out
```

```python
from contextlib import ExitStack

import numpy as np
import concourse.bass as bass
from concourse import mybir
from concourse.alu_op_type import AluOpType as ALU

F32 = mybir.dt.float32
I32 = mybir.dt.int32
U32 = mybir.dt.uint32
ACT = mybir.ActivationFunctionType
AX_X = mybir.AxisListType.X

P = 128
D = 1024
KD = D // P
SEQ = 512
NB = 8
T = SEQ + NB
HALF = T // 2
PAST = 4096
PAGE = 128
PAGES = PAST // PAGE
HD = 64
HEADS = 8
KVH = 2
GRP = HEADS // KVH
CB = 32
NCB = PAST // CB
SELB = 64
WINDOW = 512
SLOTS = 8
SG = 24
SC = 16
ST = SG * SC // P
SN = SG * 64 // P
N_EXP = 16
FF = 256
EPS = 1e-6
TURN = 4096
SIN_SCALE = 6.2831850
HUGE = 1e30

N_POOL = 320
N_STORED = 3
BRANCH_K = (3, 3, 4)

Z_U, Z_Q, Z_KV, Z_CB, Z_CC, Z_CX = 0, 3, 7, 13, 16, 19
NZ = 22
CHUNKS = ((0, HALF), (HALF, T))


def cody_waite(x, bits):
    parts = []
    for _ in range(2):
        m, e = np.frexp(x)
        part = float(np.ldexp(np.round(m * 2.0**bits), e - bits))
        parts.append(part)
        x = x - part
    return parts + [float(x)]


class Chain:

    def __init__(self, engine, sem):
        self.engine, self.sem, self.n = engine, sem, 0

    def __call__(self, ins):
        self.n += 1
        ins.then_inc(self.sem, 1)
        self.engine.wait_ge(self.sem, self.n)


def constants():
    p = np.arange(P)
    slope = 2.0 ** -(1.0 + np.arange(HEADS))
    by_pos = np.array([slope[m + GRP * g] for m in range(GRP) for g in range(KVH)])
    q, j = np.arange(P)[:, None], np.arange(SEQ)[None]
    dist = (q - j + SEQ - P).astype(np.float64)
    t = (np.arange(4)[None, :, None, None] * P + p[:, None, None, None])
    dc = t - (CB * np.arange(16) + CB - 1.0)
    b, g, c = p // 16, p // 8 % 2, p % 8
    factor = np.where(g == 0, 1.0, 2.0**-GRP)
    at = np.arange(SELB)
    h64 = np.arange(64)
    force = np.zeros((16, SELB))
    force[:, [0, PAST // SELB - 1]] = 1e4
    keys = np.arange(24)
    return {
        "ident": np.eye(P),
        "dist": np.where(dist >= 0, dist, HUGE),
        "bias_p": np.where(dc >= 0, -by_pos[:, None] * dc, -HUGE).reshape(P, 512),
        "valid_p": (dc >= 0).reshape(P, 64),
        "blocks": (p[:, None] // 16 == np.arange(512)[None] // HD),
        "rep_c": (np.arange(16)[:, None] == p[None] % 16),
        "bias_s": -slope[h64 % 8][:, None] * (PAST - (CB * np.arange(NCB) + CB - 1.0)),
        "sum_g": (h64[:, None] // 4 == np.arange(16)[None]),
        "force": force,
        "rep16": (np.arange(16)[:, None] == p[None] // 8),
        "rep8": (np.arange(8)[:, None] == p[None] // 16),
        "slot": (c[:, None] == np.arange(8)),
        "iota": np.tile(np.arange(PAGES), (P, 1)),
        "group": np.stack([g, g == 0, g == 1], 1),
        "npos": np.tile(-at, (P, 1)),
        "rank": np.tile([4.0, 3.0, 2.0, 1.0], (P, 1)),
        "keep": np.where(c < 7, factor, 0.0)[:, None],
        "add7": np.where((c[:, None] == 7) & (at > 0), HUGE, 0.0),
        "dist_w": factor[:, None] * (WINDOW - 1 - SELB * c[:, None] - at),
        "sel_g": (np.arange(KVH)[None, :, None] == g[:, None, None]) & (np.arange(NB) == b[:, None, None]),
        "gate_k": (keys[:, None, None] // 8 == np.arange(3)[:, None]) & (keys[:, None, None] % 4 == np.arange(GRP)),
        "gate_g": (keys[:, None] // 4 % 2 == p[None] // HD),
    }


def pack():
    at, n, rows_ = {}, 0, {}
    for name, v in constants().items():
        v = v.reshape(v.shape[0], -1).astype(np.float32)
        at[name], rows_[name] = (n, n + v.shape[1]), v
        n += v.shape[1]
    out = np.zeros((P, n), np.float32)
    for name, (a, b) in at.items():
        out[0:rows_[name].shape[0], a:b] = rows_[name]
    return at, n, out


CST, CST_N, CST_ARRAY = pack()


def build(nc, io):
    ctx = ExitStack()
    with ctx:
        def sb(name, shape, dt=F32):
            return ctx.enter_context(nc.sbuf_tensor(name, shape, dt))

        def sem(name):
            return ctx.enter_context(nc.semaphore(name))

        bank = [ctx.enter_context(nc.psum_tensor(f"bank{i}", [P, 512], F32)) for i in range(8)]
        H = sb("H", [P, KD, T])
        Z = sb("Z", [P, NZ, T])
        W_RING = sb("W_RING", [P, 2, KD, P])
        CMP = sb("CMP", [P, 2, PAGES * 256])
        X = CMP[:, 1, 0:KD * T].rearrange("p (k t) -> p k t", k=KD)
        WORK = sb("WORK", [P, 12, 512])
        TWICE = sb("TWICE", [P, 3200])
        tvec = TWICE[:, 0:SEQ]
        w_glu = TWICE[:, 512:1664].rearrange("p (k n) -> p k n", k=ST)
        BT = TWICE[:, 1664:2432].rearrange("p (c r n) -> p c r n", c=ST, r=2)
        CT = TWICE[:, 2432:3200].rearrange("p (i r n) -> p i r n", i=SN, r=2)
        VC = TWICE[:, 0:1024].rearrange("p (b n) -> p b n", b=NB)
        CB2 = TWICE[:, 1024:2064].rearrange("p (e t) -> p e t", e=2)
        QN = TWICE[0:NB, 2064:2576]
        sm = TWICE[:, 2576:3088]
        ones = sb("ones", [P, P])
        gains = sb("gains", [P, 3, KD])
        rstd = sb("rstd", [P, T])
        epsb = sb("epsb", [P, 1])
        halfpi = sb("halfpi", [P, 1])
        prm = sb("prm", [P, 3, SN])
        spar = sb("spar", [P, 24, SN])
        spi = sb("spi", [P, SN], I32)
        h0 = sb("h0", [P, SN, 2, NB])
        hlast = sb("hlast", [P, SN, 2, NB + 1])
        RIs = sb("RIs", [P, SN, 2, NB])
        stmp = sb("stmp", [P, 2, SN, NB])
        sdb = sb("sdb", [P, 2, ST])
        cw = sb("cw", [P, ST, 3])
        cprev = sb("cprev", [P, ST, 2, NB])
        clast = sb("clast", [P, ST, 2, NB + 1])
        wgt = sb("wgt", [P, KD, 24])
        Gt = sb("Gt", [24, T])

        cst = sb("cst", [P, CST_N])
        AUX = sb("AUX", [P, 4 * T])
        w1 = AUX[:, 0:2048].rearrange("p (v r h) -> p v r h", v=2, r=16)
        w2 = sb("w2", [P, 2, HD])
        pe_t = sb("pe_t", [P, 2, 16])
        cbias = sb("cbias", [P, 1])
        kcp = sb("kcp", [P, 16])
        vcp = sb("vcp", [16, P])
        Gn = sb("Gn", [P, 4, 24])
        nmax = sb("nmax", [P, 64])
        lsum = sb("lsum", [P, 64])
        cmax = sb("cmax", [P, 32])
        csum = sb("csum", [P, 32])
        wts = sb("wts", [P, 3, HEADS])
        ptab = sb("ptab", [1, NB * PAGES], I32)
        pt8 = sb("pt8", [NB, PAGES], I32)
        pt8f = sb("pt8f", [NB, PAGES])
        smi = sb("smi", [16, SLOTS], U32)
        rowi = sb("rowi", [P, 4], I32)
        small = sb("small", [P, 256])
        stat = sb("stat", [P, 2, 2 * GRP])
        stW = sb("stW", [2 * GRP, 3, 16])
        wn = sb("wn", [P, 2 * GRP])
        gmask = sb("gmask", [24, 12, NB])
        gbc = sb("gbc", [P, 3, GRP, NB])
        ya = sb("ya", [P, 3, GRP, NB])
        rw = sb("rw", [P, KD, 20])
        rb = sb("rb", [1, 20])

        WF = WORK[:, :, :].rearrange("p a b -> p (a b)")
        ZF = Z[:, :, :].rearrange("p a b -> p (a b)")

        def cc(name, rows=P):
            a, b = CST[name]
            return cst[0:rows, a:b]

        identity = cc("ident")
        KCT = ZF[:, 20 * T:20 * T + 1024].rearrange("p (b n) -> p b n", b=NB)
        XPT = W_RING[:, :, :, :].rearrange("p w k n -> p w (k n)")
        tmpx = XPT[:, 0].rearrange("p (k s n) -> p k s n", k=2, s=2)
        XP = XPT[:, 1].rearrange("p (k g r b) -> p k g r b", k=2, g=2, r=16)
        VN = WF[:, 0:1024].rearrange("p (b k n) -> p b k n", b=2, k=4)
        Sb = [WF[:, 1024 + 512 * j:1536 + 512 * j] for j in range(2)]
        Ex = [WF[:, 2048 + 512 * j:2560 + 512 * j] for j in range(2)]
        PT = [WF[:, 3072 + 512 * j:3584 + 512 * j] for j in range(2)]
        SCc, PTC, VB, YN = (WF[:, 4096 + 512 * j:4608 + 512 * j] for j in range(4))
        M = WF[:, 0:KD * T].rearrange("p (n t) -> p n t", n=KD)
        KG, VG = (CMP[:, 0, 4096 * j:4096 * (j + 1)] for j in range(2))
        KW, VW = (CMP[:, 1, 4096 * j:4096 * (j + 1)] for j in range(2))
        KVT = [[KG, VG], [KW, VW]]
        LATE = WF[:, KD * T:]
        QR = LATE[:, 0:256].rearrange("p (m d) -> p m d", m=GRP)
        SE = LATE[:, 256:768].rearrange("p (b m n) -> p b m n", b=2, m=GRP)
        O2 = LATE[:, 768:1280].rearrange("p (b m d) -> p b m d", b=2, m=GRP)
        KN = LATE[0:NB, 1280:1792].rearrange("p (s n) -> p s n", s=4)
        rt = LATE[0:104, 0:240].rearrange("p (a j k) -> p a j k", a=12, j=5)
        comb = LATE[0:104, 240:320].rearrange("p (j e) -> p j e", j=5)
        lg = LATE[0:104, 320:420].rearrange("p (j e) -> p j e", j=5)
        stT = TWICE[0:2 * GRP, 1024:1280].rearrange("p (a n) -> p a n", a=2)
        cu = rstd[:]
        HID = W_RING[:, 0, 0:4, :].rearrange("p (b k) n -> p b (k n)", b=2)
        combT = ZF[0:N_EXP, 12 * T:13 * T]
        WB = ZF[:, 20 * T:20 * T + 1024].rearrange("p (s k n) -> p s k n", s=2, k=4)
        SG = AUX[:, 0:2 * T].rearrange("p (s t) -> p s t", s=2)
        BB = AUX[:, 2 * T:4 * T].rearrange("p (s t) -> p s t", s=2)
        GU = [r.rearrange("p (w k f) -> p w k f", w=2, k=KD) for r in (CMP[:, 0, 0:4096], ZF[:, 0:4096])]
        WD = [CMP[:, 0, 4096 + 2048 * j:6144 + 2048 * j].rearrange("p (f n) -> p f n", f=2) for j in range(2)]
        A = [ZF[:, (8 + 2 * j) * T:(10 + 2 * j) * T].rearrange("p (f t) -> p f t", f=2) for j in range(2)]
        PROD = ZF[:, 3 * T:3 * T + 4096]
        page = [CMP[:, b, :].rearrange("p (g v h r c) -> p g v h r c", g=PAGES, v=2, h=2, r=16) for b in range(2)]

        x_in = sem("x_in")
        small_in = sem("small_in")
        wg_in = sem("wg_in")
        w_in = [sem("w_in0"), sem("w_in1")]
        consts_done = sem("consts_done")
        dve_const = sem("dve_const")
        sq_ready = sem("sq_ready")
        ms_ready = sem("ms_ready")
        rms_ready = sem("rms_ready")
        norm_ready = sem("norm_ready")
        z_done = sem("z_done")
        z_ready = sem("z_ready")
        dve_step = sem("dve_step")
        pool_step = sem("pool_step")
        ang_ready = sem("ang_ready")
        trig_ready = sem("trig_ready")
        bu_ready = sem("bu_ready")
        v_done = sem("v_done")
        ris_ready = sem("ris_ready")
        h_ready = sem("h_ready")
        y_done = sem("y_done")
        skip_ready = sem("skip_ready")
        gelu_ready = sem("gelu_ready")
        hs_ready = sem("hs_ready")
        ys_done = sem("ys_done")
        glu_done = sem("glu_done")
        glu_sig = sem("glu_sig")
        yssm_ready = sem("yssm_ready")
        yconv_ready = sem("yconv_ready")
        stored = sem("stored")
        cst_in = sem("cst_in")
        tmpx_ready = sem("tmpx_ready")
        xp_in = sem("xp_in")
        ptab_in = sem("ptab_in")
        pages_in = [sem("pages_in0"), sem("pages_in1")]
        odd_pages_in = [sem("odd_pages_in0"), sem("odd_pages_in1")]
        cb_done, cb_ready = sem("cb_done"), sem("cb_ready")
        hid_done, hid_ready = sem("hid_done"), sem("hid_ready")
        kc_done, kc_ready = sem("kc_done"), sem("kc_ready")
        vb_rep, vb_ready = sem("vb_rep"), sem("vb_ready")
        vt_done, vt_ready = sem("vt_done"), sem("vt_ready")
        gt_done, gt_ready = sem("gt_done"), sem("gt_ready")
        sc_done, sc_ready, ec_ready, ecm_ready = sem("sc_done"), sem("sc_ready"), sem("ec_ready"), sem("ecm_ready")
        ptc_done, ptc_ready, oc_done = sem("ptc_done"), sem("ptc_ready"), sem("oc_done")
        s_done, sb_ready, e_ready, t_done, pt_ready, pv_done = (
            sem(n) for n in ("s_done", "sb_ready", "e_ready", "t_done", "pt_ready", "pv_done"))
        qn_done, qn_ready, qr_done, qr_ready = (sem(n) for n in ("qn_done", "qn_ready", "qr_done", "qr_ready"))
        kn_done = sem("kn_done")
        gm_ready, gb_done = sem("gm_ready"), sem("gb_done")
        qs_done, qs_copied, st_done = sem("qs_done"), sem("qs_copied"), sem("st_done")
        ss_ready, es_ready, p_ready = sem("ss_ready"), sem("es_ready"), sem("p_ready")
        imp_done, pts_ready, ocs_done, idx_ready, idx_done = (
            sem(n) for n in ("imp_done", "pts_ready", "ocs_done", "idx_ready", "idx_done"))
        row_ready, kg_in, kw_in, kn_in, kn_in_w = (
            sem(n) for n in ("row_ready", "kg_in", "kw_in", "kn_in", "kn_in_w"))
        se_ready, ex_ready, o2_ready = sem("se_ready"), sem("ex_ready"), sem("o2_ready")
        stt_done, w8_ready, ew_ready, wn_ready, wn_done, o2_scaled, ot_done, ya_ready = (
            sem(n) for n in ("stt_done", "w8_ready", "ew_ready", "wn_ready", "wn_done", "o2_scaled", "ot_done",
                             "ya_ready"))
        wb_in = [sem("wb_in0"), sem("wb_in1")]
        mz_done, mz_ready, mb_done, mb_ready, mm_ready = (
            sem(n) for n in ("mz_done", "mz_ready", "mb_done", "mb_ready", "mm_ready"))
        x_again, mo_done, mo_ready, win_stored = sem("x_again"), sem("mo_done"), sem("mo_ready"), sem("win_stored")
        lg_done, rx_ready, re_ready, comb_ready, ct_done, ct_ready, comb_stored = (
            sem(n) for n in ("lg_done", "rx_ready", "re_ready", "comb_ready", "ct_done", "ct_ready", "comb_stored"))
        gu_in, wd_in, cb_in = ([sem(f"{n}{j}") for j in range(2)] for n in ("gu_in", "wd_in", "cb_in"))
        gu_done, silu_ready, up_ready, a_ready, dn_done, dn_ready = (
            sem(n) for n in ("gu_done", "silu_ready", "up_ready", "a_ready", "dn_done", "dn_ready"))
        y_out = sem("y_out")
        y_nat, yt_done, yt_ready = sem("y_nat"), sem("yt_done"), sem("yt_ready")

        ki, kf, uu, au = (WORK[:, i, :] for i in range(4))
        vr, vi = WORK[:, 0, :], WORK[:, 1, :]
        sn, cs = (WORK[:, 4, :], WORK[:, 5, :]), (WORK[:, 6, :], WORK[:, 7, :])
        pw, qw = WORK[:, 8, :], WORK[:, 9, :]
        hr, hi = WORK[:, 10, :], WORK[:, 11, :]
        kint = ki.bitcast(I32)
        glu_g = WORK[:, :, :].rearrange("p a b -> p (a b)")[:, 0:ST * T].rearrange("p (k t) -> p k t", k=ST)
        (A_RE, A_IM, LDT) = range(3)
        (DT, MAG, TH, MF, TQ, MH, RR, UQ, AQ, SI, CO, ABR, ABI, AM1, DEN, RDEN, CR, CI, NCI, NABI,
         T1, T2) = range(22)

        def par(k, i=None):
            return spar[:, k, :] if i is None else spar[:, k, i:i + 1]

        beside = [[t for t in (3 + 2 * i, 4 + 2 * i) if t < NZ] for i in range(SN)]

        N_UNITS = 64

        def unit(n):
            return n // 16, n // 8 % 2, n % 8, (n // 16 + 1) * P

        block = ctx.enter_context(nc.Block())

        def load_pages(engine, s, b, first, groups, arrived, later):
            with engine.Fori(0, groups) as i:
                at = [engine.value_load(ptab[0:1, bass.ds(s * PAGES + first + 8 * i + 2 * j, 1)], min_val=0,
                                        max_val=N_POOL - 1) for j in range(4)]
                if later:
                    engine.wait_ge(hid_done, s)
                for j in range(4):
                    engine.dma_start(CMP[:, b, bass.ds((first + 8 * i + 2 * j) * 256, 256)],
                                     io["cmp"][bass.ds(at[j], 1)].rearrange("o p n -> p (o n)")).then_inc(arrived, 16)

        @block.sync
        def _(sp):
            for k in range(0, KD, 2):
                sp.dma_start(X[:, k:k + 2, :], io["xT"][:, k:k + 2, :]).then_inc(x_in, 16)
            sp.dma_start(gains[:], io["gains"]).then_inc(small_in, 16)
            sp.dma_start(prm[:], io["prm"]).then_inc(small_in, 16)
            sp.dma_start(BT, io["BT"]).then_inc(small_in, 16)
            sp.dma_start(CT, io["CT"]).then_inc(small_in, 16)
            sp.dma_start(ptab[:], io["ptab"]).then_inc(ptab_in, 16)
            sp.wait_ge(ptab_in, 16)

            for t in range(NZ):
                if t >= 2:
                    sp.wait_ge(z_done, t - 1)
                sp.dma_start(W_RING[:, t % 2], io["w_z"][t]).then_inc(w_in[t % 2], 16)
                if 3 <= t < 19 and t % 2:
                    s, g = divmod((t - 3) // 2, 4)
                    if s == 1 and g == 0:
                        sp.wait_ge(norm_ready, KD)
                    load_pages(sp, s, s, 8 * g, 1, pages_in[s], False)
                if t == 1:
                    sp.dma_start(h0[:], io["h0"]).then_inc(small_in, 16)
                    sp.dma_start(sdb[:], io["sdb"]).then_inc(small_in, 16)
                    sp.dma_start(w_glu, io["w_glu"]).then_inc(small_in, 16)
                    sp.dma_start(cw[:], io["cw"]).then_inc(small_in, 16)
                    sp.dma_start(cprev[:], io["cprev"]).then_inc(small_in, 16)
                    sp.dma_start(wgt[:], io["w_gates"]).then_inc(wg_in, 16)
                    sp.dma_start(cst[:], io["cst"]).then_inc(cst_in, 16)
                    sp.dma_start(w1, io["w1"]).then_inc(cst_in, 16)
                    sp.dma_start(w2[:], io["w2"]).then_inc(cst_in, 16)
                    sp.dma_start(pe_t[:], io["pe"]).then_inc(cst_in, 16)
                    sp.dma_start(pt8[:], io["pt8"]).then_inc(cst_in, 16)
            with sp.Fori(1, 4) as i:
                for b in range(2):
                    load_pages(sp, 2 * i + b, b, 0, PAGES // 8, pages_in[b], True)
            sp.wait_ge(hid_done, NB + 1)
            for v, dst in enumerate((KW, VW)):
                src = io["win"][v]
                sp.dma_start(dst[0:P - 1, :], src[HD:HD + (P - 1) * 4096].rearrange("(p n) -> p n", p=P - 1))\
                    .then_inc(kw_in, 16)
                sp.dma_start(dst[P - 1:P, 0:63 * HD], src[HD + (P - 1) * 4096:].rearrange("(p n) -> p n", p=1))\
                    .then_inc(kw_in, 16)

            def new_row(sem_, dst, s, pos):
                for g in range(KVH):
                    sp.dma_start(dst[SLOTS * g + SLOTS - 1::16, pos * HD:pos * HD + HD],
                                 KN[:, s, g * HD:g * HD + HD]).then_inc(sem_, 16)

            sp.wait_ge(qr_ready, 1)
            sp.wait_ge(kw_in, 64)
            new_row(kn_in_w, KW, 2, SELB - 1)
            new_row(kn_in_w, VW, 3, SELB - 1)
            sp.wait_ge(kc_done, NB + 1)
            sp.wait_ge(qs_done, 1)

            def merge_loads(br, first):
                nk = BRANCH_K[br]
                with sp.Fori(first, 4) as i:
                    for b in range(2):
                        q = 8 * br + 2 * i + b
                        if br or first:
                            sp.wait_ge(mz_done, q - 1)
                            sp.wait_ge(mb_done, q - 1)
                        sp.dma_start(W_RING[:, b], io["w_m"][bass.ds(q, 1)].rearrange("o p k n -> p (o k) n"))\
                            .then_inc(w_in[b], 16)
                        sp.dma_start(WB[:, b, 0:nk], io[f"w_b{br}"][bass.ds(2 * i + b, 1)]
                                     .rearrange("o p k n -> p (o k) n")).then_inc(wb_in[b], 16)

            for b in range(2):
                sp.dma_start(W_RING[:, b], io["w_m"][b]).then_inc(w_in[b], 16)
                sp.dma_start(WB[:, b, 0:BRANCH_K[0]], io["w_b0"][b]).then_inc(wb_in[b], 16)
            sp.wait_ge(kg_in, 32)
            new_row(kn_in, KG, 0, 0)
            new_row(kn_in, VG, 1, 0)
            merge_loads(0, 1)
            merge_loads(1, 0)
            sp.wait_ge(kn_in_w, 64)
            for v, src in enumerate((KW, VW)):
                sp.dma_start(io["o_win"][v], src).then_inc(win_stored, 16)
            merge_loads(2, 0)
            sp.dma_start(rw[:], io["w_r"]).then_inc(x_again, 16)
            sp.dma_start(rb[:], io["b_r"]).then_inc(x_again, 16)
            sp.wait_ge(o2_ready, 2)
            sp.wait_ge(win_stored, 32)
            sp.dma_start(X, io["xT"]).then_inc(x_again, 16)
            sp.dma_start(GU[0], io["w_gu"][0]).then_inc(gu_in[0], 16)
            sp.dma_start(WD[0], io["w_d"][0]).then_inc(wd_in[0], 16)
            for b in range(2):
                sp.wait_ge(mz_done, 23 + b)
                sp.dma_start(W_RING[:, b], io["w_o"][b]).then_inc(w_in[b], 16)
            with sp.Fori(1, 4) as i:
                for b in range(2):
                    sp.wait_ge(mo_done, 2 * i)
                    sp.dma_start(W_RING[:, b], io["w_o"][bass.ds(2 * i + b, 1)].rearrange("o p k n -> p (o k) n"))\
                        .then_inc(w_in[b], 16)
            sp.wait_ge(mm_ready, 26)
            sp.dma_start(GU[1], io["w_gu"][1]).then_inc(gu_in[1], 16)
            sp.dma_start(WD[1], io["w_d"][1]).then_inc(wd_in[1], 16)
            sp.wait_ge(ct_ready, 2)
            sp.dma_start(io["comb"], combT).then_inc(comb_stored, 16)
            sp.wait_ge(comb_stored, 16)

            def comb_load(b, e):
                sp.dma_start(CB2[:, b, :], io["comb"][bass.ds(e, 1), :].to_broadcast([P, T])).then_inc(cb_in[b], 16)

            comb_load(0, 0)
            comb_load(1, 1)
            with sp.Fori(1, N_EXP // 2) as i:
                for b in range(2):
                    e = 2 * i + b
                    sp.wait_ge(gu_done, 2 * e - 2)
                    sp.dma_start(GU[b], io["w_gu"][bass.ds(e, 1)].rearrange("o p w k f -> p (o w) k f"))\
                        .then_inc(gu_in[b], 16)
                    sp.wait_ge(a_ready, 2 * e - 2)
                    comb_load(b, e)
                    sp.wait_ge(dn_done, 8 * e - 8)
                    sp.dma_start(WD[b], io["w_d"][bass.ds(e, 1)].rearrange("o p f n -> p (o f) n"))\
                        .then_inc(wd_in[b], 16)
            sp.wait_ge(norm_ready, 3 * KD)
            sp.dma_start(io["o_yT"], H[:]).then_inc(y_out, 16)
            sp.wait_ge(y_out, 16)
            sp.wait_ge(stored, N_STORED * 16)

        @block.gpsimd
        def _(pool):
            step = Chain(pool, pool_step)
            pool.memset(halfpi[:], float(np.pi / 2)).then_inc(consts_done, 1)
            pool.memset(epsb[:], EPS).then_inc(consts_done, 1)
            pool.iota(tvec, [[1, SEQ]], base=0, channel_multiplier=0,
                      allow_small_or_imprecise_dtypes=True).then_inc(consts_done, 1)

            pool.wait_ge(ptab_in, 16)
            for s in range(2):
                if s == 1:
                    pool.wait_ge(norm_ready, KD)
                load_pages(pool, s, s, 1, PAGES // 8, odd_pages_in[s], False)
            pool.wait_ge(small_in, 9 * 16)
            pool.wait_ge(z_ready, NZ)
            for c in range(ST):
                y, gb, tmp = Z[:, Z_CC + c, :], Z[:, Z_CB + c, :], Z[:, Z_CX + c, :]
                step(pool.tensor_tensor(cu, Z[:, Z_CC + c, :], Z[:, Z_CX + c, :], ALU.mult))
                step(pool.tensor_copy(clast[:, c, :, 0], cu[:, SEQ - 2:SEQ]))
                step(pool.tensor_copy(clast[:, c, 0, 1:], cprev[:, c, 1, :]))
                step(pool.tensor_copy(clast[:, c, 1, 1:], cu[:, SEQ:T]))
                step(pool.tensor_scalar(y, cu, cw[:, c, 2:3], None, ALU.mult))
                for j, lag in ((1, 1), (0, 2)):
                    w = cw[:, c, j:j + 1]
                    step(pool.tensor_scalar(tmp[:, lag:SEQ], cu[:, 0:SEQ - lag], w, None, ALU.mult))
                    step(pool.tensor_scalar(tmp[:, SEQ:T], cprev[:, c, j, :], w, None, ALU.mult))
                    step(pool.tensor_tensor(y[:, lag:T], y[:, lag:T], tmp[:, lag:T], ALU.add))
                step(pool.tensor_tensor(gb, gb, y, ALU.mult))
            pool.sem_inc(yconv_ready, 1)
            pool.dma_start(io["o_kvT"].rearrange("s p t -> p s t"), Z[:, Z_KV:Z_KV + 6, :]).then_inc(stored, 16)
            pool.dma_start(io["o_clast"], clast[:]).then_inc(stored, 16)

            for v in range(2):
                pool.tensor_copy(tmpx[:, v].rearrange("p s (r b) -> p s r b", r=16),
                                 Z[:, Z_KV + v, 0:SEQ].rearrange("p (b r s) -> p s r b", r=16, s=2))\
                    .then_inc(tmpx_ready, 1)
            pool.wait_ge(tmpx_ready, 2)
            for v in range(2):
                for g in range(KVH):
                    for par_ in range(2):
                        pool.dma_start(XP[par_ * HD:par_ * HD + HD, v, g].rearrange("p r b -> p (r b)"),
                                       tmpx[g * HD:g * HD + HD, v, par_]).then_inc(xp_in, 16)
            pool.wait_ge(hs_ready, 1)
            pool.dma_start(io["o_hlast"], hlast[:]).then_inc(stored, 16)

            with pool.Fori(1, 4) as i:
                for b in range(2):
                    load_pages(pool, 2 * i + b, b, 1, PAGES // 8, odd_pages_in[b], True)
            pool.wait_ge(row_ready, 1)
            pool.wait_ge(hid_done, NB + 1)
            for dst, src in ((KG, "kslc"), (VG, "vslc")):
                pool.indirect_dma_start(out=dst, out_offset=None, in_=io[src],
                                        in_offset=bass.IndirectOffsetOnAxis(ap=rowi[:, 0:1], axis=0))\
                    .then_inc(kg_in, 16)
            pool.sem_inc(mm_ready, 2)
            pool.wait_ge(y_nat, 4)
            pool.wait_ge(pv_done, N_UNITS)
            for br in range(3):
                with pool.Fori(0, 4) as i:
                    for b in range(2):
                        q = 8 * br + 2 * i + b
                        pool.wait_ge(mb_ready, q + 2)
                        out = M[:, bass.ds(2 * i + b, 1), :].rearrange("p o t -> p (o t)")
                        if br == 0:
                            pool.tensor_tensor(out, SG[:, b], BB[:, b], ALU.mult).then_inc(mm_ready, 1)
                        else:
                            pool.tensor_tensor(SG[:, b], SG[:, b], BB[:, b], ALU.mult).then_inc(pool_step, 1)
                            pool.wait_ge(pool_step, step.n + 8 * (br - 1) + 2 * i + b + 1)
                            pool.tensor_tensor(out, out, SG[:, b], ALU.add).then_inc(mm_ready, 1)
            with pool.Fori(0, N_EXP // 2) as i:
                for b in range(2):
                    pool.wait_ge(cb_in[b], 16 * (i + 1))
                    for f in range(2):
                        pool.wait_ge(up_ready, 2 * (2 * i + b) + f + 1)
                        pool.tensor_tensor(A[b][:, f, :], A[b][:, f, :], CB2[:, b, :], ALU.mult).then_inc(a_ready, 1)

        def rms_scalar(act, n, src):
            for k in range(KD):
                act.activation(H[:, k, :], src(k), ACT.Square).then_inc(sq_ready, 1)
            act.wait_ge(ms_ready, n + 1)
            for c, (a, b) in enumerate(CHUNKS):
                act.activation(rstd[:, a:b], bank[c][:, 0:HALF], ACT.Sqrt, bias=epsb[:],
                               scale=1.0 / D).then_inc(rms_ready, 1)

        def rms_tensor(pe, n):
            for k in range(KD):
                pe.wait_ge(sq_ready, KD * n + k + 1)
                for c, (a, b) in enumerate(CHUNKS):
                    mm = pe.matmul(bank[c][:, 0:HALF], ones[:], H[:, k, a:b], start=(k == 0), stop=(k == KD - 1))
            mm.then_inc(ms_ready, 1)

        def rms_vector(dve, step, n, src, dst):
            dve.wait_ge(rms_ready, 2 * (n + 1))
            step(dve.reciprocal(rstd[:], rstd[:]))
            for k in range(KD):
                dve.scalar_tensor_tensor(dst(k), src(k), gains[:, n, k:k + 1], rstd[:], ALU.mult,
                                         ALU.mult).then_inc(norm_ready, 1)

        @block.scalar
        def _(act):
            act.wait_ge(consts_done, 3)
            act.wait_ge(x_in, 64)
            rms_scalar(act, 0, lambda k: X[:, k, :])

            def z_copy(t):
                act.wait_ge(z_done, t + 1)
                for c, (a, b) in enumerate(CHUNKS):
                    mm = act.activation(Z[:, t, a:b], bank[2 * (t % 2) + c][:, 0:HALF], ACT.Copy,
                                        scale=HD**-0.5 if Z_Q <= t < Z_KV else 1.0)
                mm.then_inc(z_ready, 1)

            def sincos(u, a, s, c, n):
                act.wait_ge(ang_ready, n)
                act.activation(s, u, ACT.Sin, scale=SIN_SCALE).then_inc(trig_ready, 1)
                act.activation(c, a, ACT.Sin, scale=-SIN_SCALE, bias=halfpi[:]).then_inc(trig_ready, 1)

            act.wait_ge(small_in, 9 * 16)
            act.activation(par(DT), prm[:, LDT, :], ACT.Exp).then_inc(trig_ready, 1)
            act.wait_ge(ang_ready, 1)
            act.activation(par(MAG), par(T1), ACT.Exp).then_inc(trig_ready, 1)
            sincos(par(UQ), par(AQ), par(SI), par(CO), 2)
            sincos(uu, au, sn[0], cs[0], 3)
            for t in range(3):
                z_copy(t)
            for i in range(SN):
                act.wait_ge(bu_ready, i + 1)
                act.activation(RIs[:, i], bank[7][:, 0:2 * NB].rearrange("p (r b) -> p r b", r=2),
                               ACT.Copy).then_inc(ris_ready, 1)
                if i + 1 < SN:
                    sincos(uu, au, sn[(i + 1) % 2], cs[(i + 1) % 2], 4 + i)
                for t in beside[i]:
                    z_copy(t)
                if i == 9:
                    act.wait_ge(z_done, NZ + 1)
                    for c, (a, b) in enumerate(CHUNKS):
                        mm = act.activation(Gt[:, a:b], bank[c][0:24, 0:HALF], ACT.Sigmoid)
                    mm.then_inc(z_ready, 1)
                if i % 4 == 3:
                    c = i // 4
                    act.wait_ge(skip_ready, c + 1)
                    act.activation(Z[:, c, 0:SEQ], Z[:, c, 0:SEQ], ACT.Gelu_apprx_tanh).then_inc(gelu_ready, 1)
            act.wait_ge(skip_ready, ST + 1)
            act.activation(Z[:, 0:ST, SEQ:T], Z[:, 0:ST, SEQ:T], ACT.Gelu_apprx_tanh).then_inc(gelu_ready, 1)
            for n in range(ST):
                act.wait_ge(glu_done, n + 1)
                for c, (a, b) in enumerate(CHUNKS):
                    mm = act.activation(glu_g[:, n, a:b], bank[2 * (n % 2) + c][:, 0:HALF], ACT.Sigmoid,
                                        bias=sdb[:, 1, n:n + 1])
                mm.then_inc(glu_sig, 1)

            act.wait_ge(cb_done, 1)
            act.activation(cbias[:], bank[3][:, 0:1], ACT.Copy).then_inc(cb_ready, 1)
            act.wait_ge(cb_ready, 1)
            act.wait_ge(hid_done, 1)
            act.activation(HID[:, 0, 0:32], bank[0][:, 0:32], ACT.Gelu_apprx_tanh, bias=cbias[:]).then_inc(hid_ready, 1)
            act.wait_ge(kc_done, 1)
            act.activation(kcp[:], bank[2][:, 0:16], ACT.Copy).then_inc(kc_ready, 1)
            act.activation(vcp[:], bank[3][0:16, 0:P], ACT.Copy).then_inc(kc_ready, 1)
            act.wait_ge(yssm_ready, 1)
            for b in range(2):
                act.wait_ge(vt_done, b + 1)
                act.activation(VN[:, b].rearrange("p k n -> p (k n)"), bank[4 + b][:, :], ACT.Copy).then_inc(vt_ready, 1)
            act.wait_ge(gt_done, 1)
            act.activation(Gn[:].rearrange("p q n -> p (q n)"), bank[7][:, 0:96], ACT.Copy).then_inc(gt_ready, 1)
            act.wait_ge(sc_ready, 1)
            act.activation(SCc, SCc, ACT.Exp).then_inc(ec_ready, 1)
            act.wait_ge(ptc_done, 1)
            act.activation(PTC, bank[7][:, :], ACT.Copy).then_inc(ptc_ready, 1)

            def pt_copy(n):
                L = unit(n)[3]
                act.wait_ge(t_done, n + 1)
                if n >= 2:
                    act.wait_ge(pv_done, n - 1)
                act.activation(PT[n % 2][:, 0:L], bank[2 + n % 2][:, 0:L], ACT.Copy).then_inc(pt_ready, 1)

            def yt_copy(qt):
                act.wait_ge(yt_done, qt + 1)
                act.activation(Z[:, Z_CC:Z_CC + GRP, qt * P:(qt + 1) * P],
                               bank[7][:, :].rearrange("p (m q) -> p m q", m=GRP), ACT.Copy).then_inc(yt_ready, 1)

            def hid_gelu(smp):
                act.wait_ge(hid_done, smp + 2)
                act.wait_ge(kc_done, smp + 1)
                act.activation(HID[:, smp % 2, :], bank[7][:, 0:2 * NCB], ACT.Gelu_apprx_tanh, bias=cbias[:])\
                    .then_inc(hid_ready, 1)

            def kc_copy(smp):
                act.wait_ge(kc_done, smp + 2)
                act.activation(KCT[:, smp, :], bank[7][:, 2 * NCB:3 * NCB], ACT.Copy).then_inc(kc_ready, 1)
                act.activation(VC[:, smp, :], bank[7][:, 3 * NCB:4 * NCB], ACT.Copy).then_inc(kc_ready, 1)

            for n in range(N_UNITS):
                qt, br, pos, L = unit(n)
                at = n % 16
                act.wait_ge(sb_ready, n + 1)
                if n >= 2:
                    act.wait_ge(t_done, n - 1)
                act.activation(Ex[n % 2][:, 0:L], Sb[n % 2][:, 0:L], ACT.Exp, bias=nmax[:, n:n + 1],
                               accum_out=lsum[:, n:n + 1]).then_inc(e_ready, 1)
                if n >= 1:
                    pt_copy(n - 1)
                if at == 0 and qt:
                    hid_gelu(2 * qt - 1)
                if at == 1 and qt:
                    kc_copy(2 * qt - 1)
                if at == 3 and qt:
                    yt_copy(qt - 1)
                if at == 9:
                    hid_gelu(2 * qt)
                if at == 10:
                    kc_copy(2 * qt)
            pt_copy(N_UNITS - 1)
            hid_gelu(NB - 1)
            kc_copy(NB - 1)
            yt_copy(3)
            act.wait_ge(ss_ready, 1)
            act.activation(sm[0:64, 64:192], sm[0:64, 64:192], ACT.Exp, bias=small[0:64, 0:1],
                           accum_out=small[0:64, 1:2]).then_inc(es_ready, 1)

            act.sem_inc(mz_ready, 1)
            act.sem_inc(mb_ready, 1)

            def merge_copies(br):
                with act.Fori(0, 4) as i:
                    for b in range(2):
                        q = 8 * br + 2 * i + b
                        act.wait_ge(mz_done, q + 1)
                        act.wait_ge(mm_ready, q + 1)
                        for c, (lo, hi_) in enumerate(CHUNKS):
                            mm = act.activation(SG[:, b, lo:hi_], bank[c][:, 0:HALF], ACT.Sigmoid)
                        mm.then_inc(mz_ready, 1)
                        act.wait_ge(mb_done, q + 1)
                        for c, (lo, hi_) in enumerate(CHUNKS):
                            mm = act.activation(BB[:, b, lo:hi_], bank[2 + c][:, 0:HALF], ACT.Copy)
                        mm.then_inc(mb_ready, 1)

            def chunk_exp(n):
                act.wait_ge(se_ready, n + 1)
                act.activation(SE[:, 1 - n].rearrange("p m n -> p (m n)"), SE[:, 1 - n].rearrange("p m n -> p (m n)"),
                               ACT.Exp).then_inc(ex_ready, 1)

            merge_copies(0)
            chunk_exp(0)
            merge_copies(1)
            chunk_exp(1)
            act.wait_ge(w8_ready, 1)
            act.activation(stT[:, 0, :], stT[:, 0, :], ACT.Exp).then_inc(ew_ready, 1)
            merge_copies(2)

            act.wait_ge(mo_ready, KD + 2)
            act.wait_ge(mz_done, 24)
            rms_scalar(act, 1, lambda k: X[:, k, :])
            act.wait_ge(rx_ready, 1)
            act.activation(rt[:, 0], rt[:, 0], ACT.Exp).then_inc(re_ready, 1)
            act.wait_ge(rx_ready, 2)
            act.activation(rt[:, 1], rt[:, 1], ACT.Exp).then_inc(re_ready, 1)
            with act.Fori(0, N_EXP // 2) as i:
                for b in range(2):
                    e = 2 * i + b
                    for f in range(2):
                        act.wait_ge(gu_done, 2 * e + f + 1)
                        if f == 0:
                            act.wait_ge(dn_ready, 8 * e + 1)
                        for c, (lo, hi_) in enumerate(CHUNKS):
                            mm = act.activation(A[b][:, f, lo:hi_], bank[4 * ((b + f) % 2) + c][:, 0:HALF], ACT.Silu)
                        mm.then_inc(silu_ready, 1)
            act.wait_ge(dn_ready, 8 * N_EXP + 9)
            rms_scalar(act, 2, lambda k: X[:, k, :])

        @block.vector
        def _(dve):
            step = Chain(dve, dve_step)
            dve.memset(ones[:], 1.0).then_inc(dve_const, 1)
            dve.wait_ge(small_in, 9 * 16)
            dve.wait_ge(consts_done, 3)
            dve.wait_ge(ms_ready, 1)
            rms_vector(dve, step, 0, lambda k: X[:, k, :], lambda k: H[:, k, :])

            dve.wait_ge(trig_ready, 1)
            step(dve.tensor_tensor(par(T1), prm[:, A_RE, :], par(DT), ALU.mult))
            dve.sem_inc(ang_ready, 1)
            step(dve.tensor_tensor(par(TH), prm[:, A_IM, :], par(DT), ALU.mult))
            step(dve.tensor_scalar(spi[:], par(TH), TURN / (2 * np.pi), None, ALU.mult))
            step(dve.tensor_copy(par(MF), spi[:]))
            for c in cody_waite(2 * np.pi / TURN, 8):
                step(dve.scalar_tensor_tensor(par(TH), par(MF), -c, par(TH), ALU.mult, ALU.add))
            step(dve.tensor_scalar(par(RR), par(TH), 1 / (2 * np.pi), None, ALU.mult))
            step(dve.tensor_scalar(spi[:], par(MF), 1.0 / TURN, None, ALU.mult))
            step(dve.tensor_copy(par(TQ), spi[:]))
            step(dve.scalar_tensor_tensor(par(MH), par(MF), 1.0 / TURN, par(TQ), ALU.mult, ALU.subtract))
            step(dve.tensor_tensor(par(UQ), par(MH), par(RR), ALU.add))
            step(dve.tensor_scalar(spi[:], par(UQ), 1.0, None, ALU.mult))
            step(dve.tensor_tensor(par(UQ), par(UQ), spi[:], ALU.subtract))
            step(dve.scalar_tensor_tensor(par(AQ), par(UQ), -1.0, par(UQ), ALU.mult, ALU.max))
            dve.sem_inc(ang_ready, 1)

            def angle(i):
                if i >= 1:
                    dve.wait_ge(trig_ready, 4 + 2 * i)
                step(dve.tensor_scalar(kint, tvec, par(MH, i), None, ALU.mult))
                step(dve.scalar_tensor_tensor(kf, tvec, par(MH, i), kint, ALU.mult, ALU.subtract))
                step(dve.scalar_tensor_tensor(uu, tvec, par(RR, i), kf, ALU.mult, ALU.add))
                step(dve.tensor_scalar(kint, uu, 1.0, None, ALU.mult))
                step(dve.tensor_tensor(uu, uu, kint, ALU.subtract))
                step(dve.scalar_tensor_tensor(au, uu, -1.0, uu, ALU.mult, ALU.max))
                dve.sem_inc(ang_ready, 1)

            angle(0)
            dve.wait_ge(trig_ready, 4)
            step(dve.tensor_tensor(par(ABR), par(MAG), par(CO), ALU.mult))
            step(dve.tensor_tensor(par(ABI), par(MAG), par(SI), ALU.mult))
            step(dve.tensor_scalar(par(AM1), par(ABR), -1.0, None, ALU.add))
            step(dve.tensor_tensor(par(DEN), prm[:, A_RE, :], prm[:, A_RE, :], ALU.mult))
            step(dve.tensor_tensor(par(T1), prm[:, A_IM, :], prm[:, A_IM, :], ALU.mult))
            step(dve.tensor_tensor(par(DEN), par(DEN), par(T1), ALU.add))
            step(dve.reciprocal(par(RDEN), par(DEN)))
            step(dve.tensor_tensor(par(T1), par(AM1), prm[:, A_RE, :], ALU.mult))
            step(dve.tensor_tensor(par(T2), par(ABI), prm[:, A_IM, :], ALU.mult))
            step(dve.tensor_tensor(par(T1), par(T1), par(T2), ALU.add))
            step(dve.tensor_tensor(par(CR), par(T1), par(RDEN), ALU.mult))
            step(dve.tensor_tensor(par(T1), par(ABI), prm[:, A_RE, :], ALU.mult))
            step(dve.tensor_tensor(par(T2), par(AM1), prm[:, A_IM, :], ALU.mult))
            step(dve.tensor_tensor(par(T1), par(T1), par(T2), ALU.subtract))
            step(dve.tensor_tensor(par(CI), par(T1), par(RDEN), ALU.mult))
            step(dve.tensor_scalar(par(NCI), par(CI), -1.0, None, ALU.mult))
            step(dve.tensor_scalar(CT[:, :, 1, :], CT[:, :, 1, :], -1.0, None, ALU.mult))
            dve.memset(hlast[:, :, :, 0], 0.0)

            for i in range(SN):
                if i + 1 < SN:
                    angle(i + 1)
                s, c = sn[i % 2], cs[i % 2]
                dve.wait_ge(trig_ready, 6 + 2 * i)
                step(dve.tensor_scalar(pw, c, par(CR, i), None, ALU.mult))
                step(dve.scalar_tensor_tensor(pw, s, par(CI, i), pw, ALU.mult, ALU.add))
                step(dve.tensor_scalar(qw, s, par(CR, i), None, ALU.mult))
                step(dve.scalar_tensor_tensor(qw, c, par(CI, i), qw, ALU.mult, ALU.subtract))
                dve.wait_ge(bu_ready, i + 1)
                R, I = bank[4][:, :], bank[5][:, :]
                step(dve.tensor_tensor(vi, qw, I, ALU.mult))
                step(dve.tensor_tensor(vr, pw, R, ALU.mult))
                step(dve.tensor_tensor(vr, vr, vi, ALU.subtract))
                step(dve.tensor_tensor(pw, pw, I, ALU.mult))
                step(dve.tensor_tensor(qw, qw, R, ALU.mult))
                dve.sem_inc(v_done, 1)
                step(dve.tensor_tensor(vi, pw, qw, ALU.add))
                mag = par(MAG, i).to_broadcast([P, SEQ])
                step(dve.tensor_tensor_scan(pw, mag, vr, 0.0, ALU.mult, ALU.add))
                step(dve.tensor_tensor_scan(qw, mag, vi, 0.0, ALU.mult, ALU.add))
                if i >= 1:
                    dve.wait_ge(y_done, i)
                step(dve.tensor_tensor(vr, c, pw, ALU.mult))
                step(dve.tensor_tensor(vi, s, qw, ALU.mult))
                step(dve.tensor_tensor(hr, vr, vi, ALU.subtract))
                step(dve.tensor_tensor(vr, s, pw, ALU.mult))
                step(dve.tensor_tensor(vi, c, qw, ALU.mult))
                step(dve.tensor_tensor(hi, vr, vi, ALU.add))
                dve.sem_inc(h_ready, 1)
                step(dve.tensor_copy(hlast[:, i, 0, 0:1], hr[:, SEQ - 1:SEQ]))
                step(dve.tensor_copy(hlast[:, i, 1, 0:1], hi[:, SEQ - 1:SEQ]))
                if i % 4 == 3:
                    c = i // 4
                    dve.wait_ge(y_done, i + 1)
                    step(dve.scalar_tensor_tensor(Z[:, c, 0:SEQ], Z[:, c, 0:SEQ], sdb[:, 0, c:c + 1],
                                                  bank[6][:, :], ALU.mult, ALU.add))
                    dve.sem_inc(skip_ready, 1)
            dve.wait_ge(ris_ready, SN)

            def row(k):
                return spar[:, k, :].unsqueeze(2).broadcast_to([P, SN, NB])

            def madd(dst, terms):
                t0, t1 = stmp[:, 0], stmp[:, 1]
                for n, (k, x, sub) in enumerate(terms):
                    step(dve.tensor_tensor(t0 if n == 0 else t1, x, row(k), ALU.mult))
                    if n:
                        last = n == len(terms) - 1
                        step(dve.tensor_tensor(dst if last else t0, t0, t1, ALU.subtract if sub else ALU.add))

            madd(hlast[:, :, 0, 1:], [(ABR, h0[:, :, 0], 0), (ABI, h0[:, :, 1], 1),
                                      (CR, RIs[:, :, 0], 0), (CI, RIs[:, :, 1], 1)])
            madd(hlast[:, :, 1, 1:], [(ABR, h0[:, :, 1], 0), (ABI, h0[:, :, 0], 0),
                                      (CR, RIs[:, :, 1], 0), (CI, RIs[:, :, 0], 0)])
            dve.sem_inc(hs_ready, 1)
            dve.wait_ge(ys_done, 1)
            for c in range(ST):
                step(dve.scalar_tensor_tensor(Z[:, c, SEQ:T], Z[:, c, SEQ:T], sdb[:, 0, c:c + 1],
                                              bank[6][:, NB * c:NB * c + NB], ALU.mult, ALU.add))
            dve.sem_inc(skip_ready, 1)
            for n in range(ST):
                dve.wait_ge(glu_sig, n + 1)
                if n == 0:
                    dve.wait_ge(glu_done, ST)
                step(dve.tensor_tensor(Z[:, n, :], Z[:, n, :], glu_g[:, n, :], ALU.mult))
            dve.sem_inc(yssm_ready, 1)

            dve.wait_ge(cst_in, 5 * 16)
            dve.wait_ge(vb_rep, 1)
            step(dve.tensor_tensor(VB.rearrange("p (m n) -> p m n", m=GRP),
                                   bank[3][:, 0:P].unsqueeze(1).broadcast_to([P, GRP, P]),
                                   cc("blocks").rearrange("p (m n) -> p m n", m=GRP), ALU.mult))
            dve.sem_inc(vb_ready, 1)
            dve.wait_ge(sc_done, 1)
            sc3 = SCc.rearrange("p (a c) -> p a c", c=16)
            for g in range(KVH):
                def of_g(x):
                    return x.rearrange("p (a g c) -> p a g c", g=KVH, c=16)[:, :, g, :]
                step(dve.tensor_tensor(of_g(SCc), bank[6 if g == 0 else 1][:, 0:256]
                                       .rearrange("p (a c) -> p a c", c=16), of_g(cc("bias_p")), ALU.add))
            step(dve.tensor_reduce(cmax[:], sc3, AX_X, ALU.max))
            step(dve.tensor_tensor(sc3, sc3, cmax[:].unsqueeze(2).broadcast_to([P, 32, 16]), ALU.subtract))
            dve.sem_inc(sc_ready, 1)
            dve.wait_ge(ec_ready, 1)
            sc4 = SCc.rearrange("p (q h c) -> p q h c", q=4, c=16)
            step(dve.tensor_tensor(sc4, sc4, cc("valid_p").rearrange("p (q c) -> p q c", q=4).unsqueeze(2)
                                   .broadcast_to([P, 4, HEADS, 16]), ALU.mult))
            dve.sem_inc(ecm_ready, 1)
            step(dve.tensor_reduce(csum[:], sc3, AX_X, ALU.add))
            step(dve.tensor_scalar(csum[:], csum[:], 1.0, None, ALU.max))
            step(dve.reciprocal(csum[:], csum[:]))

            def combine(qt):
                gate = Gn[:, qt].rearrange("p (b g m) -> p b m g", b=3, g=KVH)
                n = 16 * qt
                if qt == 0:
                    dve.wait_ge(gt_ready, 1)
                dve.wait_ge(e_ready, n + 16)
                step(dve.tensor_scalar(lsum[:, n:n + 16], lsum[:, n:n + 16], 1.0, None, ALU.max))
                step(dve.reciprocal(lsum[:, n:n + 16], lsum[:, n:n + 16]))
                w = wts[:].rearrange("p b (m g) -> p b m g", g=KVH)
                step(dve.tensor_tensor(w[:, 0], csum[:, 8 * qt:8 * qt + 8].rearrange("p (m g) -> p m g", g=KVH),
                                       gate[:, 0], ALU.mult))
                for b in range(2):
                    step(dve.tensor_tensor(w[:, 1 + b], lsum[:, n + 8 * b:n + 8 * b + 8]
                                           .rearrange("p (m g) -> p m g", g=KVH), gate[:, 1 + b], ALU.mult))

                def weighted(out, o, b):
                    step(dve.tensor_tensor(out.rearrange("p (h d) -> p h d", d=HD),
                                           o.rearrange("p (h d) -> p h d", d=HD),
                                           wts[:, b].unsqueeze(2).broadcast_to([P, HEADS, HD]), ALU.mult))

                dve.wait_ge(oc_done, qt + 1)
                if qt:
                    dve.wait_ge(yt_done, qt)
                else:
                    dve.wait_ge(ptc_done, 1)
                weighted(YN, bank[6][:, :], 0)
                dve.wait_ge(pv_done, n + 16)
                for b in range(2):
                    weighted(SCc, bank[4 + b][:, :], 1 + b)
                    step(dve.tensor_tensor(YN, YN, SCc, ALU.add))
                dve.sem_inc(y_nat, 1)

            for n in range(N_UNITS):
                qt, br, pos, L = unit(n)
                head = pos // 2 + GRP * (pos % 2)
                dve.wait_ge(s_done, n + 1)
                if n >= 2:
                    dve.wait_ge(e_ready, n - 1)
                s = Sb[n % 2][:, 0:L]
                step(dve.scalar_tensor_tensor(s, cc("dist")[:, SEQ - L:SEQ], -2.0**-(head + 1), bank[n % 2][:, 0:L],
                                              ALU.mult, ALU.add))
                dve.tensor_reduce(nmax[:, n:n + 1], s, AX_X, ALU.max, negate=True).then_inc(sb_ready, 1)
                if n % 16 == 1 and qt:
                    combine(qt - 1)
            combine(3)

            dve.wait_ge(qn_done, 1)
            step(dve.tensor_copy(QN, bank[6][0:NB, :]))
            dve.sem_inc(qn_ready, 1)
            dve.wait_ge(kn_done, 1)
            step(dve.tensor_copy(KN.rearrange("p s n -> p (s n)"), bank[7][0:NB, :]))
            step(dve.tensor_copy(pt8f[:], pt8[:]))
            step(dve.tensor_tensor(gmask[:], cc("gate_k", 24).unsqueeze(2).broadcast_to([24, 12, NB]),
                                   Gt[:, SEQ:T].unsqueeze(1).broadcast_to([24, 12, NB]), ALU.mult))
            dve.sem_inc(gm_ready, 1)
            dve.wait_ge(qr_done, 1)
            q4 = bank[5][:, :].rearrange("p (m g d) -> p m g d", m=GRP, g=KVH)
            step(dve.tensor_scalar(QR, q4[:, :, 0], cc("group")[:, 1:2], None, ALU.mult))
            step(dve.scalar_tensor_tensor(QR, q4[:, :, 1], cc("group")[:, 2:3], QR, ALU.mult, ALU.add))
            dve.wait_ge(gb_done, 1)
            step(dve.tensor_copy(gbc[:].rearrange("p a m b -> p (a m b)"), bank[4][:, 0:96]))
            dve.sem_inc(qr_ready, 1)

            dve.wait_ge(qs_done, 1)
            for g in range(KVH):
                step(dve.tensor_copy(sm[:, 0:64].rearrange("p (b g m) -> p b g m", g=KVH, m=GRP)[:, :, g, :],
                                     bank[6 + g][:, 0:32].rearrange("p (b m) -> p b m", m=GRP)))
            dve.sem_inc(qs_copied, 1)
            ps = sm[0:64, 64:192]
            dve.wait_ge(st_done, 1)
            step(dve.tensor_tensor(ps, bank[4][0:64, 0:P], cc("bias_s", 64), ALU.add))
            step(dve.tensor_reduce(small[0:64, 0:1], ps, AX_X, ALU.max, negate=True))
            dve.sem_inc(ss_ready, 1)
            dve.wait_ge(es_ready, 1)
            step(dve.tensor_scalar(small[0:64, 1:2], small[0:64, 1:2], 1.0, None, ALU.max))
            step(dve.reciprocal(small[0:64, 1:2], small[0:64, 1:2]))
            step(dve.tensor_scalar(ps, ps, small[0:64, 1:2], None, ALU.mult))
            dve.sem_inc(p_ready, 1)
            dve.wait_ge(imp_done, 1)
            imp = sm[0:16, 192:256]
            step(dve.tensor_reduce(imp, bank[5][0:16, 0:P].rearrange("p (s t) -> p s t", t=2), AX_X, ALU.add))
            step(dve.tensor_tensor(imp, imp, cc("force", 16), ALU.add))
            step(dve.max(small[0:16, 8:16], imp))
            step(dve.max_index(smi[:], small[0:16, 8:16], imp))
            step(dve.tensor_copy(small[0:16, 16:24], smi[:]))
            step(dve.memset(small[0:16, 23:24], 0.0))
            dve.sem_inc(idx_ready, 1)
            step(dve.tensor_copy(sm[:, 256:320], bank[4][:, 0:64]))
            dve.sem_inc(pts_ready, 1)
            dve.wait_ge(idx_done, 1)
            blk, pgf, half, row = (small[:, 32 + j:33 + j] for j in range(4))
            step(dve.tensor_tensor(small[:, 40:48], bank[7][:, 0:8], cc("slot"), ALU.mult))
            step(dve.tensor_reduce(blk, small[:, 40:48], AX_X, ALU.add))
            step(dve.tensor_copy(rowi[:, 1:2], blk))
            step(dve.tensor_scalar(rowi[:, 2:3], rowi[:, 1:2], 1, None, ALU.logical_shift_right))
            step(dve.tensor_copy(pgf, rowi[:, 2:3]))
            step(dve.scalar_tensor_tensor(half, pgf, -2.0, blk, ALU.mult, ALU.add))
            step(dve.tensor_scalar(small[:, 64:96], cc("iota"), pgf, None, ALU.is_equal))
            step(dve.tensor_tensor(small[:, 64:96], small[:, 64:96], bank[7][:, 8:40], ALU.mult))
            step(dve.tensor_reduce(row, small[:, 64:96], AX_X, ALU.add))
            step(dve.scalar_tensor_tensor(row, row, 2.0, half, ALU.mult, ALU.add))
            step(dve.scalar_tensor_tensor(row, row, 2.0, cc("group")[:, 0:1], ALU.mult, ALU.add))
            step(dve.tensor_copy(rowi[:, 0:1], row))
            dve.sem_inc(row_ready, 1)
            dsel = small[:, 128:192]
            step(dve.tensor_scalar(half, blk, -float(SELB), float(PAST), ALU.mult, ALU.add))
            step(dve.tensor_scalar(dsel, cc("npos"), half, cc("keep"), ALU.add, ALU.mult))
            step(dve.tensor_tensor(dsel, dsel, cc("add7"), ALU.add))

            dve.wait_ge(stored, 32)
            P3 = PROD.rearrange("p (n d) -> p n d", d=HD)
            for n, br in enumerate((1, 0)):
                if br:
                    dve.wait_ge(kn_in_w, 64)
                    dve.wait_ge(qs_done, 1)
                else:
                    dve.wait_ge(kn_in, 64)
                K, V = (x.rearrange("p (n d) -> p n d", d=HD) for x in KVT[br])
                for m in range(GRP):
                    step(dve.tensor_tensor(P3, K, QR[:, m].unsqueeze(1).broadcast_to([P, SELB, HD]), ALU.mult))
                    step(dve.tensor_reduce(SE[:, br, m, :], P3, AX_X, ALU.add))
                    step(dve.scalar_tensor_tensor(SE[:, br, m, :], cc("dist_w") if br else dsel, -2.0**-(m + 1),
                                                  SE[:, br, m, :], ALU.mult, ALU.add))
                step(dve.tensor_reduce(stat[:, 0, GRP * br:GRP * br + GRP], SE[:, br], AX_X, ALU.max))
                step(dve.tensor_tensor(SE[:, br], SE[:, br], stat[:, 0, GRP * br:GRP * br + GRP].unsqueeze(2)
                                       .broadcast_to([P, GRP, SELB]), ALU.subtract))
                dve.sem_inc(se_ready, 1)
                dve.wait_ge(ex_ready, n + 1)
                step(dve.tensor_reduce(stat[:, 1, GRP * br:GRP * br + GRP], SE[:, br], AX_X, ALU.add))
                for m in range(GRP):
                    step(dve.tensor_tensor(P3, V, SE[:, br, m].unsqueeze(2).broadcast_to([P, SELB, HD]), ALU.mult))
                    step(dve.tensor_reduce(O2[:, br, m, :], P3.rearrange("p n d -> p d n"), AX_X, ALU.add))
                dve.sem_inc(o2_ready, 1)
            dve.wait_ge(stt_done, 1)
            step(dve.tensor_copy(stT, bank[6][0:8, 0:256].rearrange("p (a n) -> p a n", a=2)))
            by_group = [stT[:, a].rearrange("p (g c) -> p g c", c=SLOTS) for a in range(2)]

            def per_group(x):
                return x.unsqueeze(2).broadcast_to([8, 16, SLOTS])

            step(dve.tensor_reduce(stW[:, 0], by_group[0], AX_X, ALU.max))
            step(dve.tensor_tensor(by_group[0], by_group[0], per_group(stW[:, 0]), ALU.subtract))
            dve.sem_inc(w8_ready, 1)
            dve.wait_ge(ew_ready, 1)
            step(dve.tensor_tensor(stT[:, 1], stT[:, 1], stT[:, 0], ALU.mult))
            step(dve.tensor_reduce(stW[:, 1], by_group[1], AX_X, ALU.add))
            step(dve.tensor_scalar(stW[:, 1], stW[:, 1], 1.0, None, ALU.max))
            step(dve.reciprocal(stW[:, 2], stW[:, 1]))
            step(dve.tensor_tensor(by_group[0], by_group[0], per_group(stW[:, 2]), ALU.mult))
            dve.sem_inc(wn_ready, 1)
            dve.wait_ge(wn_done, 1)
            step(dve.tensor_copy(wn[:], bank[6][:, 256:264]))
            o2v = O2.rearrange("p b m d -> p (b m) d")
            step(dve.tensor_tensor(o2v, o2v, wn[:].unsqueeze(2).broadcast_to([P, 8, HD]), ALU.mult))
            dve.sem_inc(o2_scaled, 1)
            dve.wait_ge(ot_done, 1)
            for g in range(KVH):
                r = slice(g * HD, g * HD + HD)
                step(dve.tensor_tensor(ya[r, 0], bank[5][r, P:P + 64].rearrange("p (b h) -> p h b", h=HEADS)
                                       [:, GRP * g:GRP * g + GRP, :], gbc[r, 0], ALU.mult))
            step(dve.tensor_tensor(ya[:, 1:3].rearrange("p a m b -> p (a m b)"), bank[7][:, 64:128],
                                   gbc[:, 1:3].rearrange("p a m b -> p (a m b)"), ALU.mult))
            step(dve.tensor_tensor(ya[:, 0], ya[:, 0], ya[:, 1], ALU.add))
            step(dve.tensor_tensor(Z[:, Z_CC:Z_CC + GRP, SEQ:T], ya[:, 0], ya[:, 2], ALU.add))
            dve.sem_inc(ya_ready, 1)

            dve.sem_inc(mo_ready, 2)
            dve.wait_ge(x_again, 48)
            with dve.Fori(0, 4) as i:
                for b in range(2):
                    dve.wait_ge(mo_done, 2 * i + b + 1)
                    for c, (lo, hi_) in enumerate(CHUNKS):
                        x = X[:, bass.ds(2 * i + b, 1), lo:hi_].rearrange("p o t -> p (o t)")
                        mm = dve.tensor_tensor(x, x, bank[2 * b + c][:, 0:HALF], ALU.add)
                    mm.then_inc(mo_ready, 1)
            dve.wait_ge(mo_ready, KD + 2)
            dve.wait_ge(ms_ready, 2)
            rms_vector(dve, step, 1, lambda k: X[:, k, :], lambda k: H[:, k, :])

            dve.wait_ge(lg_done, 1)
            step(dve.tensor_copy(lg, bank[4][0:104, 0:100].rearrange("p (j e) -> p j e", j=5)))
            s5 = [small[0:104, 192 + 5 * j:197 + 5 * j] for j in range(12)]

            def over4(x):
                return x.unsqueeze(2).broadcast_to([104, 5, 4])

            def first_max(x, top, oh):
                step(dve.tensor_reduce(top, x, AX_X, ALU.max))
                step(dve.tensor_tensor(oh, x, over4(top), ALU.is_equal))
                step(dve.tensor_tensor(oh, oh, cc("rank", 104).unsqueeze(1).broadcast_to([104, 5, 4]), ALU.mult))
                step(dve.tensor_reduce(s5[11], oh, AX_X, ALU.max))
                step(dve.tensor_tensor(oh, oh, over4(s5[11]), ALU.is_equal))

            e_g, e_4, oh_g, oh_1, oh_2, le4, c4 = (rt[:, j] for j in range(7))
            t16 = rt[:, 8:12].rearrange("p a j k -> p (a j k)").rearrange("p (j g k) -> p j g k", j=5, g=4)
            c16 = comb.rearrange("p j (g k) -> p j g k", g=4)
            l16 = lg[:, :, 4:20].rearrange("p j (g k) -> p j g k", g=4)
            first_max(lg[:, :, 0:4], s5[0], oh_g)
            step(dve.tensor_tensor(e_g, lg[:, :, 0:4], over4(s5[0]), ALU.subtract))
            dve.sem_inc(rx_ready, 1)
            for j in range(5):
                step(dve.tensor_tensor(t16[:, j], l16[:, j], oh_g[:, j].unsqueeze(2).broadcast_to([104, 4, 4]),
                                       ALU.mult))
            for j in range(5):
                step(dve.tensor_reduce(le4[:, j], t16[:, j].rearrange("p g k -> p k g"), AX_X, ALU.add))
            step(dve.tensor_reduce(s5[1], le4, AX_X, ALU.max))
            step(dve.tensor_tensor(e_4, le4, over4(s5[1]), ALU.subtract))
            dve.sem_inc(rx_ready, 1)
            dve.wait_ge(re_ready, 1)
            step(dve.tensor_reduce(s5[2], e_g, AX_X, ALU.add))
            step(dve.reciprocal(s5[2], s5[2]))
            dve.wait_ge(re_ready, 2)
            first_max(e_4, s5[3], oh_1)
            step(dve.scalar_tensor_tensor(e_4, oh_1, -2.0, e_4, ALU.mult, ALU.add))
            first_max(e_4, s5[4], oh_2)
            step(dve.tensor_tensor(s5[5], s5[3], s5[4], ALU.add))
            step(dve.reciprocal(s5[5], s5[5]))
            step(dve.tensor_tensor(s5[5], s5[5], s5[2], ALU.mult))
            step(dve.tensor_tensor(s5[3], s5[3], s5[5], ALU.mult))
            step(dve.tensor_tensor(s5[4], s5[4], s5[5], ALU.mult))
            step(dve.tensor_tensor(oh_1, oh_1, over4(s5[3]), ALU.mult))
            step(dve.tensor_tensor(oh_2, oh_2, over4(s5[4]), ALU.mult))
            step(dve.tensor_tensor(c4, oh_1, oh_2, ALU.add))
            for j in range(5):
                step(dve.tensor_tensor(c16[:, j], oh_g[:, j].unsqueeze(2).broadcast_to([104, 4, 4]),
                                       c4[:, j].unsqueeze(1).broadcast_to([104, 4, 4]), ALU.mult))
            dve.sem_inc(comb_ready, 1)
            dve.wait_ge(ct_done, 1)
            step(dve.tensor_copy(combT[:, 0:416], bank[5][0:N_EXP, 0:416]))
            dve.sem_inc(ct_ready, 1)
            step(dve.tensor_copy(combT[:, 416:T], bank[6][0:N_EXP, 0:104]))
            dve.sem_inc(ct_ready, 1)

            dve.sem_inc(dn_ready, KD + 1)

            def up_mul(e, b):
                for f in range(2):
                    dve.wait_ge(silu_ready, 2 * e + f + 1)
                    for c, (lo, hi_) in enumerate(CHUNKS):
                        a = A[b][:, f, lo:hi_]
                        mm = dve.tensor_tensor(a, a, bank[4 * ((b + f) % 2) + 2 + c][:, 0:HALF], ALU.mult)
                    mm.then_inc(up_ready, 1)

            def add_down(e, b):
                with dve.Fori(0, 4) as n:
                    for j in range(2):
                        dve.wait_ge(dn_done, 8 * e + 2 * n + j + 1)
                        for c, (lo, hi_) in enumerate(CHUNKS):
                            x = X[:, bass.ds(2 * n + j, 1), lo:hi_].rearrange("p o t -> p (o t)")
                            mm = dve.tensor_tensor(x, x, bank[4 * (1 - b) + 2 * j + c][:, 0:HALF], ALU.add)
                        mm.then_inc(dn_ready, 1)

            up_mul(0, 0)
            with dve.Fori(0, N_EXP // 2 - 1) as i:
                for b in range(2):
                    up_mul(2 * i + 1 + b, 1 - b)
                    add_down(2 * i + b, b)
            up_mul(N_EXP - 1, 1)
            add_down(N_EXP - 2, 0)
            add_down(N_EXP - 1, 1)
            dve.wait_ge(dn_ready, 8 * N_EXP + 9)
            dve.wait_ge(ms_ready, 3)
            rms_vector(dve, step, 2, lambda k: X[:, k, :], lambda k: H[:, k, :])

        @block.tensor
        def _(pe):
            pe.wait_ge(dve_const, 1)
            rms_tensor(pe, 0)

            def z_tile(t):
                if t == 0:
                    pe.wait_ge(rms_ready, 2)
                pe.wait_ge(w_in[t % 2], 16 * (t // 2 + 1))
                if t >= 2:
                    pe.wait_ge(z_ready, t - 1)
                for k in range(KD):
                    if t == 0:
                        pe.wait_ge(norm_ready, k + 1)
                    for c, (a, b) in enumerate(CHUNKS):
                        mm = pe.matmul(bank[2 * (t % 2) + c][:, 0:HALF], W_RING[:, t % 2, k, :], H[:, k, a:b],
                                       start=(k == 0), stop=(k == KD - 1))
                mm.then_inc(z_done, 1)

            def bu(i):
                if i >= 1:
                    pe.wait_ge(v_done, i)
                    pe.wait_ge(ris_ready, i)
                r = slice(32 * (i % 4), 32 * (i % 4) + 32)
                for part in range(2):
                    w = BT[r, i // 4, part, :]
                    pe.matmul(bank[4 + part][:, :], w, Z[r, i // 4, 0:SEQ], start=True, stop=True,
                              tile_position=(32 * (i % 4), 0))
                    mm = pe.matmul(bank[7][:, NB * part:NB * part + NB], w, Z[r, i // 4, SEQ:T], start=True,
                                   stop=True, tile_position=(32 * (i % 4), 0))
                mm.then_inc(bu_ready, 1)

            def y(i):
                r = slice(32 * (i % 4), 32 * (i % 4) + 32)
                pe.wait_ge(h_ready, i + 1)
                if i >= 4:
                    pe.wait_ge(skip_ready, i // 4)
                pe.matmul(bank[6][r, :], CT[:, i, 0, :], hr, start=True, stop=False, tile_position=(0, r.start))
                pe.matmul(bank[6][r, :], CT[:, i, 1, :], hi, start=False, stop=True,
                          tile_position=(0, r.start)).then_inc(y_done, 1)

            pe.wait_ge(small_in, 9 * 16)
            for t in range(3):
                z_tile(t)
            pe.wait_ge(z_ready, 3)
            bu(0)
            for i in range(SN):
                for t in beside[i]:
                    z_tile(t)
                if i == 9:
                    pe.wait_ge(wg_in, 16)
                    pe.wait_ge(z_ready, NZ - 1)
                    for k in range(KD):
                        for c, (a, b) in enumerate(CHUNKS):
                            mm = pe.matmul(bank[c][0:24, 0:HALF],
                                           wgt[:, k, :], H[:, k, a:b], start=(k == 0), stop=(k == KD - 1))
                    mm.then_inc(z_done, 1)
                if i + 1 < SN:
                    bu(i + 1)
                y(i)
            pe.wait_ge(skip_ready, ST)
            pe.wait_ge(hs_ready, 1)
            for i in range(SN):
                r = slice(32 * (i % 4), 32 * (i % 4) + 32)
                c = i // 4
                for part in range(2):
                    mm = pe.matmul(bank[6][r, NB * c:NB * c + NB], CT[:, i, part, :], hlast[:, i, part, 1:],
                                   start=(part == 0), stop=(part == 1), tile_position=(0, r.start))
            mm.then_inc(ys_done, 1)
            pe.wait_ge(gelu_ready, ST + 1)
            pe.wait_ge(z_ready, NZ + 1)
            for n in range(ST):
                if n >= 2:
                    pe.wait_ge(glu_sig, n - 1)
                for k in range(ST):
                    for c, (a, b) in enumerate(CHUNKS):
                        mm = pe.matmul(bank[2 * (n % 2) + c][:, 0:HALF], w_glu[:, k, n * P:(n + 1) * P],
                                       Z[:, k, a:b], start=(k == 0), stop=(k == ST - 1))
                mm.then_inc(glu_done, 1)

            pe.wait_ge(cst_in, 5 * 16)
            pe.wait_ge(glu_sig, ST)
            for v in range(2):
                for r in range(16):
                    mm = pe.matmul(bank[3][v * HD:v * HD + HD, 0:1], w1[:, v, r, :], pe_t[:, v, r:r + 1],
                                   start=(r == 0), stop=(r == 15), tile_position=(0, v * HD))
            mm.then_inc(cb_done, 1)

            def hidden(out, rhs):
                for v in range(2):
                    for r in range(16):
                        mm = pe.matmul(out[v * HD:v * HD + HD], w1[:, v, r, :], rhs(v, r), start=(r == 0),
                                       stop=(r == 15), tile_position=(0, v * HD))
                mm.then_inc(hid_done, 1)

            def second(hid, n, kc, vc):
                for g in range(KVH):
                    pe.matmul(vc[0:n, g * HD:g * HD + HD], hid[:, g * n:g * n + n], w2[:, 1, :], start=True, stop=True)
                for g in range(KVH):
                    mm = pe.matmul(kc[g * HD:g * HD + HD, 0:n], w2[:, 0, :], hid[:, g * n:g * n + n], start=True,
                                   stop=True, tile_position=(0, g * HD))
                mm.then_inc(kc_done, 1)

            pe.wait_ge(xp_in, 8 * 16)
            hidden(bank[0][:, 0:32], lambda v, r: XP[:, v, :, r, :])
            pe.wait_ge(cb_ready, 1)
            pe.wait_ge(hid_ready, 1)
            second(HID[:, 0], 16, bank[2], bank[3])
            pe.wait_ge(kc_ready, 2)
            pe.matmul(bank[3][:, 0:P], cc("rep_c", 16), vcp[:], start=True, stop=True).then_inc(vb_rep, 1)

            for b in range(2):
                for kt in range(4):
                    mm = pe.transpose(bank[4 + b][:, kt * P:(kt + 1) * P], Z[:, Z_KV + 3 + 2 * b, kt * P:(kt + 1) * P],
                                      identity)
                mm.then_inc(vt_done, 1)
            for qt in range(4):
                mm = pe.transpose(bank[7][:, 24 * qt:24 * qt + 24], Gt[:, qt * P:(qt + 1) * P], identity[0:24, 0:24])
            mm.then_inc(gt_done, 1)
            for qt in range(4):
                for pos in range(HEADS):
                    m, g = divmod(pos, 2)
                    r = slice(g * HD, g * HD + HD)
                    at = (qt * GRP + m) * 16
                    mm = pe.matmul(bank[6 if g == 0 else 1][:, at:at + 16], Z[r, Z_Q + m, qt * P:(qt + 1) * P], kcp[r, :], start=True,
                                   stop=True, tile_position=(g * HD, 0))
            mm.then_inc(sc_done, 1)

            def scores(n):
                qt, br, pos, L = unit(n)
                m, g = divmod(pos, 2)
                r = slice(g * HD, g * HD + HD)
                if n >= 2:
                    pe.wait_ge(sb_ready, n - 1)
                pe.matmul(bank[n % 2][:, 0:L], Z[r, Z_Q + m, qt * P:(qt + 1) * P], Z[r, Z_KV + 2 + 2 * br, 0:L],
                          start=True, stop=True, tile_position=(g * HD, 0)).then_inc(s_done, 1)

            def turn(n):
                L = unit(n)[3]
                pe.wait_ge(e_ready, n + 1)
                if n >= 2:
                    pe.wait_ge(pt_ready, n - 1)
                for k in range(L // P):
                    mm = pe.transpose(bank[2 + n % 2][:, k * P:(k + 1) * P], Ex[n % 2][:, k * P:(k + 1) * P], identity)
                mm.then_inc(t_done, 1)

            def pv(n):
                qt, br, pos, L = unit(n)
                g = pos % 2
                pe.wait_ge(pt_ready, n + 1)
                if n == 0:
                    pe.wait_ge(vt_ready, 2)
                if n % 16 == 0 and qt:
                    pe.wait_ge(y_nat, qt)
                for k in range(L // P):
                    mm = pe.matmul(bank[4 + br][:, pos * HD:pos * HD + HD], PT[n % 2][:, k * P:(k + 1) * P],
                                   VN[:, br, k, g * HD:g * HD + HD], start=(k == 0), stop=(k == L // P - 1))
                mm.then_inc(pv_done, 1)

            def out_c(qt):
                if qt:
                    pe.wait_ge(y_nat, qt)
                pe.matmul(bank[6][:, :], PTC[:, qt * P:(qt + 1) * P], VB, start=True, stop=True).then_inc(oc_done, 1)

            def y_turn(qt):
                pe.wait_ge(y_nat, qt + 1)
                pe.wait_ge(kc_ready, 2 + 4 * (qt + 1))
                for m in range(GRP):
                    mm = pe.transpose(bank[7][:, m * P:(m + 1) * P], YN[:, m * P:(m + 1) * P], identity)
                mm.then_inc(yt_done, 1)

            pe.wait_ge(kc_ready, 2)
            scores(0)
            pe.wait_ge(ecm_ready, 1)
            pe.wait_ge(gt_ready, 1)
            for qt in range(4):
                mm = pe.transpose(bank[7][:, qt * P:(qt + 1) * P], SCc[:, qt * P:(qt + 1) * P], identity)
            mm.then_inc(ptc_done, 1)
            pe.wait_ge(ptc_ready, 1)
            pe.wait_ge(vb_ready, 1)
            pe.wait_ge(yconv_ready, 1)

            def hidden_part(smp, part):
                b = smp % 2
                if part == 0:
                    pe.wait_ge(pages_in[b], 8 * PAGES * (smp // 2 + 1))
                    pe.wait_ge(odd_pages_in[b], 8 * PAGES * (smp // 2 + 1))
                    pe.wait_ge(kc_ready, 2 + 2 * smp)
                    if b == 0 and smp:
                        pe.wait_ge(yt_ready, smp // 2)
                for at in range(32 * part // 5, 32 * (part + 1) // 5):
                    v, r = divmod(at, 16)
                    mm = pe.matmul(bank[7][v * HD:v * HD + HD, 0:2 * NCB], w1[:, v, r, :],
                                   page[b][:, :, v, :, r, :].rearrange("p g h c -> p h g c"), start=(r == 0),
                                   stop=(r == 15), tile_position=(0, v * HD))
                if part == 4:
                    mm.then_inc(hid_done, 1)

            def second_layer(smp):
                pe.wait_ge(hid_ready, smp + 2)
                second(HID[:, smp % 2], NCB, bank[7][:, 2 * NCB:3 * NCB], bank[7][:, 3 * NCB:4 * NCB])

            for n in range(N_UNITS):
                qt, at = divmod(n, 16)
                if n + 1 < N_UNITS:
                    scores(n + 1)
                turn(n)
                if n >= 1:
                    pv(n - 1)
                if at == 0:
                    out_c(qt)
                if at == 1 and qt:
                    second_layer(2 * qt - 1)
                if at == 2 and qt:
                    y_turn(qt - 1)
                if 4 <= at < 9:
                    hidden_part(2 * qt, at - 4)
                if at == 10:
                    second_layer(2 * qt)
                if at >= 11:
                    hidden_part(2 * qt + 1, at - 11)
            pv(N_UNITS - 1)
            second_layer(NB - 1)
            y_turn(3)

            for m in range(GRP):
                mm = pe.transpose(bank[6][0:NB, m * P:(m + 1) * P], Z[:, Z_Q + m, SEQ:T], identity)
            mm.then_inc(qn_done, 1)
            pe.wait_ge(yt_ready, 4)
            for j in range(4):
                mm = pe.transpose(bank[7][0:NB, j * P:(j + 1) * P], Z[:, Z_KV + 2 + j, SEQ:T], identity)
            mm.then_inc(kn_done, 1)
            pe.wait_ge(qn_ready, 1)
            pe.matmul(bank[5][:, :], cc("rep8", NB), QN, start=True, stop=True).then_inc(qr_done, 1)
            pe.wait_ge(gm_ready, 1)
            pe.matmul(bank[4][:, 0:96], cc("gate_g", 24), gmask[:].rearrange("p a b -> p (a b)"), start=True,
                      stop=True).then_inc(gb_done, 1)
            pe.wait_ge(qr_ready, 1)

            pe.wait_ge(kc_ready, 2 + 2 * NB)
            for g in range(KVH):
                r = slice(g * HD, g * HD + HD)
                for b in range(NB):
                    mm = pe.matmul(bank[6 + g][:, GRP * b:GRP * b + GRP], KCT[r, b, :], Z[r, Z_Q:Z_Q + GRP, SEQ + b],
                                   start=True, stop=True, tile_position=(g * HD, 0))
            mm.then_inc(qs_done, 1)
            pe.wait_ge(qs_copied, 1)
            pe.transpose(bank[4][0:64, 0:P], sm[:, 0:64], identity).then_inc(st_done, 1)
            pe.wait_ge(p_ready, 1)
            pe.transpose(bank[4][:, 0:64], sm[0:64, 64:192], identity[0:64, 0:64])
            pe.matmul(bank[5][0:16, 0:P], cc("sum_g", 64), sm[0:64, 64:192], start=True, stop=True)\
                .then_inc(imp_done, 1)
            pe.wait_ge(idx_ready, 1)
            pe.matmul(bank[7][:, 0:8], cc("rep16", 16), small[0:16, 16:24], start=True, stop=True)
            pe.matmul(bank[7][:, 8:40], cc("rep8", NB), pt8f[:], start=True, stop=True).then_inc(idx_done, 1)
            pe.wait_ge(pts_ready, 1)
            for b in range(NB):
                mm = pe.matmul(bank[5][:, P + HEADS * b:P + HEADS * b + HEADS], VC[:, b, :],
                               sm[:, 256 + HEADS * b:256 + HEADS * b + HEADS], start=True, stop=True)
            mm.then_inc(ocs_done, 1)

            def merge(br, y0):
                nk = BRANCH_K[br]
                with pe.Fori(0, 4) as i:
                    for b in range(2):
                        q = 8 * br + 2 * i + b
                        pe.wait_ge(w_in[b], 16 * (NZ // 2 + 4 * br + i + 1))
                        pe.wait_ge(mz_ready, q + 1)
                        for k in range(KD):
                            for c, (lo, hi_) in enumerate(CHUNKS):
                                mm = pe.matmul(bank[c][:, 0:HALF], W_RING[:, b, k, :], H[:, k, lo:hi_], start=(k == 0),
                                               stop=(k == KD - 1))
                        mm.then_inc(mz_done, 1)
                        pe.wait_ge(wb_in[b], 16 * (4 * br + i + 1))
                        pe.wait_ge(mb_ready, q + 1)
                        for k in range(nk):
                            for c, (lo, hi_) in enumerate(CHUNKS):
                                mm = pe.matmul(bank[2 + c][:, 0:HALF], WB[:, b, k, :], Z[:, y0 + k, lo:hi_],
                                               start=(k == 0), stop=(k == nk - 1))
                        mm.then_inc(mb_done, 1)

            merge(0, Z_U)
            merge(1, Z_CB)
            pe.wait_ge(o2_ready, 2)
            for a in range(2):
                mm = pe.transpose(bank[6][0:8, a * P:(a + 1) * P], stat[:, a, :], identity)
            mm.then_inc(stt_done, 1)
            pe.wait_ge(wn_ready, 1)
            pe.transpose(bank[6][:, 256:264], stT[:, 0, :], identity[0:8, 0:8]).then_inc(wn_done, 1)
            pe.wait_ge(o2_scaled, 1)
            for br in range(2):
                for m in range(GRP):
                    for g in range(KVH):
                        at = 64 + (GRP * br + m) * NB
                        mm = pe.matmul(bank[7][g * HD:g * HD + HD, at:at + NB], O2[:, br, m, :],
                                       cc("sel_g").rearrange("p (g b) -> p g b", g=KVH)[:, g, :], start=True, stop=True,
                                       tile_position=(0, g * HD))
            mm.then_inc(ot_done, 1)
            pe.wait_ge(ya_ready, 1)
            merge(2, Z_CC)
            pe.wait_ge(mm_ready, 26)
            pe.wait_ge(mb_ready, 25)
            with pe.Fori(0, 4) as i:
                for b in range(2):
                    pe.wait_ge(w_in[b], 16 * (NZ // 2 + 12 + i + 1))
                    pe.wait_ge(mo_ready, 2 * i + b + 1)
                    for k in range(KD):
                        for c, (lo, hi_) in enumerate(CHUNKS):
                            mm = pe.matmul(bank[2 * b + c][:, 0:HALF], W_RING[:, b, k, :], M[:, k, lo:hi_],
                                           start=(k == 0), stop=(k == KD - 1))
                    mm.then_inc(mo_done, 1)

            pe.wait_ge(mo_ready, KD + 2)
            rms_tensor(pe, 1)
            pe.wait_ge(x_again, 48)
            pe.wait_ge(norm_ready, 2 * KD)
            for j in range(5):
                out = bank[4][0:104, 20 * j:20 * j + 20]
                pe.matmul(out, ones[0:1, 0:104], rb[:], start=True, stop=False)
                for k in range(KD):
                    mm = pe.matmul(out, H[:, k, 104 * j:104 * j + 104], rw[:, k, :], start=False, stop=(k == KD - 1))
            mm.then_inc(lg_done, 1)
            pe.wait_ge(comb_ready, 1)
            for j in range(5):
                out = bank[5][0:N_EXP, 104 * j:104 * j + 104] if j < 4 else bank[6][0:N_EXP, 0:104]
                mm = pe.transpose(out, comb[:, j, :], identity[0:104, 0:104])
            mm.then_inc(ct_done, 1)
            pe.wait_ge(ct_ready, 2)

            def gate_up(e, b):
                pe.wait_ge(gu_in[b], 16 * (e // 2 + 1) if isinstance(e, int) else 16 * e[1])
                e = e if isinstance(e, int) else e[0]
                for f in range(2):
                    if f == 1:
                        pe.wait_ge(dn_ready, 8 * e + 1)
                    elif not (isinstance(e, int) and e == 0):
                        pe.wait_ge(up_ready, 2 * e)
                    for w in range(2):
                        for k in range(KD):
                            for c, (lo, hi_) in enumerate(CHUNKS):
                                mm = pe.matmul(bank[4 * ((b + f) % 2) + 2 * w + c][:, 0:HALF],
                                               GU[b][:, w, k, f * P:(f + 1) * P], H[:, k, lo:hi_], start=(k == 0),
                                               stop=(k == KD - 1))
                    mm.then_inc(gu_done, 1)

            def down(e, b, uses):
                pe.wait_ge(a_ready, 2 * e + 2)
                pe.wait_ge(wd_in[b], 16 * uses)
                for n in range(KD):
                    if n >= 2:
                        pe.wait_ge(dn_ready, 8 * e + n - 1 + 9)
                    for f in range(2):
                        for c, (lo, hi_) in enumerate(CHUNKS):
                            mm = pe.matmul(bank[4 * (1 - b) + 2 * (n % 2) + c][:, 0:HALF],
                                           WD[b][:, f, n * P:(n + 1) * P], A[b][:, f, lo:hi_], start=(f == 0),
                                           stop=(f == 1))
                    mm.then_inc(dn_done, 1)

            gate_up(0, 0)
            with pe.Fori(0, N_EXP // 2 - 1) as i:
                gate_up((2 * i + 1, i + 1), 1)
                pe.wait_ge(up_ready, 4 * i + 3)
                down(2 * i, 0, i + 1)
                gate_up((2 * i + 2, i + 2), 0)
                pe.wait_ge(up_ready, 4 * i + 5)
                down(2 * i + 1, 1, i + 1)
            gate_up(N_EXP - 1, 1)
            pe.wait_ge(up_ready, 2 * N_EXP - 1)
            down(N_EXP - 2, 0, N_EXP // 2)
            pe.wait_ge(up_ready, 2 * N_EXP)
            down(N_EXP - 1, 1, N_EXP // 2)
            rms_tensor(pe, 2)


def tiles(w):
    k, n = w.shape
    return w.reshape(k // P, P, n // P, P).transpose(2, 1, 0, 3)


def rows(v):
    return np.moveaxis(v.reshape(*v.shape[:-1], v.shape[-1] // P, P), -1, 0)


def lay_out(i):
    x = np.concatenate([i["x_prompt"][0], i["x_sample"][:, 0]])
    w = i["w_in"][0]
    qcols = [384 + h * HD + d for j in range(GRP) for h in (j, j + GRP) for d in range(HD)]
    cols = np.concatenate([np.arange(0, 384), qcols, np.arange(896, 1664), np.arange(1688, 2840)])
    BT = np.zeros((ST, 4, 2, SC, 2, 2, 64), np.float32)
    CT = np.zeros((SN, 2, 64, 2, 2, SC), np.float32)
    for part, (b, c) in enumerate((("ssm_b_re", "ssm_c_re"), ("ssm_b_im", "ssm_c_im"))):
        b, c = i[b][0].reshape(ST, 4, 2, 64, SC), i[c][0].reshape(SN, 2, SC, 64)
        for g in range(2):
            BT[:, :, g, :, part, g, :] = b[:, :, g].transpose(0, 1, 3, 2)
            CT[:, g, :, part, g, :] = c[:, g].transpose(0, 2, 1)

    def state(v):
        return v.reshape(SN, 2, 64).transpose(1, 2, 0).reshape(P, SN)

    ldt = np.repeat(i["ssm_log_dt"][0], 64)
    return {
        "xT": x.T.reshape(KD, P, T).transpose(1, 0, 2),
        "gains": rows(np.stack([i["norm_attn_g"][0], i["norm_ffn_g"][0], i["norm_final_g"]])),
        "w_z": tiles(w[:, cols]),
        "w_gates": w[:, 1664:1688].reshape(KD, P, 24).transpose(1, 0, 2),
        "prm": np.stack([state(i["ssm_a_re"][0]), state(i["ssm_a_im"][0]), state(ldt)], 1),
        "BT": BT.transpose(1, 2, 3, 0, 4, 5, 6).reshape(P, ST, 2, P),
        "CT": CT.transpose(1, 2, 0, 3, 4, 5).reshape(P, SN, 2, 32),
        "h0": i["state_ssm"][0].reshape(NB, SN, 2, 64, 2).transpose(2, 3, 1, 4, 0).reshape(P, SN, 2, NB),
        "sdb": rows(np.stack([i["ssm_d"][0], i["ssm_b_glu"][0]])),
        "w_glu": i["ssm_w_glu"][0].reshape(ST, P, SG * SC).transpose(1, 0, 2),
        "cw": i["conv_w"][0].reshape(3, ST, P).transpose(2, 1, 0),
        "cst": CST_ARRAY,
        "ptab": i["page_table"].reshape(1, -1),
        "pt8": i["page_table"],
        "cmp": i["cache_kv"][0][:, :, 0:2].reshape(N_POOL, 4, 16, 2, 2, KVH, HD).transpose(0, 3, 6, 4, 5, 2, 1)
        .reshape(N_POOL, P, 256),
        "w1": i["cmp_w1"][0].reshape(2, 16, 2, HD, HD).transpose(2, 3, 0, 1, 4).reshape(P, 2, 16, HD),
        "w2": np.stack([np.pad(i["cmp_w2"][0][v], ((HD * v, HD - HD * v), (0, 0))) for v in range(2)], 1),
        "pe": i["cmp_pe"][0].reshape(2, 16, 2, HD).transpose(2, 3, 0, 1).reshape(P, 2, 16),
        "win": i["cache_win"][0].transpose(2, 0, 3, 1, 4).reshape(2, -1),
        "kslc": i["cache_kv"][0][:, :, 2].reshape(N_POOL, 2, SELB, KVH, HD).transpose(0, 1, 3, 2, 4)
        .reshape(-1, SELB * HD),
        "vslc": i["cache_kv"][0][:, :, 3].reshape(N_POOL, 2, SELB, KVH, HD).transpose(0, 1, 3, 2, 4)
        .reshape(-1, SELB * HD),
        "w_m": np.concatenate([tiles(w[:, 2840 + j * D:2840 + (j + 1) * D]) for j in (0, 2, 1)]),
        "w_b0": tiles(i["w_br_ssm"][0]),
        "w_b1": tiles(i["w_br_conv"][0]),
        "w_b2": tiles(i["w_br_attn"][0][np.array(qcols) - 384]),
        "w_o": tiles(i["w_out"][0]),
        "w_r": np.concatenate([i["w_router_group"][0], i["w_router_expert"][0]], 1).reshape(KD, P, 20)
        .transpose(1, 0, 2),
        "b_r": np.concatenate([i["b_router_group"][0], i["b_router_expert"][0]])[None],
        "w_gu": np.stack([i["moe_w_gate"][0], i["moe_w_up"][0]], 1).reshape(N_EXP, 2, KD, P, FF)
        .transpose(0, 3, 1, 2, 4),
        "w_d": i["moe_w_down"][0].reshape(N_EXP, 2, P, D).transpose(0, 2, 1, 3),
        "cprev": i["state_conv"][0].reshape(NB, 2, ST, P).transpose(3, 2, 1, 0),
    }


OUTS = {
    "o_yT": (P, KD, T),
    "o_win": (2, P, SELB * HD),
    "o_kvT": (6, P, T),
    "o_clast": (P, ST, 2, NB + 1),
    "o_hlast": (P, SN, 2, NB + 1),
}


def give_back(r):
    kv = r["o_kvT"].reshape(6, KVH, HD, T)
    hl = r["o_hlast"].reshape(2, 64, SN, 2, NB + 1).transpose(4, 2, 0, 1, 3).reshape(NB + 1, SG, 64, 2)
    cl = r["o_clast"].transpose(3, 2, 1, 0).reshape(NB + 1, 2, SG * SC)
    kv_rows = kv[:4].transpose(3, 0, 1, 2)
    y = r["o_yT"].transpose(2, 1, 0).reshape(T, D)
    win_p = kv[4:].transpose(3, 0, 1, 2)
    win_s = r["o_win"].reshape(2, NB, KVH, WINDOW, HD).transpose(1, 3, 0, 2, 4)
    return tuple(np.ascontiguousarray(a) for a in (
        y[None, :SEQ], y[SEQ:, None], kv_rows[None, None, :SEQ], kv_rows[None, SEQ:, None], win_p[None, None, :SEQ],
        win_s[None], hl[None, :1], hl[None, 1:], cl[None, :1], cl[None, 1:]))


def kernel(**inputs):
    import concourse.bacc as bacc
    from concourse.bass_utils import run_bass_kernel_spmd

    arrays = {k: np.ascontiguousarray(v) for k, v in lay_out({k: np.asarray(v) for k, v in inputs.items()}).items()}
    nc = bacc.Bacc("TRN2", target_bir_lowering=False, num_devices=1)
    io = {k: nc.dram_tensor("in_" + k, v.shape, mybir.dt.from_np(v.dtype), kind="ExternalInput").ap()
          for k, v in arrays.items()}
    io |= {k: nc.dram_tensor(k, s, F32, kind="ExternalOutput").ap() for k, s in OUTS.items()}
    io["comb"] = nc.dram_tensor("comb", (N_EXP, T), F32, kind="Internal").ap()
    build(nc, io)
    r = run_bass_kernel_spmd(nc, [{"in_" + k: v for k, v in arrays.items()}], core_ids=[0]).results[0]
    return give_back(r)
```

```python
from contextlib import ExitStack

import numpy as np
import concourse.bass as bass
from concourse import mybir
from concourse.alu_op_type import AluOpType as ALU

F32 = mybir.dt.float32
F32R = mybir.dt.float32r
I32 = mybir.dt.int32
U32 = mybir.dt.uint32
ACT = mybir.ActivationFunctionType
AX_X = mybir.AxisListType.X

P = 128
D = 1024
KD = D // P
SEQ = 512
NB = 8
T = SEQ + NB
HALF = T // 2
PAST = 4096
PAGE = 128
PAGES = PAST // PAGE
HD = 64
HEADS = 8
KVH = 2
GRP = HEADS // KVH
CB = 32
NCB = PAST // CB
SELB = 64
WINDOW = 512
SLOTS = 8
SG = 24
SC = 16
ST = SG * SC // P
SN = SG * 64 // P
N_EXP = 16
FF = 256
EPS = 1e-6
TURN = 4096
SIN_SCALE = 6.2831850
HUGE = 1e30

N_POOL = 320
N_STORED = 3
BRANCH_K = (3, 3, 4)

Z_U, Z_Q, Z_KV, Z_CB, Z_CC, Z_CX = 0, 3, 7, 13, 16, 19
NZ = 22
Z_ORDER = [*range(Z_U, Z_Q), *range(Z_KV, Z_CB), *(z + c for c in range(3) for z in (Z_CB, Z_CC, Z_CX)),
           *range(Z_Q, Z_KV)]
CHUNKS = ((0, HALF), (HALF, T))


def cody_waite(x, bits):
    parts = []
    for _ in range(2):
        m, e = np.frexp(x)
        part = float(np.ldexp(np.round(m * 2.0**bits), e - bits))
        parts.append(part)
        x = x - part
    return parts + [float(x)]


class Chain:

    def __init__(self, engine, sem):
        self.engine, self.sem, self.n = engine, sem, 0

    def __call__(self, ins, lag=0):
        self.n += 1
        ins.then_inc(self.sem, 1)
        self.engine.wait_ge(self.sem, self.n - lag)


def constants():
    p = np.arange(P)
    slope = 2.0 ** -(1.0 + np.arange(HEADS))
    by_pos = np.array([slope[m + GRP * g] for m in range(GRP) for g in range(KVH)])
    q, j = np.arange(P)[:, None], np.arange(SEQ)[None]
    dist = (q - j + SEQ - P).astype(np.float64)
    t = (np.arange(4)[None, :, None, None] * P + p[:, None, None, None])
    dc = t - (CB * np.arange(16) + CB - 1.0)
    b, g, c = p // 16, p // 8 % 2, p % 8
    factor = np.where(g == 0, 1.0, 2.0**-GRP)
    at = np.arange(SELB)
    h64 = np.arange(64)
    force = np.zeros((16, SELB))
    force[:, [0, PAST // SELB - 1]] = 1e4
    keys = np.arange(24)
    return {
        "ident": np.eye(P),
        "dist": np.where(dist >= 0, dist, HUGE),
        "bias_p": np.where(dc >= 0, -by_pos[:, None] * dc, -HUGE).reshape(P, 512),
        "valid_p": (dc >= 0).reshape(P, 64),
        "blocks": (p[:, None] // 16 == np.arange(512)[None] // HD),
        "rep_c": (np.arange(16)[:, None] == p[None] % 16),
        "bias_s": -slope[h64 % 8][:, None] * (PAST - (CB * np.arange(NCB) + CB - 1.0)),
        "sum_g": (h64[:, None] // 4 == np.arange(16)[None]),
        "force": force,
        "rep16": (np.arange(16)[:, None] == p[None] // 8),
        "rep8": (np.arange(8)[:, None] == p[None] // 16),
        "slot": (c[:, None] == np.arange(8)),
        "iota": np.tile(np.arange(PAGES), (P, 1)),
        "group": np.stack([g, g == 0, g == 1], 1),
        "npos": np.tile(-at, (P, 1)),
        "rank": np.tile([4.0, 3.0, 2.0, 1.0], (P, 1)),
        "keep": np.where(c < 7, factor, 0.0)[:, None],
        "add7": np.where((c[:, None] == 7) & (at > 0), HUGE, 0.0),
        "dist_w": factor[:, None] * (WINDOW - 1 - SELB * c[:, None] - at),
        "sel_g": (np.arange(KVH)[None, :, None] == g[:, None, None]) & (np.arange(NB) == b[:, None, None]),
        "gate_k": (keys[:, None, None] // 8 == np.arange(3)[:, None]) & (keys[:, None, None] % 4 == np.arange(GRP)),
        "gate_g": (keys[:, None] // 4 % 2 == p[None] // HD),
    }


def pack():
    at, n, rows_ = {}, 0, {}
    for name, v in constants().items():
        v = v.reshape(v.shape[0], -1).astype(np.float32)
        at[name], rows_[name] = (n, n + v.shape[1]), v
        n += v.shape[1]
    out = np.zeros((P, n), np.float32)
    for name, (a, b) in at.items():
        out[0:rows_[name].shape[0], a:b] = rows_[name]
    return at, n, out


CST, CST_N, CST_ARRAY = pack()


def build(nc, io):
    ctx = ExitStack()
    with ctx:
        mixers = ExitStack()

        def sb(name, shape, dt=F32, stack=ctx):
            return stack.enter_context(nc.sbuf_tensor(name, shape, dt))

        def sem(name):
            return ctx.enter_context(nc.semaphore(name))

        bank = [ctx.enter_context(nc.psum_tensor(f"bank{i}", [P, 512], F32)) for i in range(8)]
        H = sb("H", [P, KD, T], stack=mixers)
        Z = sb("Z", [P, NZ, T], stack=mixers)
        W_RING = sb("W_RING", [P, 2, KD, P], stack=mixers)
        CMP = sb("CMP", [P, 2, PAGES * 256], stack=mixers)
        X = CMP[:, 1, 0:KD * T].rearrange("p (k t) -> p k t", k=KD)
        WORK = sb("WORK", [P, 12, 512], stack=mixers)
        TWICE = sb("TWICE", [P, 3200], stack=mixers)
        tvec = TWICE[:, 0:SEQ]
        w_glu = TWICE[:, 512:1664].rearrange("p (k n) -> p k n", k=ST)
        BT = TWICE[:, 1664:2432].rearrange("p (c r n) -> p c r n", c=ST, r=2)
        CT = TWICE[:, 2432:3200].rearrange("p (i r n) -> p i r n", i=SN, r=2)
        VC = TWICE[:, 0:1024].rearrange("p (b n) -> p b n", b=NB)
        CB2 = TWICE[:, 1024:2064].rearrange("p (e t) -> p e t", e=2)
        QN = TWICE[0:NB, 2064:2576]
        sm = TWICE[:, 2576:3088]
        AUX = sb("AUX", [P, 4 * T], stack=mixers)
        mixers.close()
        HL = sb("HL", [P, KD, T], F32R)
        GL1 = sb("GL1", [P, 2, KD, FF], F32R)
        sb("gap_z0", [P, 8 * T - 4096])
        AL = [sb(f"AL{j}", [P, 2, T], F32R) for j in range(2)]
        sb("gap_combT", [P, T])
        GH0 = sb("GH0", [P, 2, KD, FF], F32R)
        sb("gap_z1", [P, 9 * T - 4096])
        GH1_UP = sb("GH1_UP", [P, KD, FF], F32R)
        GL0 = sb("GL0", [P, 2, KD, FF], F32R)
        WL = [sb(f"WL{j}", [P, 2, D], F32R) for j in range(2)]
        sb("gap_x", [P, KD * T])
        WH0 = sb("WH0", [P, 2, D], F32R)
        AH1 = sb("AH1", [P, 2, T], F32R)
        sb("gap_cmp", [P, 8192 - 10 * T - 2048])
        HH = sb("HH", [P, KD, T], F32R)
        sb("gap_routing", [P, 512])
        WH1_0 = sb("WH1_0", [P, D], F32R)
        sb("gap_work", [P, 6144 - 8 * T - 512 - D])
        WH1_1 = sb("WH1_1", [P, D], F32R)
        sb("gap_cb2", [P, 2 * T])
        AH0 = sb("AH0", [P, 2, T], F32R)
        sb("gap_twice", [P, 3200 - D - 4 * T])
        GH1_GATE = sb("GH1_GATE", [P, KD, FF], F32R)
        sb("gap_aux", [P, 4 * T - 2048])
        GL, AH = [GL0, GL1], [AH0, AH1]
        GH = [[GH0[:, 0], GH0[:, 1]], [GH1_GATE[:], GH1_UP[:]]]
        WH = [[WH0[:, 0], WH0[:, 1]], [WH1_0[:], WH1_1[:]]]

        def wide(x):
            return x.bitcast(F32)

        ones = sb("ones", [P, P])
        gains = sb("gains", [P, 3, KD])
        rstd = sb("rstd", [P, T])
        epsb = sb("epsb", [P, 1])
        halfpi = sb("halfpi", [P, 1])
        prm = sb("prm", [P, 3, SN])
        spar = sb("spar", [P, 24, SN])
        spi = sb("spi", [P, SN], I32)
        h0 = sb("h0", [P, SN, 2, NB])
        hlast = sb("hlast", [P, SN, 2, NB + 1])
        RIs = sb("RIs", [P, SN, 2, NB])
        stmp = sb("stmp", [P, 2, SN, NB])
        sdb = sb("sdb", [P, 2, ST])
        cw = sb("cw", [P, ST, 3])
        cprev = sb("cprev", [P, ST, 2, NB])
        clast = sb("clast", [P, ST, 2, NB + 1])
        wgt = sb("wgt", [P, KD, 24])
        Gt = sb("Gt", [24, T])

        cst = sb("cst", [P, CST_N])
        w1 = AUX[:, 0:2048].rearrange("p (v r h) -> p v r h", v=2, r=16)
        w2 = sb("w2", [P, 2, HD])
        pe_t = sb("pe_t", [P, 2, 16])
        cbias = sb("cbias", [P, 1])
        vcp = sb("vcp", [16, P])
        Gn = sb("Gn", [P, 4, 24])
        nmax = sb("nmax", [P, 64])
        lsum = sb("lsum", [P, 64])
        cmax = sb("cmax", [P, 32])
        csum = sb("csum", [P, 32])
        wts = sb("wts", [P, 3, HEADS])
        ptab = sb("ptab", [1, NB * PAGES], I32)
        pt8 = sb("pt8", [NB, PAGES], I32)
        pt8f = sb("pt8f", [NB, PAGES])
        smi = sb("smi", [16, SLOTS], U32)
        rowi = sb("rowi", [P, 4], I32)
        small = sb("small", [P, 256])
        stat = sb("stat", [P, 2, 2 * GRP])
        stW = sb("stW", [2 * GRP, 3, 16])
        wn = sb("wn", [P, 2 * GRP])
        gmask = sb("gmask", [24, 12, NB])
        gbc = sb("gbc", [P, 3, GRP, NB])
        ya = sb("ya", [P, 3, GRP, NB])
        rw = sb("rw", [P, KD, 20])
        rb = sb("rb", [20, 1])

        WF = WORK[:, :, :].rearrange("p a b -> p (a b)")
        ZF = Z[:, :, :].rearrange("p a b -> p (a b)")

        def cc(name, rows=P):
            a, b = CST[name]
            return cst[0:rows, a:b]

        identity = cc("ident")
        KCT = ZF[:, 20 * T:20 * T + 1024].rearrange("p (b n) -> p b n", b=NB)
        tmpx = CMP[:, 1, 0:1024].rearrange("p (k s n) -> p k s n", k=2, s=2)
        XP = CMP[:, 1, 1024:2048].rearrange("p (k g r b) -> p k g r b", k=2, g=2, r=16)
        VN = WF[:, 0:1024].rearrange("p (b k n) -> p b k n", b=2, k=4)
        Sb = [WF[:, 1024 + 512 * j:1536 + 512 * j] for j in range(2)]
        Ex = [WF[:, 2048 + 512 * j:2560 + 512 * j] for j in range(2)]
        PT = [WF[:, 3072 + 512 * j:3584 + 512 * j] for j in range(2)]
        SCc, PTC, VB, YN = (WF[:, 4096 + 512 * j:4608 + 512 * j] for j in range(4))
        M = WF[:, 0:KD * T].rearrange("p (n t) -> p n t", n=KD)
        KW, VW = (CMP[:, 0, 4096 * j:4096 * (j + 1)] for j in range(2))
        KG, VG = (CMP[:, 1, 4096 * j:4096 * (j + 1)] for j in range(2))
        KVT = [[KG, VG], [KW, VW]]
        LATE = WF[:, KD * T:]
        QR = LATE[:, 0:256].rearrange("p (m d) -> p m d", m=GRP)
        SE = LATE[:, 256:768].rearrange("p (b m n) -> p b m n", b=2, m=GRP)
        O2 = LATE[:, 768:1280].rearrange("p (b m d) -> p b m d", b=2, m=GRP)
        KN = LATE[0:NB, 1280:1792].rearrange("p (s n) -> p s n", s=4)
        rt = LATE[0:104, 0:240].rearrange("p (a j k) -> p a j k", a=12, j=5)
        comb = LATE[0:104, 240:320].rearrange("p (j e) -> p j e", j=5)
        lg = LATE[0:104, 320:420].rearrange("p (j e) -> p j e", j=5)
        stT = TWICE[0:2 * GRP, 1024:1280].rearrange("p (a n) -> p a n", a=2)
        cu = rstd[:]
        KB = W_RING[:, 1, :, :].rearrange("p k n -> p (k n)")[:, 0:640]
        SCT = W_RING[:, 0, 4:8, :].rearrange("p k n -> p (k n)")
        HID = W_RING[:, 0, 0:4, :].rearrange("p (b k) n -> p b (k n)", b=2)
        combT = ZF[0:N_EXP, 12 * T:13 * T]
        lgT = ZF[0:20, 12 * T:13 * T]
        WB = ZF[:, 20 * T:20 * T + 1024].rearrange("p (s k n) -> p s k n", s=2, k=4)
        SG = AUX[:, 0:2 * T].rearrange("p (s t) -> p s t", s=2)
        BB = AUX[:, 2 * T:4 * T].rearrange("p (s t) -> p s t", s=2)
        GU = [r.rearrange("p (w k f) -> p w k f", w=2, k=KD) for r in (CMP[:, 0, 0:4096], ZF[:, 0:4096])]
        WD = [CMP[:, 0, 4096 + 2048 * j:6144 + 2048 * j].rearrange("p (f n) -> p f n", f=2) for j in range(2)]
        A = [ZF[:, (8 + 2 * j) * T:(10 + 2 * j) * T].rearrange("p (f t) -> p f t", f=2) for j in range(2)]
        PROD = ZF[:, 3 * T:3 * T + 4096]
        page = [CMP[:, b, :].rearrange("p (g v h r c) -> p g v h r c", g=PAGES, v=2, h=2, r=16) for b in range(2)]

        x_in = [sem(f"x_in{j}") for j in range(KD // 2)]
        small_in = sem("small_in")
        wg_in = sem("wg_in")
        w_in = [sem("w_in0"), sem("w_in1")]
        consts_done = sem("consts_done")
        dve_const = sem("dve_const")
        sq_ready = sem("sq_ready")
        ms_ready = sem("ms_ready")
        rms_ready = sem("rms_ready")
        norm_ready = sem("norm_ready")
        z_done = sem("z_done")
        z_ready = sem("z_ready")
        dve_step = sem("dve_step")
        pool_step = sem("pool_step")
        ang_ready = sem("ang_ready")
        trig_ready = sem("trig_ready")
        bu_ready = sem("bu_ready")
        v_done = sem("v_done")
        ris_ready = sem("ris_ready")
        h_ready = sem("h_ready")
        y_done = sem("y_done")
        skip_ready = sem("skip_ready")
        gelu_ready = sem("gelu_ready")
        hs_ready = sem("hs_ready")
        ys_done = sem("ys_done")
        glu_done = sem("glu_done")
        glu_sig = sem("glu_sig")
        yssm_ready = sem("yssm_ready")
        yconv_ready = sem("yconv_ready")
        stored = sem("stored")
        cst_in = sem("cst_in")
        tmpx_ready = sem("tmpx_ready")
        xp_in = sem("xp_in")
        ptab_in = sem("ptab_in")
        pages_in = [sem("pages_in0"), sem("pages_in1")]
        odd_pages_in = [sem("odd_pages_in0"), sem("odd_pages_in1")]
        kb_zeroed, sct_done, sct_ready = sem("kb_zeroed"), sem("sct_done"), sem("sct_ready")
        cb_done, cb_ready = sem("cb_done"), sem("cb_ready")
        hid_done, hid_ready = sem("hid_done"), sem("hid_ready")
        kc_done, kc_ready = sem("kc_done"), sem("kc_ready")
        vb_rep, vb_ready = sem("vb_rep"), sem("vb_ready")
        vt_done, vt_ready = sem("vt_done"), sem("vt_ready")
        gt_done, gt_ready = sem("gt_done"), sem("gt_ready")
        sc_done, sc_ready, ec_ready, ecm_ready = sem("sc_done"), sem("sc_ready"), sem("ec_ready"), sem("ecm_ready")
        ptc_done, ptc_ready, oc_done = sem("ptc_done"), sem("ptc_ready"), sem("oc_done")
        s_done, sb_ready, e_ready, t_done, pt_ready, pv_done = (
            sem(n) for n in ("s_done", "sb_ready", "e_ready", "t_done", "pt_ready", "pv_done"))
        qn_done, qn_ready, qr_done, qr_ready = (sem(n) for n in ("qn_done", "qn_ready", "qr_done", "qr_ready"))
        kn_done = sem("kn_done")
        gm_ready, gb_done = sem("gm_ready"), sem("gb_done")
        qs_done, qs_copied, st_done = sem("qs_done"), sem("qs_copied"), sem("st_done")
        ss_ready, es_ready, p_ready = sem("ss_ready"), sem("es_ready"), sem("p_ready")
        imp_done, pts_ready, ocs_done, idx_ready, idx_done = (
            sem(n) for n in ("imp_done", "pts_ready", "ocs_done", "idx_ready", "idx_done"))
        row_ready, kg_in, kw_in, kn_in, kn_in_w = (
            sem(n) for n in ("row_ready", "kg_in", "kw_in", "kn_in", "kn_in_w"))
        se_ready, ex_ready, o2_ready = sem("se_ready"), sem("ex_ready"), sem("o2_ready")
        stt_done, w8_ready, ew_ready, wn_ready, wn_done, o2_scaled, ot_done, ya_ready = (
            sem(n) for n in ("stt_done", "w8_ready", "ew_ready", "wn_ready", "wn_done", "o2_scaled", "ot_done",
                             "ya_ready"))
        wb_in = [sem("wb_in0"), sem("wb_in1")]
        mz_done, mz_ready, mb_done, mb_ready, mm_ready = (
            sem(n) for n in ("mz_done", "mz_ready", "mb_done", "mb_ready", "mm_ready"))
        x_again, mo_done, mo_ready, win_stored = sem("x_again"), sem("mo_done"), sem("mo_ready"), sem("win_stored")
        lt_done, lt_ready = sem("lt_done"), sem("lt_ready")
        lg_done, rx_ready, re_ready, comb_ready, ct_done, ct_ready, comb_stored = (
            sem(n) for n in ("lg_done", "rx_ready", "re_ready", "comb_ready", "ct_done", "ct_ready", "comb_stored"))
        gu_in, wd_in, cb_in = ([sem(f"{n}{j}") for j in range(2)] for n in ("gu_in", "wd_in", "cb_in"))
        gu_done, silu_ready, up_ready, a_ready, dn_done, dn_ready = (
            sem(n) for n in ("gu_done", "silu_ready", "up_ready", "a_ready", "dn_done", "dn_ready"))
        hh_ready, hl_ready, gh_ready, gl_ready, wh_ready, wl_ready, ah_ready, al_ready = (
            sem(n) for n in ("hh_ready", "hl_ready", "gh_ready", "gl_ready", "wh_ready", "wl_ready", "ah_ready",
                             "al_ready"))
        y_out = sem("y_out")
        y_nat, yt_done, yt_ready = sem("y_nat"), sem("yt_done"), sem("yt_ready")

        ki, kf, uu, au = (WORK[:, i, :] for i in range(4))
        sn, cs = (WORK[:, 4, :], WORK[:, 5, :]), (WORK[:, 6, :], WORK[:, 7, :])
        pw, qw = WORK[:, 8, :], WORK[:, 9, :]
        hr, hi = WORK[:, 10, :], WORK[:, 11, :]
        pR, pI, qR, qI, vr, vi, gr, gi, cgr, cgi, sgr, sgi = (
            CMP[:, 1, 2048 + 512 * j:2560 + 512 * j] for j in range(12))
        kint = ki.bitcast(I32)
        glu_g = WORK[:, :, :].rearrange("p a b -> p (a b)")[:, 2048:2048 + ST * T].rearrange("p (k t) -> p k t", k=ST)
        (A_RE, A_IM, LDT) = range(3)
        (DT, MAG, TH, MF, TQ, MH, RR, UQ, AQ, SI, CO, ABR, ABI, AM1, DEN, RDEN, CR, CI,
         T1, T2) = range(20)

        def par(k, i=None):
            return spar[:, k, :] if i is None else spar[:, k, i:i + 1]

        beside = [[t for t in (3 + 2 * i, 4 + 2 * i) if t < NZ] for i in range(SN)]

        N_UNITS = 64

        def unit(n):
            return n // 16, n // 8 % 2, n % 8, (n // 16 + 1) * P

        block = ctx.enter_context(nc.Block())

        def load_pages(engine, s, b, first, groups, arrived, later):
            with engine.Fori(0, groups) as i:
                at = [engine.value_load(ptab[0:1, bass.ds(s * PAGES + first + 8 * i + 2 * j, 1)], min_val=0,
                                        max_val=N_POOL - 1) for j in range(4)]
                if later:
                    engine.wait_ge(hid_done, s)
                for j in range(4):
                    engine.dma_start(CMP[:, b, bass.ds((first + 8 * i + 2 * j) * 256, 256)],
                                     io["cmp"][bass.ds(at[j], 1)].rearrange("o p n -> p (o n)")).then_inc(arrived, 16)

        @block.sync
        def _(sp):
            for k in range(0, KD, 2):
                sp.dma_start(X[:, k:k + 2, :], io["xT"][:, k:k + 2, :]).then_inc(x_in[k // 2], 16)
            sp.dma_start(gains[:], io["gains"]).then_inc(small_in, 16)
            sp.dma_start(prm[:], io["prm"]).then_inc(small_in, 16)
            sp.dma_start(BT, io["BT"]).then_inc(small_in, 16)
            sp.dma_start(CT, io["CT"]).then_inc(small_in, 16)
            sp.dma_start(ptab[:], io["ptab"]).then_inc(ptab_in, 16)
            sp.wait_ge(ptab_in, 16)

            for t in range(NZ):
                if t >= 2:
                    sp.wait_ge(z_done, t - 1)
                sp.dma_start(W_RING[:, t % 2], io["w_z"][t]).then_inc(w_in[t % 2], 16)
                if t in (3, 5, 7, 9):
                    load_pages(sp, 0, 0, 4 * (t - 3), 1, pages_in[0], False)
                if t == 1:
                    sp.dma_start(h0[:], io["h0"]).then_inc(small_in, 16)
                    sp.dma_start(sdb[:], io["sdb"]).then_inc(small_in, 16)
                    sp.dma_start(w_glu, io["w_glu"]).then_inc(small_in, 16)
                    sp.dma_start(cw[:], io["cw"]).then_inc(small_in, 16)
                    sp.dma_start(cprev[:], io["cprev"]).then_inc(small_in, 16)
                    sp.dma_start(wgt[:], io["w_gates"]).then_inc(wg_in, 16)
                    sp.dma_start(cst[:], io["cst"]).then_inc(cst_in, 16)
                    sp.dma_start(w1, io["w1"]).then_inc(cst_in, 16)
                    sp.dma_start(w2[:], io["w2"]).then_inc(cst_in, 16)
                    sp.dma_start(pe_t[:], io["pe"]).then_inc(cst_in, 16)
                    sp.dma_start(pt8[:], io["pt8"]).then_inc(cst_in, 16)
            sp.wait_ge(hs_ready, 1)
            load_pages(sp, 1, 1, 0, PAGES // 8, pages_in[1], True)
            with sp.Fori(1, 4) as i:
                for b in range(2):
                    load_pages(sp, 2 * i + b, b, 0, PAGES // 8, pages_in[b], True)
            sp.wait_ge(hid_done, NB)
            for v, dst in enumerate((KW, VW)):
                src = io["win"][v]
                sp.dma_start(dst[0:P - 1, :], src[HD:HD + (P - 1) * 4096].rearrange("(p n) -> p n", p=P - 1))\
                    .then_inc(kw_in, 16)
                sp.dma_start(dst[P - 1:P, 0:63 * HD], src[HD + (P - 1) * 4096:].rearrange("(p n) -> p n", p=1))\
                    .then_inc(kw_in, 16)

            def new_row(sem_, dst, s, pos):
                for g in range(KVH):
                    sp.dma_start(dst[SLOTS * g + SLOTS - 1::16, pos * HD:pos * HD + HD],
                                 KN[:, s, g * HD:g * HD + HD]).then_inc(sem_, 16)

            sp.wait_ge(kc_done, NB + 1)
            for b in range(2):
                sp.dma_start(W_RING[:, b], io["w_m"][b]).then_inc(w_in[b], 16)
            sp.wait_ge(qr_ready, 1)
            sp.wait_ge(kw_in, 64)
            new_row(kn_in_w, KW, 2, SELB - 1)
            new_row(kn_in_w, VW, 3, SELB - 1)
            def merge_loads(br, first):
                nk = BRANCH_K[br]
                with sp.Fori(first, 4) as i:
                    for b in range(2):
                        q = 8 * br + 2 * i + b
                        if br or first:
                            sp.wait_ge(mz_done, q - 1)
                            sp.wait_ge(mb_done, q - 1)
                        sp.dma_start(W_RING[:, b], io["w_m"][bass.ds(q, 1)].rearrange("o p k n -> p (o k) n"))\
                            .then_inc(w_in[b], 16)
                        sp.dma_start(WB[:, b, 0:nk], io[f"w_b{br}"][bass.ds(2 * i + b, 1)]
                                     .rearrange("o p k n -> p (o k) n")).then_inc(wb_in[b], 16)

            sp.wait_ge(qs_done, 1)
            for b in range(2):
                sp.dma_start(WB[:, b, 0:BRANCH_K[0]], io["w_b0"][b]).then_inc(wb_in[b], 16)
            merge_loads(0, 1)
            sp.wait_ge(kg_in, 32)
            new_row(kn_in, KG, 0, 0)
            new_row(kn_in, VG, 1, 0)
            merge_loads(1, 0)
            sp.wait_ge(kn_in_w, 64)
            for v, src in enumerate((KW, VW)):
                sp.dma_start(io["o_win"][v], src).then_inc(win_stored, 16)
            merge_loads(2, 0)
            sp.dma_start(rw[:], io["w_r"]).then_inc(x_again, 16)
            sp.dma_start(rb[:], io["b_r"]).then_inc(x_again, 16)
            sp.wait_ge(o2_ready, 2)
            sp.wait_ge(win_stored, 32)
            sp.dma_start(X, io["xT"]).then_inc(x_again, 16)
            sp.dma_start(GU[0], io["w_gu"][0]).then_inc(gu_in[0], 16)
            sp.dma_start(WD[0], io["w_d"][0]).then_inc(wd_in[0], 16)
            for b in range(2):
                sp.wait_ge(mz_done, 23 + b)
                sp.dma_start(W_RING[:, b], io["w_o"][b]).then_inc(w_in[b], 16)
            with sp.Fori(1, 4) as i:
                for b in range(2):
                    sp.wait_ge(mo_done, 2 * i + b - 1)
                    sp.dma_start(W_RING[:, b], io["w_o"][bass.ds(2 * i + b, 1)].rearrange("o p k n -> p (o k) n"))\
                        .then_inc(w_in[b], 16)
            sp.wait_ge(mm_ready, 26)
            sp.dma_start(GU[1], io["w_gu"][1]).then_inc(gu_in[1], 16)
            sp.dma_start(WD[1], io["w_d"][1]).then_inc(wd_in[1], 16)
            sp.wait_ge(ct_ready, 2)
            sp.dma_start(io["comb"], combT).then_inc(comb_stored, 16)
            sp.wait_ge(comb_stored, 16)

            def comb_load(b, e):
                sp.dma_start(CB2[:, b, :], io["comb"][bass.ds(e, 1), :].to_broadcast([P, T])).then_inc(cb_in[b], 16)

            comb_load(0, 0)
            comb_load(1, 1)
            with sp.Fori(1, N_EXP // 2) as i:
                for b in range(2):
                    e = 2 * i + b
                    sp.wait_ge(gu_done, 2 * e - 2)
                    sp.dma_start(GU[b], io["w_gu"][bass.ds(e, 1)].rearrange("o p w k f -> p (o w) k f"))\
                        .then_inc(gu_in[b], 16)
                    sp.wait_ge(a_ready, 2 * e - 2)
                    comb_load(b, e)
                    sp.wait_ge(dn_done, 8 * e - 8)
                    sp.dma_start(WD[b], io["w_d"][bass.ds(e, 1)].rearrange("o p f n -> p (o f) n"))\
                        .then_inc(wd_in[b], 16)
            for k in range(0, KD, 2):
                sp.wait_ge(norm_ready, 2 * KD + k + 2)
                sp.dma_start(io["o_yT"][:, k:k + 2, :], H[:, k:k + 2, :]).then_inc(y_out, 16)
            sp.wait_ge(y_out, KD // 2 * 16)
            sp.wait_ge(stored, N_STORED * 16)

        @block.gpsimd
        def _(pool):
            step = Chain(pool, pool_step)
            pool.memset(halfpi[:], float(np.pi / 2)).then_inc(consts_done, 1)
            pool.memset(epsb[:], EPS).then_inc(consts_done, 1)
            pool.iota(tvec, [[1, SEQ]], base=0, channel_multiplier=0,
                      allow_small_or_imprecise_dtypes=True).then_inc(consts_done, 1)

            pool.wait_ge(ptab_in, 16)
            load_pages(pool, 0, 0, 1, PAGES // 8, odd_pages_in[0], False)
            pool.wait_ge(z_ready, Z_ORDER.index(Z_KV + 1) + 1)
            for v in range(2):
                pool.tensor_copy(tmpx[:, v].rearrange("p s (r b) -> p s r b", r=16),
                                 Z[:, Z_KV + v, 0:SEQ].rearrange("p (b r s) -> p s r b", r=16, s=2))\
                    .then_inc(tmpx_ready, 1)
            pool.wait_ge(tmpx_ready, 2)
            for v in range(2):
                for g in range(KVH):
                    for par_ in range(2):
                        pool.dma_start(XP[par_ * HD:par_ * HD + HD, v, g].rearrange("p r b -> p (r b)"),
                                       tmpx[g * HD:g * HD + HD, v, par_]).then_inc(xp_in, 16)
            pool.wait_ge(small_in, 9 * 16)
            for c in range(ST):
                pool.wait_ge(z_ready, Z_ORDER.index(Z_CX + c) + 1)
                y, gb, tmp = Z[:, Z_CC + c, :], Z[:, Z_CB + c, :], Z[:, Z_CX + c, :]
                step(pool.tensor_tensor(cu, Z[:, Z_CC + c, :], Z[:, Z_CX + c, :], ALU.mult))
                step(pool.tensor_copy(clast[:, c, :, 0], cu[:, SEQ - 2:SEQ]))
                step(pool.tensor_copy(clast[:, c, 0, 1:], cprev[:, c, 1, :]))
                step(pool.tensor_copy(clast[:, c, 1, 1:], cu[:, SEQ:T]))
                step(pool.tensor_scalar(y, cu, cw[:, c, 2:3], None, ALU.mult))
                for j, lag in ((1, 1), (0, 2)):
                    w = cw[:, c, j:j + 1]
                    step(pool.tensor_scalar(tmp[:, lag:SEQ], cu[:, 0:SEQ - lag], w, None, ALU.mult))
                    step(pool.tensor_scalar(tmp[:, SEQ:T], cprev[:, c, j, :], w, None, ALU.mult))
                    step(pool.tensor_tensor(y[:, lag:T], y[:, lag:T], tmp[:, lag:T], ALU.add))
                step(pool.tensor_tensor(gb, gb, y, ALU.mult))
            pool.sem_inc(yconv_ready, 1)
            pool.wait_ge(z_done, NZ)
            pool.memset(KB, 0.0).then_inc(kb_zeroed, 1)
            pool.dma_start(io["o_kvT"].rearrange("s p t -> p s t"), Z[:, Z_KV:Z_KV + 6, :]).then_inc(stored, 16)
            pool.dma_start(io["o_clast"], clast[:]).then_inc(stored, 16)
            pool.wait_ge(hs_ready, 1)
            load_pages(pool, 1, 1, 1, PAGES // 8, odd_pages_in[1], True)
            pool.dma_start(io["o_hlast"], hlast[:]).then_inc(stored, 16)

            with pool.Fori(1, 4) as i:
                for b in range(2):
                    load_pages(pool, 2 * i + b, b, 1, PAGES // 8, odd_pages_in[b], True)
            pool.sem_inc(mm_ready, 2)
            pool.wait_ge(y_nat, 4)
            pool.wait_ge(pv_done, N_UNITS)

            def merge(br, first, last):
                with pool.Fori(first, last) as i:
                    for b in range(2):
                        q = 8 * br + 2 * i + b
                        pool.wait_ge(mb_ready, q + 2)
                        out = M[:, bass.ds(2 * i + b, 1), :].rearrange("p o t -> p (o t)")
                        if br == 0:
                            pool.tensor_tensor(out, SG[:, b], BB[:, b], ALU.mult).then_inc(mm_ready, 1)
                        else:
                            pool.tensor_tensor(SG[:, b], SG[:, b], BB[:, b], ALU.mult).then_inc(pool_step, 1)
                            pool.wait_ge(pool_step, step.n + 8 * (br - 1) + 2 * i + b + 1)
                            pool.tensor_tensor(out, out, SG[:, b], ALU.add).then_inc(mm_ready, 1)

            merge(0, 0, 2)
            pool.wait_ge(row_ready, 1)
            pool.wait_ge(hid_done, NB + 1)
            for dst, src in ((KG, "kslc"), (VG, "vslc")):
                pool.indirect_dma_start(out=dst, out_offset=None, in_=io[src],
                                        in_offset=bass.IndirectOffsetOnAxis(ap=rowi[:, 0:1], axis=0))\
                    .then_inc(kg_in, 16)
            merge(0, 2, 4)
            merge(1, 0, 4)
            merge(2, 0, 4)
            pool.wait_ge(lt_done, 1)
            for k in range(KD):
                pool.wait_ge(hh_ready, k + 1)
                pool.tensor_tensor(HL[:, k, :], H[:, k, :], wide(HH[:, k, :]), ALU.subtract).then_inc(hl_ready, 1)
            with pool.Fori(0, N_EXP // 2) as i:
                for b in range(2):
                    e = 2 * i + b
                    pool.wait_ge(cb_in[b], 16 * (i + 1))
                    for f in range(2):
                        pool.wait_ge(up_ready, 2 * e + f + 1)
                        pool.tensor_tensor(A[b][:, f, :], A[b][:, f, :], CB2[:, b, :], ALU.mult).then_inc(a_ready, 1)
                    for f in range(2):
                        pool.wait_ge(wh_ready, 2 * e + f + 1)
                        pool.tensor_tensor(WL[b][:, f, :], WD[b][:, f, :], wide(WH[b][f]), ALU.subtract)\
                            .then_inc(wl_ready, 1)
                    for f in range(2):
                        pool.wait_ge(ah_ready, 2 * e + f + 1)
                        pool.tensor_tensor(AL[b][:, f, :], A[b][:, f, :], wide(AH[b][:, f, :]), ALU.subtract)\
                            .then_inc(al_ready, 1)

        def rms_scalar(act, n, src, wait=None):
            for k in range(KD):
                if wait:
                    wait(k)
                act.activation(H[:, k, :], src(k), ACT.Square).then_inc(sq_ready, 1)
            act.wait_ge(ms_ready, n + 1)
            for c, (a, b) in enumerate(CHUNKS):
                act.activation(rstd[:, a:b], bank[c + (4 if n else 0)][:, 0:HALF], ACT.Sqrt, bias=epsb[:],
                               scale=1.0 / D).then_inc(rms_ready, 1)

        def rms_tensor(pe, n):
            for k in range(KD):
                pe.wait_ge(sq_ready, KD * n + k + 1)
                for c, (a, b) in enumerate(CHUNKS):
                    mm = pe.matmul(bank[c + (4 if n else 0)][:, 0:HALF], ones[:], H[:, k, a:b], start=(k == 0),
                                   stop=(k == KD - 1))
            mm.then_inc(ms_ready, 1)

        def rms_vector(dve, step, n, src, dst):
            dve.wait_ge(rms_ready, 2 * (n + 1))
            step(dve.reciprocal(rstd[:], rstd[:]))
            for k in range(KD):
                dve.scalar_tensor_tensor(dst(k), src(k), gains[:, n, k:k + 1], rstd[:], ALU.mult,
                                         ALU.mult).then_inc(norm_ready, 1)

        @block.scalar
        def _(act):
            act.wait_ge(consts_done, 3)
            rms_scalar(act, 0, lambda k: X[:, k, :], lambda k: act.wait_ge(x_in[k // 2], 16))

            def z_copy(t):
                act.wait_ge(z_done, t + 1)
                at = Z_ORDER[t]
                for c, (a, b) in enumerate(CHUNKS):
                    mm = act.activation(Z[:, at, a:b], bank[2 * (t % 2) + c][:, 0:HALF], ACT.Copy,
                                        scale=HD**-0.5 if Z_Q <= at < Z_KV else 1.0)
                mm.then_inc(z_ready, 1)

            def sincos(u, a, s, c, n):
                act.wait_ge(ang_ready, n)
                act.activation(s, u, ACT.Sin, scale=SIN_SCALE).then_inc(trig_ready, 1)
                act.activation(c, a, ACT.Sin, scale=-SIN_SCALE, bias=halfpi[:]).then_inc(trig_ready, 1)

            act.wait_ge(small_in, 9 * 16)
            act.activation(par(DT), prm[:, LDT, :], ACT.Exp).then_inc(trig_ready, 1)
            act.wait_ge(ang_ready, 1)
            act.activation(par(MAG), par(T1), ACT.Exp).then_inc(trig_ready, 1)
            sincos(par(UQ), par(AQ), par(SI), par(CO), 2)
            sincos(uu, au, sn[0], cs[0], 3)
            for t in range(3):
                z_copy(t)
            for i in range(SN):
                act.wait_ge(bu_ready, i + 1)
                act.activation(RIs[:, i], bank[7][:, 0:2 * NB].rearrange("p (r b) -> p r b", r=2),
                               ACT.Copy).then_inc(ris_ready, 1)
                if i + 1 < SN:
                    sincos(uu, au, sn[(i + 1) % 2], cs[(i + 1) % 2], 4 + i)
                for t in beside[i]:
                    z_copy(t)
                if i == 9:
                    act.wait_ge(z_done, NZ + 1)
                    for c, (a, b) in enumerate(CHUNKS):
                        mm = act.activation(Gt[:, a:b], bank[c][0:24, 0:HALF], ACT.Sigmoid)
                    mm.then_inc(z_ready, 1)
                if i == SN - 2:
                    act.wait_ge(cb_done, 1)
                    act.activation(cbias[:], bank[3][:, 0:1], ACT.Copy).then_inc(cb_ready, 1)
                    act.wait_ge(cb_ready, 1)
                    act.wait_ge(hid_done, 1)
                    act.activation(HID[:, 0, 0:32], bank[0][:, 0:32], ACT.Gelu_apprx_tanh,
                                   bias=cbias[:]).then_inc(hid_ready, 1)
                    act.wait_ge(kc_done, 1)
                    act.wait_ge(kb_zeroed, 1)
                    for g in range(KVH):
                        r = slice(g * HD, g * HD + HD)
                        mm = act.activation(KB[r].rearrange("p (m x) -> p m x", x=160)[:, :, 16 * g:16 * g + 16],
                                            bank[2][r, 0:16].unsqueeze(1).broadcast_to([HD, GRP, 16]), ACT.Copy)
                    mm.then_inc(kc_ready, 1)
                    act.activation(vcp[:], bank[3][0:16, 0:P], ACT.Copy).then_inc(kc_ready, 1)
                    act.wait_ge(sct_done, 1)
                    act.activation(SCT, bank[0][:, :], ACT.Copy).then_inc(sct_ready, 1)
                if i % 4 == 3:
                    c = i // 4
                    act.wait_ge(skip_ready, c + 1)
                    act.activation(Z[:, c, 0:SEQ], Z[:, c, 0:SEQ], ACT.Gelu_apprx_tanh).then_inc(gelu_ready, 1)
            act.wait_ge(skip_ready, ST + 1)
            act.activation(Z[:, 0:ST, SEQ:T], Z[:, 0:ST, SEQ:T], ACT.Gelu_apprx_tanh).then_inc(gelu_ready, 1)
            for b in range(2):
                act.wait_ge(vt_done, b + 1)
                act.activation(VN[:, b].rearrange("p k n -> p (k n)"), bank[4 + b][:, :], ACT.Copy).then_inc(vt_ready, 1)
            act.wait_ge(gt_done, 1)
            act.activation(Gn[:].rearrange("p q n -> p (q n)"), bank[7][:, 0:96], ACT.Copy).then_inc(gt_ready, 1)
            act.wait_ge(sc_ready, 1)
            act.activation(SCc, SCc, ACT.Exp).then_inc(ec_ready, 1)
            for n in range(ST):
                act.wait_ge(glu_done, n + 1)
                for c, (a, b) in enumerate(CHUNKS):
                    mm = act.activation(glu_g[:, n, a:b], bank[2 + 2 * (n % 2) + c][:, 0:HALF], ACT.Sigmoid,
                                        bias=sdb[:, 1, n:n + 1])
                mm.then_inc(glu_sig, 1)

            act.wait_ge(ptc_done, 1)
            act.activation(PTC, bank[7][:, :], ACT.Copy).then_inc(ptc_ready, 1)

            def pt_copy(n):
                L = unit(n)[3]
                act.wait_ge(t_done, n + 1)
                if n >= 2:
                    act.wait_ge(pv_done, n - 1)
                act.activation(PT[n % 2][:, 0:L], bank[2 + n % 2][:, 0:L], ACT.Copy).then_inc(pt_ready, 1)

            def yt_copy(qt):
                act.wait_ge(yt_done, qt + 1)
                act.activation(Z[:, Z_CC:Z_CC + GRP, qt * P:(qt + 1) * P],
                               bank[7][:, :].rearrange("p (m q) -> p m q", m=GRP), ACT.Copy).then_inc(yt_ready, 1)

            def hid_gelu(smp):
                act.wait_ge(hid_done, smp + 2)
                act.wait_ge(kc_done, smp + 1)
                act.activation(HID[:, smp % 2, :], bank[6 + smp % 2][:, 0:2 * NCB], ACT.Gelu_apprx_tanh,
                               bias=cbias[:]).then_inc(hid_ready, 1)

            def kc_copy(smp):
                act.wait_ge(kc_done, smp + 2)
                out = bank[6 + smp % 2]
                act.activation(KCT[:, smp, :], out[:, 2 * NCB:3 * NCB], ACT.Copy).then_inc(kc_ready, 1)
                act.activation(VC[:, smp, :], out[:, 3 * NCB:4 * NCB], ACT.Copy).then_inc(kc_ready, 1)

            for n in range(N_UNITS):
                qt, br, pos, L = unit(n)
                at = n % 16
                act.wait_ge(sb_ready, n + 1)
                if n >= 2:
                    act.wait_ge(t_done, n - 1)
                act.activation(Ex[n % 2][:, 0:L], Sb[n % 2][:, 0:L], ACT.Exp, bias=nmax[:, n:n + 1],
                               accum_out=lsum[:, n:n + 1]).then_inc(e_ready, 1)
                if n >= 1:
                    pt_copy(n - 1)
                if at == 2 and qt:
                    hid_gelu(2 * qt - 1)
                if at == 3 and qt:
                    kc_copy(2 * qt - 1)
                if at == 5 and qt:
                    yt_copy(qt - 1)
                if at == 9:
                    hid_gelu(2 * qt)
                if at == 10:
                    kc_copy(2 * qt)
            pt_copy(N_UNITS - 1)
            hid_gelu(NB - 1)
            kc_copy(NB - 1)
            yt_copy(3)
            act.sem_inc(mz_ready, 1)
            act.sem_inc(mb_ready, 1)
            act.wait_ge(ss_ready, 1)
            act.activation(sm[0:64, 64:192], sm[0:64, 64:192], ACT.Exp, bias=small[0:64, 0:1],
                           accum_out=small[0:64, 1:2]).then_inc(es_ready, 1)


            def merge_copies(br, first=0, last=4):
                with act.Fori(first, last) as i:
                    for b in range(2):
                        q = 8 * br + 2 * i + b
                        act.wait_ge(mz_done, q + 1)
                        act.wait_ge(mm_ready, q + 1)
                        for c, (lo, hi_) in enumerate(CHUNKS):
                            mm = act.activation(SG[:, b, lo:hi_], bank[c][:, 0:HALF], ACT.Sigmoid)
                        mm.then_inc(mz_ready, 1)
                        act.wait_ge(mb_done, q + 1)
                        for c, (lo, hi_) in enumerate(CHUNKS):
                            mm = act.activation(BB[:, b, lo:hi_], bank[2 + c][:, 0:HALF], ACT.Copy)
                        mm.then_inc(mb_ready, 1)

            def chunk_exp(n):
                act.wait_ge(se_ready, n + 1)
                act.activation(SE[:, 1 - n].rearrange("p m n -> p (m n)"), SE[:, 1 - n].rearrange("p m n -> p (m n)"),
                               ACT.Exp).then_inc(ex_ready, 1)

            merge_copies(0, 0, 2)
            chunk_exp(0)
            merge_copies(0, 2, 4)
            merge_copies(1, 0, 2)
            chunk_exp(1)
            merge_copies(1, 2, 4)
            act.wait_ge(w8_ready, 1)
            act.activation(stT[:, 0, :], stT[:, 0, :], ACT.Exp).then_inc(ew_ready, 1)
            merge_copies(2)

            def gu_high(b, uses):
                act.wait_ge(gu_in[b], 16 * uses)
                for w in range(2):
                    act.activation(GH[b][w], GU[b][:, w], ACT.Copy).then_inc(gh_ready, 1)

            act.wait_ge(mm_ready, 26)
            gu_high(0, 1)
            act.wait_ge(mz_done, 24)
            rms_scalar(act, 1, lambda k: X[:, k, :], lambda k: act.wait_ge(mo_ready, k + 3))
            for k in range(KD):
                act.wait_ge(norm_ready, KD + k + 1)
                act.activation(HH[:, k, :], H[:, k, :], ACT.Copy).then_inc(hh_ready, 1)
            gu_high(1, 1)
            act.wait_ge(rx_ready, 1)
            act.activation(rt[:, 0], rt[:, 0], ACT.Exp).then_inc(re_ready, 1)
            act.wait_ge(rx_ready, 2)
            act.activation(rt[:, 1], rt[:, 1], ACT.Exp).then_inc(re_ready, 1)

            def silu(e, b, f):
                act.wait_ge(gu_done, 2 * e + f + 1)
                if f == 0:
                    act.wait_ge(dn_ready, 8 * e + 1)
                for c, (lo, hi_) in enumerate(CHUNKS):
                    mm = act.activation(A[b][:, f, lo:hi_], bank[4 * ((b + f) % 2) + c][:, 0:HALF], ACT.Silu)
                mm.then_inc(silu_ready, 1)

            def down_high(e, b, uses):
                act.wait_ge(wd_in[b], 16 * uses)
                for f in range(2):
                    act.activation(WH[b][f], WD[b][:, f, :], ACT.Copy).then_inc(wh_ready, 1)
                for f in range(2):
                    act.wait_ge(a_ready, 2 * e + f + 1)
                    act.activation(AH[b][:, f, :], A[b][:, f, :], ACT.Copy).then_inc(ah_ready, 1)

            silu(0, 0, 0)
            silu(0, 0, 1)
            down_high(0, 0, 1)
            with act.Fori(0, N_EXP // 2 - 1) as i:
                for b in (1, 0):
                    e = 2 * i + 2 - b
                    silu(e, b, 0)
                    gu_high(1 - b, i + 2)
                    silu(e, b, 1)
                    down_high(e, b, i + 2 - b)
            silu(N_EXP - 1, 1, 0)
            silu(N_EXP - 1, 1, 1)
            down_high(N_EXP - 1, 1, N_EXP // 2)
            act.wait_ge(gu_done, 2 * N_EXP)
            rms_scalar(act, 2, lambda k: X[:, k, :], lambda k: act.wait_ge(dn_ready, 8 * N_EXP + 2 + k))

        @block.vector
        def _(dve):
            step = Chain(dve, dve_step)
            dve.memset(ones[:], 1.0).then_inc(dve_const, 1)
            dve.wait_ge(small_in, 9 * 16)
            dve.wait_ge(consts_done, 3)
            dve.wait_ge(ms_ready, 1)
            rms_vector(dve, step, 0, lambda k: X[:, k, :], lambda k: H[:, k, :])

            dve.wait_ge(trig_ready, 1)
            step(dve.tensor_tensor(par(T1), prm[:, A_RE, :], par(DT), ALU.mult))
            dve.sem_inc(ang_ready, 1)
            step(dve.tensor_tensor(par(TH), prm[:, A_IM, :], par(DT), ALU.mult))
            step(dve.tensor_scalar(spi[:], par(TH), TURN / (2 * np.pi), None, ALU.mult))
            step(dve.tensor_copy(par(MF), spi[:]))
            for c in cody_waite(2 * np.pi / TURN, 8):
                step(dve.scalar_tensor_tensor(par(TH), par(MF), -c, par(TH), ALU.mult, ALU.add))
            step(dve.tensor_scalar(par(RR), par(TH), 1 / (2 * np.pi), None, ALU.mult))
            step(dve.tensor_scalar(spi[:], par(MF), 1.0 / TURN, None, ALU.mult))
            step(dve.tensor_copy(par(TQ), spi[:]))
            step(dve.scalar_tensor_tensor(par(MH), par(MF), 1.0 / TURN, par(TQ), ALU.mult, ALU.subtract))
            step(dve.tensor_tensor(par(UQ), par(MH), par(RR), ALU.add))
            step(dve.tensor_scalar(spi[:], par(UQ), 1.0, None, ALU.mult))
            step(dve.tensor_tensor(par(UQ), par(UQ), spi[:], ALU.subtract))
            step(dve.scalar_tensor_tensor(par(AQ), par(UQ), -1.0, par(UQ), ALU.mult, ALU.max))
            dve.sem_inc(ang_ready, 1)

            def angle(i, part, lag=1):
                if part == 0:
                    step(dve.tensor_scalar(kint, tvec, par(MH, i), None, ALU.mult), lag)
                elif part == 1:
                    step(dve.scalar_tensor_tensor(kf, tvec, par(MH, i), kint, ALU.mult, ALU.subtract), lag)
                elif part == 2:
                    step(dve.scalar_tensor_tensor(uu, tvec, par(RR, i), kf, ALU.mult, ALU.add), lag)
                elif part == 3:
                    step(dve.tensor_scalar(kint, uu, 1.0, None, ALU.mult), lag)
                elif part == 4:
                    step(dve.tensor_tensor(uu, uu, kint, ALU.subtract), lag)
                else:
                    step(dve.scalar_tensor_tensor(au, uu, -1.0, uu, ALU.mult, ALU.max), lag)

            for part in range(6):
                angle(0, part, lag=0)
            dve.sem_inc(ang_ready, 1)
            dve.wait_ge(trig_ready, 4)
            step(dve.tensor_tensor(par(ABR), par(MAG), par(CO), ALU.mult))
            step(dve.tensor_tensor(par(ABI), par(MAG), par(SI), ALU.mult))
            step(dve.tensor_scalar(par(AM1), par(ABR), -1.0, None, ALU.add))
            step(dve.tensor_tensor(par(DEN), prm[:, A_RE, :], prm[:, A_RE, :], ALU.mult))
            step(dve.tensor_tensor(par(T1), prm[:, A_IM, :], prm[:, A_IM, :], ALU.mult))
            step(dve.tensor_tensor(par(DEN), par(DEN), par(T1), ALU.add))
            step(dve.reciprocal(par(RDEN), par(DEN)))
            step(dve.tensor_tensor(par(T1), par(AM1), prm[:, A_RE, :], ALU.mult))
            step(dve.tensor_tensor(par(T2), par(ABI), prm[:, A_IM, :], ALU.mult))
            step(dve.tensor_tensor(par(T1), par(T1), par(T2), ALU.add))
            step(dve.tensor_tensor(par(CR), par(T1), par(RDEN), ALU.mult))
            step(dve.tensor_tensor(par(T1), par(ABI), prm[:, A_RE, :], ALU.mult))
            step(dve.tensor_tensor(par(T2), par(AM1), prm[:, A_IM, :], ALU.mult))
            step(dve.tensor_tensor(par(T1), par(T1), par(T2), ALU.subtract))
            step(dve.tensor_tensor(par(CI), par(T1), par(RDEN), ALU.mult))
            step(dve.tensor_scalar(CT[:, :, 1, :], CT[:, :, 1, :], -1.0, None, ALU.mult))
            dve.memset(hlast[:, :, :, 0], 0.0)

            for i in range(SN):
                more = i + 1 < SN
                s, c = sn[i % 2], cs[i % 2]
                dve.wait_ge(trig_ready, 6 + 2 * i)
                step(dve.tensor_scalar(pw, c, par(CR, i), None, ALU.mult), 1)
                if more:
                    angle(i + 1, 0)
                step(dve.tensor_scalar(qw, s, par(CR, i), None, ALU.mult), 1)
                step(dve.scalar_tensor_tensor(pw, s, par(CI, i), pw, ALU.mult, ALU.add), 1)
                if more:
                    angle(i + 1, 1)
                step(dve.scalar_tensor_tensor(qw, c, par(CI, i), qw, ALU.mult, ALU.subtract), 1)
                if more:
                    angle(i + 1, 2)
                dve.wait_ge(bu_ready, i + 1)
                R, I = bank[4][:, :], bank[5][:, :]
                step(dve.tensor_tensor(pR, pw, R, ALU.mult), 1)
                step(dve.tensor_tensor(pI, pw, I, ALU.mult), 1)
                step(dve.tensor_tensor(qI, qw, I, ALU.mult), 1)
                if more:
                    angle(i + 1, 3)
                step(dve.tensor_tensor(qR, qw, R, ALU.mult), 1)
                step(dve.tensor_tensor(vr, pR, qI, ALU.subtract), 1)
                dve.sem_inc(v_done, 1)
                if more:
                    angle(i + 1, 4)
                step(dve.tensor_tensor(vi, pI, qR, ALU.add), 1)
                mag = par(MAG, i).to_broadcast([P, SEQ])
                step(dve.tensor_tensor_scan(gr, mag, vr, 0.0, ALU.mult, ALU.add), 1)
                if more:
                    angle(i + 1, 5)
                step(dve.tensor_tensor_scan(gi, mag, vi, 0.0, ALU.mult, ALU.add), 1)
                if more:
                    dve.sem_inc(ang_ready, 1)
                step(dve.tensor_tensor(cgr, c, gr, ALU.mult), 1)
                step(dve.tensor_tensor(sgr, s, gr, ALU.mult), 1)
                step(dve.tensor_tensor(sgi, s, gi, ALU.mult), 1)
                step(dve.tensor_tensor(cgi, c, gi, ALU.mult), 1)
                if i >= 1:
                    dve.wait_ge(y_done, i)
                step(dve.tensor_tensor(hr, cgr, sgi, ALU.subtract), 1)
                step(dve.tensor_tensor(hi, sgr, cgi, ALU.add))
                dve.sem_inc(h_ready, 1)
                step(dve.tensor_copy(hlast[:, i, 0, 0:1], hr[:, SEQ - 1:SEQ]))
                step(dve.tensor_copy(hlast[:, i, 1, 0:1], hi[:, SEQ - 1:SEQ]))
                if i % 4 == 3:
                    c = i // 4
                    dve.wait_ge(y_done, i + 1)
                    step(dve.scalar_tensor_tensor(Z[:, c, 0:SEQ], Z[:, c, 0:SEQ], sdb[:, 0, c:c + 1],
                                                  bank[6][:, :], ALU.mult, ALU.add))
                    dve.sem_inc(skip_ready, 1)
            dve.wait_ge(ris_ready, SN)

            def row(k):
                return spar[:, k, :].unsqueeze(2).broadcast_to([P, SN, NB])

            def madd(dst, terms):
                t0, t1 = stmp[:, 0], stmp[:, 1]
                for n, (k, x, sub) in enumerate(terms):
                    step(dve.tensor_tensor(t0 if n == 0 else t1, x, row(k), ALU.mult))
                    if n:
                        last = n == len(terms) - 1
                        step(dve.tensor_tensor(dst if last else t0, t0, t1, ALU.subtract if sub else ALU.add))

            madd(hlast[:, :, 0, 1:], [(ABR, h0[:, :, 0], 0), (ABI, h0[:, :, 1], 1),
                                      (CR, RIs[:, :, 0], 0), (CI, RIs[:, :, 1], 1)])
            madd(hlast[:, :, 1, 1:], [(ABR, h0[:, :, 1], 0), (ABI, h0[:, :, 0], 0),
                                      (CR, RIs[:, :, 1], 0), (CI, RIs[:, :, 0], 0)])
            dve.sem_inc(hs_ready, 1)
            dve.wait_ge(ys_done, 1)
            for c in range(ST):
                step(dve.scalar_tensor_tensor(Z[:, c, SEQ:T], Z[:, c, SEQ:T], sdb[:, 0, c:c + 1],
                                              bank[6][:, NB * c:NB * c + NB], ALU.mult, ALU.add))
            dve.sem_inc(skip_ready, 1)
            dve.wait_ge(cst_in, 5 * 16)
            dve.wait_ge(sc_done, 1)
            sc3 = SCc.rearrange("p (a c) -> p a c", c=16)
            step(dve.tensor_tensor(SCc, bank[1][:, :], cc("bias_p"), ALU.add))
            step(dve.tensor_reduce(cmax[:], sc3, AX_X, ALU.max))
            step(dve.tensor_tensor(sc3, sc3, cmax[:].unsqueeze(2).broadcast_to([P, 32, 16]), ALU.subtract))
            dve.sem_inc(sc_ready, 1)
            dve.wait_ge(ec_ready, 1)
            sc4 = SCc.rearrange("p (q h c) -> p q h c", q=4, c=16)
            step(dve.tensor_tensor(sc4, sc4, cc("valid_p").rearrange("p (q c) -> p q c", q=4).unsqueeze(2)
                                   .broadcast_to([P, 4, HEADS, 16]), ALU.mult))
            dve.sem_inc(ecm_ready, 1)
            step(dve.tensor_reduce(csum[:], sc3, AX_X, ALU.add))
            step(dve.tensor_scalar(csum[:], csum[:], 1.0, None, ALU.max))
            step(dve.reciprocal(csum[:], csum[:]))
            for n in range(ST):
                dve.wait_ge(glu_sig, n + 1)
                if n == 0:
                    dve.wait_ge(glu_done, ST)
                step(dve.tensor_tensor(Z[:, n, :], Z[:, n, :], glu_g[:, n, :], ALU.mult))
            dve.sem_inc(yssm_ready, 1)

            dve.wait_ge(cst_in, 5 * 16)
            dve.wait_ge(vb_rep, 1)
            step(dve.tensor_tensor(VB.rearrange("p (m n) -> p m n", m=GRP),
                                   bank[3][:, 0:P].unsqueeze(1).broadcast_to([P, GRP, P]),
                                   cc("blocks").rearrange("p (m n) -> p m n", m=GRP), ALU.mult))
            dve.sem_inc(vb_ready, 1)

            def combine(qt):
                gate = Gn[:, qt].rearrange("p (b g m) -> p b m g", b=3, g=KVH)
                n = 16 * qt
                if qt == 0:
                    dve.wait_ge(gt_ready, 1)
                dve.wait_ge(e_ready, n + 16)
                step(dve.tensor_scalar(lsum[:, n:n + 16], lsum[:, n:n + 16], 1.0, None, ALU.max))
                step(dve.reciprocal(lsum[:, n:n + 16], lsum[:, n:n + 16]))
                w = wts[:].rearrange("p b (m g) -> p b m g", g=KVH)
                step(dve.tensor_tensor(w[:, 0], csum[:, 8 * qt:8 * qt + 8].rearrange("p (m g) -> p m g", g=KVH),
                                       gate[:, 0], ALU.mult))
                for b in range(2):
                    step(dve.tensor_tensor(w[:, 1 + b], lsum[:, n + 8 * b:n + 8 * b + 8]
                                           .rearrange("p (m g) -> p m g", g=KVH), gate[:, 1 + b], ALU.mult))

                def weighted(out, o, b):
                    step(dve.tensor_tensor(out.rearrange("p (h d) -> p h d", d=HD),
                                           o.rearrange("p (h d) -> p h d", d=HD),
                                           wts[:, b].unsqueeze(2).broadcast_to([P, HEADS, HD]), ALU.mult))

                dve.wait_ge(oc_done, qt + 1)
                if qt:
                    dve.wait_ge(yt_done, qt)
                else:
                    dve.wait_ge(ptc_done, 1)
                weighted(YN, bank[6][:, :], 0)
                dve.wait_ge(pv_done, n + 16)
                for b in range(2):
                    weighted(SCc, bank[4 + b][:, :], 1 + b)
                    step(dve.tensor_tensor(YN, YN, SCc, ALU.add))
                dve.sem_inc(y_nat, 1)

            for n in range(N_UNITS):
                qt, br, pos, L = unit(n)
                head = pos // 2 + GRP * (pos % 2)
                dve.wait_ge(s_done, n + 1)
                if n >= 2:
                    dve.wait_ge(e_ready, n - 1)
                s = Sb[n % 2][:, 0:L]
                step(dve.scalar_tensor_tensor(s, cc("dist")[:, SEQ - L:SEQ], -2.0**-(head + 1), bank[n % 2][:, 0:L],
                                              ALU.mult, ALU.add))
                dve.tensor_reduce(nmax[:, n:n + 1], s, AX_X, ALU.max, negate=True).then_inc(sb_ready, 1)
                if n % 16 == 1 and qt:
                    combine(qt - 1)
            combine(3)

            dve.wait_ge(qn_done, 1)
            step(dve.tensor_copy(QN, bank[6][0:NB, :]))
            dve.sem_inc(qn_ready, 1)
            dve.wait_ge(kn_done, 1)
            step(dve.tensor_copy(KN.rearrange("p s n -> p (s n)"), bank[7][0:NB, :]))
            step(dve.tensor_copy(pt8f[:], pt8[:]))
            step(dve.tensor_tensor(gmask[:], cc("gate_k", 24).unsqueeze(2).broadcast_to([24, 12, NB]),
                                   Gt[:, SEQ:T].unsqueeze(1).broadcast_to([24, 12, NB]), ALU.mult))
            dve.sem_inc(gm_ready, 1)
            dve.wait_ge(qr_done, 1)
            q4 = bank[5][:, :].rearrange("p (m g d) -> p m g d", m=GRP, g=KVH)
            step(dve.tensor_scalar(QR, q4[:, :, 0], cc("group")[:, 1:2], None, ALU.mult))
            step(dve.scalar_tensor_tensor(QR, q4[:, :, 1], cc("group")[:, 2:3], QR, ALU.mult, ALU.add))
            dve.wait_ge(gb_done, 1)
            step(dve.tensor_copy(gbc[:].rearrange("p a m b -> p (a m b)"), bank[4][:, 0:96]))
            dve.sem_inc(qr_ready, 1)

            dsel = small[:, 128:192]
            P3 = PROD.rearrange("p (n d) -> p n d", d=HD)
            KV = [[x.rearrange("p (n d) -> p n d", d=HD) for x in kv] for kv in KVT]

            def chunk_scores(br, m):
                step(dve.tensor_tensor(P3, KV[br][0], QR[:, m].unsqueeze(1).broadcast_to([P, SELB, HD]), ALU.mult))
                step(dve.tensor_reduce(SE[:, br, m, :], P3, AX_X, ALU.add))
                step(dve.scalar_tensor_tensor(SE[:, br, m, :], cc("dist_w") if br else dsel, -2.0**-(m + 1),
                                              SE[:, br, m, :], ALU.mult, ALU.add))

            def chunk_maxima(br):
                step(dve.tensor_reduce(stat[:, 0, GRP * br:GRP * br + GRP], SE[:, br], AX_X, ALU.max))
                step(dve.tensor_tensor(SE[:, br], SE[:, br], stat[:, 0, GRP * br:GRP * br + GRP].unsqueeze(2)
                                       .broadcast_to([P, GRP, SELB]), ALU.subtract))
                dve.sem_inc(se_ready, 1)

            def chunk_values(br):
                dve.wait_ge(ex_ready, 2 - br)
                step(dve.tensor_reduce(stat[:, 1, GRP * br:GRP * br + GRP], SE[:, br], AX_X, ALU.add))
                for m in range(GRP):
                    step(dve.tensor_tensor(P3, KV[br][1], SE[:, br, m].unsqueeze(2).broadcast_to([P, SELB, HD]),
                                           ALU.mult))
                    step(dve.tensor_reduce(O2[:, br, m, :], P3.rearrange("p n d -> p d n"), AX_X, ALU.add))
                dve.sem_inc(o2_ready, 1)

            dve.wait_ge(qs_done, 1)
            for g in range(KVH):
                step(dve.tensor_copy(sm[:, 0:64].rearrange("p (b g m) -> p b g m", g=KVH, m=GRP)[:, :, g, :],
                                     bank[6 + g][:, 0:32].rearrange("p (b m) -> p b m", m=GRP)))
            dve.sem_inc(qs_copied, 1)
            dve.wait_ge(kn_in_w, 64)
            dve.wait_ge(stored, 32)
            chunk_scores(1, 0)
            ps = sm[0:64, 64:192]
            dve.wait_ge(st_done, 1)
            step(dve.tensor_tensor(ps, bank[4][0:64, 0:P], cc("bias_s", 64), ALU.add))
            step(dve.tensor_reduce(small[0:64, 0:1], ps, AX_X, ALU.max, negate=True))
            dve.sem_inc(ss_ready, 1)
            chunk_scores(1, 1)
            dve.wait_ge(es_ready, 1)
            step(dve.tensor_scalar(small[0:64, 1:2], small[0:64, 1:2], 1.0, None, ALU.max))
            step(dve.reciprocal(small[0:64, 1:2], small[0:64, 1:2]))
            step(dve.tensor_scalar(ps, ps, small[0:64, 1:2], None, ALU.mult))
            dve.sem_inc(p_ready, 1)
            chunk_scores(1, 2)
            dve.wait_ge(imp_done, 1)
            imp = sm[0:16, 192:256]
            step(dve.tensor_reduce(imp, bank[5][0:16, 0:P].rearrange("p (s t) -> p s t", t=2), AX_X, ALU.add))
            step(dve.tensor_tensor(imp, imp, cc("force", 16), ALU.add))
            step(dve.max(small[0:16, 8:16], imp))
            step(dve.max_index(smi[:], small[0:16, 8:16], imp))
            step(dve.tensor_copy(small[0:16, 16:24], smi[:]))
            step(dve.memset(small[0:16, 23:24], 0.0))
            dve.sem_inc(idx_ready, 1)
            step(dve.tensor_copy(sm[:, 256:320], bank[4][:, 0:64]))
            dve.sem_inc(pts_ready, 1)
            chunk_scores(1, 3)
            dve.wait_ge(idx_done, 1)
            blk, pgf, half, row = (small[:, 32 + j:33 + j] for j in range(4))
            step(dve.tensor_tensor(small[:, 40:48], bank[7][:, 0:8], cc("slot"), ALU.mult))
            step(dve.tensor_reduce(blk, small[:, 40:48], AX_X, ALU.add))
            step(dve.tensor_copy(rowi[:, 1:2], blk))
            step(dve.tensor_scalar(rowi[:, 2:3], rowi[:, 1:2], 1, None, ALU.logical_shift_right))
            step(dve.tensor_copy(pgf, rowi[:, 2:3]))
            step(dve.scalar_tensor_tensor(half, pgf, -2.0, blk, ALU.mult, ALU.add))
            step(dve.tensor_scalar(small[:, 64:96], cc("iota"), pgf, None, ALU.is_equal))
            step(dve.tensor_tensor(small[:, 64:96], small[:, 64:96], bank[7][:, 8:40], ALU.mult))
            step(dve.tensor_reduce(row, small[:, 64:96], AX_X, ALU.add))
            step(dve.scalar_tensor_tensor(row, row, 2.0, half, ALU.mult, ALU.add))
            step(dve.scalar_tensor_tensor(row, row, 2.0, cc("group")[:, 0:1], ALU.mult, ALU.add))
            step(dve.tensor_copy(rowi[:, 0:1], row))
            dve.sem_inc(row_ready, 1)
            step(dve.tensor_scalar(half, blk, -float(SELB), float(PAST), ALU.mult, ALU.add))
            step(dve.tensor_scalar(dsel, cc("npos"), half, cc("keep"), ALU.add, ALU.mult))
            step(dve.tensor_tensor(dsel, dsel, cc("add7"), ALU.add))
            chunk_maxima(1)
            chunk_values(1)
            dve.wait_ge(kn_in, 64)
            for m in range(GRP):
                chunk_scores(0, m)
            chunk_maxima(0)
            chunk_values(0)
            dve.wait_ge(stt_done, 1)
            step(dve.tensor_copy(stT, bank[6][0:8, 0:256].rearrange("p (a n) -> p a n", a=2)))
            by_group = [stT[:, a].rearrange("p (g c) -> p g c", c=SLOTS) for a in range(2)]

            def per_group(x):
                return x.unsqueeze(2).broadcast_to([8, 16, SLOTS])

            step(dve.tensor_reduce(stW[:, 0], by_group[0], AX_X, ALU.max))
            step(dve.tensor_tensor(by_group[0], by_group[0], per_group(stW[:, 0]), ALU.subtract))
            dve.sem_inc(w8_ready, 1)
            dve.wait_ge(ew_ready, 1)
            step(dve.tensor_tensor(stT[:, 1], stT[:, 1], stT[:, 0], ALU.mult))
            step(dve.tensor_reduce(stW[:, 1], by_group[1], AX_X, ALU.add))
            step(dve.tensor_scalar(stW[:, 1], stW[:, 1], 1.0, None, ALU.max))
            step(dve.reciprocal(stW[:, 2], stW[:, 1]))
            step(dve.tensor_tensor(by_group[0], by_group[0], per_group(stW[:, 2]), ALU.mult))
            dve.sem_inc(wn_ready, 1)
            dve.wait_ge(wn_done, 1)
            step(dve.tensor_copy(wn[:], bank[6][:, 256:264]))
            o2v = O2.rearrange("p b m d -> p (b m) d")
            step(dve.tensor_tensor(o2v, o2v, wn[:].unsqueeze(2).broadcast_to([P, 8, HD]), ALU.mult))
            dve.sem_inc(o2_scaled, 1)
            dve.wait_ge(ot_done, 1)
            for g in range(KVH):
                r = slice(g * HD, g * HD + HD)
                step(dve.tensor_tensor(ya[r, 0], bank[5][r, P:P + 64].rearrange("p (b h) -> p h b", h=HEADS)
                                       [:, GRP * g:GRP * g + GRP, :], gbc[r, 0], ALU.mult))
            step(dve.tensor_tensor(ya[:, 1:3].rearrange("p a m b -> p (a m b)"), bank[7][:, 64:128],
                                   gbc[:, 1:3].rearrange("p a m b -> p (a m b)"), ALU.mult))
            step(dve.tensor_tensor(ya[:, 0], ya[:, 0], ya[:, 1], ALU.add))
            step(dve.tensor_tensor(Z[:, Z_CC:Z_CC + GRP, SEQ:T], ya[:, 0], ya[:, 2], ALU.add))
            dve.sem_inc(ya_ready, 1)

            dve.sem_inc(mo_ready, 2)
            dve.wait_ge(x_again, 48)
            with dve.Fori(0, 4) as i:
                for b in range(2):
                    dve.wait_ge(mo_done, 2 * i + b + 1)
                    for c, (lo, hi_) in enumerate(CHUNKS):
                        x = X[:, bass.ds(2 * i + b, 1), lo:hi_].rearrange("p o t -> p (o t)")
                        mm = dve.tensor_tensor(x, x, bank[2 * b + c][:, 0:HALF], ALU.add)
                    mm.then_inc(mo_ready, 1)
            def gu_low(e, b):
                for w in range(2):
                    dve.wait_ge(gh_ready, 2 * e + w + 1)
                    dve.tensor_tensor(GL[b][:, w], GU[b][:, w], wide(GH[b][w]), ALU.subtract).then_inc(gl_ready, 1)

            gu_low(0, 0)
            dve.wait_ge(mo_ready, KD + 2)
            dve.wait_ge(ms_ready, 2)
            rms_vector(dve, step, 1, lambda k: X[:, k, :], lambda k: H[:, k, :])

            dve.wait_ge(lt_done, 1)
            for c, (lo, hi_) in enumerate(CHUNKS):
                step(dve.tensor_scalar(lgT[:, lo:hi_], bank[6 + c][0:20, 0:HALF], rb[:], None, ALU.add))
            dve.sem_inc(lt_ready, 1)
            dve.wait_ge(lg_done, 1)
            step(dve.tensor_copy(lg, bank[6][0:104, 0:100].rearrange("p (j e) -> p j e", j=5)))
            dve.sem_inc(dn_ready, KD + 1)
            s5 = [small[0:104, 192 + 5 * j:197 + 5 * j] for j in range(12)]

            def over4(x):
                return x.unsqueeze(2).broadcast_to([104, 5, 4])

            def first_max(x, top, oh):
                step(dve.tensor_reduce(top, x, AX_X, ALU.max))
                step(dve.tensor_tensor(oh, x, over4(top), ALU.is_equal))
                step(dve.tensor_tensor(oh, oh, cc("rank", 104).unsqueeze(1).broadcast_to([104, 5, 4]), ALU.mult))
                step(dve.tensor_reduce(s5[11], oh, AX_X, ALU.max))
                step(dve.tensor_tensor(oh, oh, over4(s5[11]), ALU.is_equal))

            e_g, e_4, oh_g, oh_1, oh_2, le4, c4 = (rt[:, j] for j in range(7))
            t16 = rt[:, 8:12].rearrange("p a j k -> p (a j k)").rearrange("p (j g k) -> p j g k", j=5, g=4)
            c16 = comb.rearrange("p j (g k) -> p j g k", g=4)
            l16 = lg[:, :, 4:20].rearrange("p j (g k) -> p j g k", g=4)
            first_max(lg[:, :, 0:4], s5[0], oh_g)
            step(dve.tensor_tensor(e_g, lg[:, :, 0:4], over4(s5[0]), ALU.subtract))
            dve.sem_inc(rx_ready, 1)
            for j in range(5):
                step(dve.tensor_tensor(t16[:, j], l16[:, j], oh_g[:, j].unsqueeze(2).broadcast_to([104, 4, 4]),
                                       ALU.mult))
            for j in range(5):
                step(dve.tensor_reduce(le4[:, j], t16[:, j].rearrange("p g k -> p k g"), AX_X, ALU.add))
            step(dve.tensor_reduce(s5[1], le4, AX_X, ALU.max))
            step(dve.tensor_tensor(e_4, le4, over4(s5[1]), ALU.subtract))
            dve.sem_inc(rx_ready, 1)
            dve.wait_ge(re_ready, 1)
            step(dve.tensor_reduce(s5[2], e_g, AX_X, ALU.add))
            step(dve.reciprocal(s5[2], s5[2]))
            dve.wait_ge(re_ready, 2)
            first_max(e_4, s5[3], oh_1)
            step(dve.scalar_tensor_tensor(e_4, oh_1, -2.0, e_4, ALU.mult, ALU.add))
            first_max(e_4, s5[4], oh_2)
            step(dve.tensor_tensor(s5[5], s5[3], s5[4], ALU.add))
            step(dve.reciprocal(s5[5], s5[5]))
            step(dve.tensor_tensor(s5[5], s5[5], s5[2], ALU.mult))
            step(dve.tensor_tensor(s5[3], s5[3], s5[5], ALU.mult))
            step(dve.tensor_tensor(s5[4], s5[4], s5[5], ALU.mult))
            step(dve.tensor_tensor(oh_1, oh_1, over4(s5[3]), ALU.mult))
            step(dve.tensor_tensor(oh_2, oh_2, over4(s5[4]), ALU.mult))
            step(dve.tensor_tensor(c4, oh_1, oh_2, ALU.add))
            for j in range(5):
                step(dve.tensor_tensor(c16[:, j], oh_g[:, j].unsqueeze(2).broadcast_to([104, 4, 4]),
                                       c4[:, j].unsqueeze(1).broadcast_to([104, 4, 4]), ALU.mult))
            dve.sem_inc(comb_ready, 1)
            gu_low(1, 1)
            dve.wait_ge(ct_done, 1)
            step(dve.tensor_copy(combT[:, 0:416], bank[0][0:N_EXP, 0:416]))
            dve.sem_inc(ct_ready, 1)
            step(dve.tensor_copy(combT[:, 416:T], bank[1][0:N_EXP, 0:104]))
            dve.sem_inc(ct_ready, 1)


            def up_mul(e, b, split=True):
                for f in range(2):
                    dve.wait_ge(silu_ready, 2 * e + f + 1)
                    for c, (lo, hi_) in enumerate(CHUNKS):
                        a = A[b][:, f, lo:hi_]
                        mm = dve.tensor_tensor(a, a, bank[4 * ((b + f) % 2) + 2 + c][:, 0:HALF], ALU.mult)
                    mm.then_inc(up_ready, 1)
                    if f == 0 and split:
                        gu_low(e + 1, 1 - b)

            def add_down(e, b):
                with dve.Fori(0, 4) as n:
                    for j in range(2):
                        dve.wait_ge(dn_done, 8 * e + 2 * n + j + 1)
                        for c, (lo, hi_) in enumerate(CHUNKS):
                            x = X[:, bass.ds(2 * n + j, 1), lo:hi_].rearrange("p o t -> p (o t)")
                            mm = dve.tensor_tensor(x, x, bank[4 * (1 - b) + 2 * j + c][:, 0:HALF], ALU.add)
                        mm.then_inc(dn_ready, 1)

            up_mul(0, 0, split=False)
            with dve.Fori(0, N_EXP // 2 - 1) as i:
                for b in range(2):
                    up_mul(2 * i + 1 + b, 1 - b)
                    add_down(2 * i + b, b)
            up_mul(N_EXP - 1, 1, split=False)
            add_down(N_EXP - 2, 0)
            add_down(N_EXP - 1, 1)
            dve.wait_ge(dn_ready, 8 * N_EXP + 9)
            dve.wait_ge(ms_ready, 3)
            rms_vector(dve, step, 2, lambda k: X[:, k, :], lambda k: H[:, k, :])

        @block.tensor
        def _(pe):
            pe.wait_ge(dve_const, 1)
            rms_tensor(pe, 0)

            def z_tile(t):
                if t == 0:
                    pe.wait_ge(rms_ready, 2)
                pe.wait_ge(w_in[t % 2], 16 * (t // 2 + 1))
                if t >= 2:
                    pe.wait_ge(z_ready, t - 1)
                for k in range(KD):
                    if t == 0:
                        pe.wait_ge(norm_ready, k + 1)
                    for c, (a, b) in enumerate(CHUNKS):
                        mm = pe.matmul(bank[2 * (t % 2) + c][:, 0:HALF], W_RING[:, t % 2, k, :], H[:, k, a:b],
                                       start=(k == 0), stop=(k == KD - 1))
                mm.then_inc(z_done, 1)

            def bu(i):
                if i >= 1:
                    pe.wait_ge(v_done, i)
                    pe.wait_ge(ris_ready, i)
                r = slice(32 * (i % 4), 32 * (i % 4) + 32)
                for part in range(2):
                    w = BT[r, i // 4, part, :]
                    pe.matmul(bank[4 + part][:, :], w, Z[r, i // 4, 0:SEQ], start=True, stop=True,
                              tile_position=(32 * (i % 4), 0))
                    mm = pe.matmul(bank[7][:, NB * part:NB * part + NB], w, Z[r, i // 4, SEQ:T], start=True,
                                   stop=True, tile_position=(32 * (i % 4), 0))
                mm.then_inc(bu_ready, 1)

            def y(i):
                r = slice(32 * (i % 4), 32 * (i % 4) + 32)
                pe.wait_ge(h_ready, i + 1)
                if i >= 4:
                    pe.wait_ge(skip_ready, i // 4)
                pe.matmul(bank[6][r, :], CT[:, i, 0, :], hr, start=True, stop=False, tile_position=(0, r.start))
                pe.matmul(bank[6][r, :], CT[:, i, 1, :], hi, start=False, stop=True,
                          tile_position=(0, r.start)).then_inc(y_done, 1)

            def second(hid, n, kc, vc):
                for g in range(KVH):
                    pe.matmul(vc[0:n, g * HD:g * HD + HD], hid[:, g * n:g * n + n], w2[:, 1, :], start=True, stop=True)
                for g in range(KVH):
                    mm = pe.matmul(kc[g * HD:g * HD + HD, 0:n], w2[:, 0, :], hid[:, g * n:g * n + n], start=True,
                                   stop=True, tile_position=(0, g * HD))
                mm.then_inc(kc_done, 1)

            def prompt_compression():
                pe.wait_ge(cst_in, 5 * 16)
                pe.wait_ge(z_ready, NZ + 1)
                for v in range(2):
                    for r in range(16):
                        mm = pe.matmul(bank[3][v * HD:v * HD + HD, 0:1], w1[:, v, r, :], pe_t[:, v, r:r + 1],
                                       start=(r == 0), stop=(r == 15), tile_position=(0, v * HD))
                mm.then_inc(cb_done, 1)
                pe.wait_ge(xp_in, 8 * 16)
                for v in range(2):
                    for r in range(16):
                        mm = pe.matmul(bank[0][v * HD:v * HD + HD, 0:32], w1[:, v, r, :], XP[:, v, :, r, :],
                                       start=(r == 0), stop=(r == 15), tile_position=(0, v * HD))
                mm.then_inc(hid_done, 1)
                pe.wait_ge(cb_ready, 1)
                pe.wait_ge(hid_ready, 1)
                second(HID[:, 0], 16, bank[2], bank[3])

            def prompt_scores():
                pe.wait_ge(kc_ready, 2)
                for m in range(GRP):
                    mm = pe.matmul(bank[0][:, :], KB[:, m * P:(m + 1) * P], Z[:, Z_Q + m, 0:SEQ], start=(m == 0),
                                   stop=(m == GRP - 1))
                mm.then_inc(sct_done, 1)

            def scores_turn():
                pe.wait_ge(sct_ready, 1)
                for qt in range(4):
                    mm = pe.transpose(bank[1][:, qt * P:(qt + 1) * P], SCT[:, qt * P:(qt + 1) * P], identity)
                mm.then_inc(sc_done, 1)

            pe.wait_ge(small_in, 9 * 16)
            for t in range(3):
                z_tile(t)
            pe.wait_ge(z_ready, 3)
            bu(0)
            for i in range(SN):
                for t in beside[i]:
                    z_tile(t)
                if i == 9:
                    pe.wait_ge(wg_in, 16)
                    pe.wait_ge(z_ready, NZ - 1)
                    for k in range(KD):
                        for c, (a, b) in enumerate(CHUNKS):
                            mm = pe.matmul(bank[c][0:24, 0:HALF],
                                           wgt[:, k, :], H[:, k, a:b], start=(k == 0), stop=(k == KD - 1))
                    mm.then_inc(z_done, 1)
                if i + 1 < SN:
                    bu(i + 1)
                if i == SN - 2:
                    prompt_compression()
                if i == SN - 1:
                    prompt_scores()
                y(i)
            scores_turn()
            pe.wait_ge(v_done, SN)
            pe.wait_ge(ris_ready, SN)
            for b in range(2):
                for kt in range(4):
                    mm = pe.transpose(bank[4 + b][:, kt * P:(kt + 1) * P], Z[:, Z_KV + 3 + 2 * b, kt * P:(kt + 1) * P],
                                      identity)
                mm.then_inc(vt_done, 1)
            for qt in range(4):
                mm = pe.transpose(bank[7][:, 24 * qt:24 * qt + 24], Gt[:, qt * P:(qt + 1) * P], identity[0:24, 0:24])
            mm.then_inc(gt_done, 1)
            pe.wait_ge(skip_ready, ST)
            pe.wait_ge(hs_ready, 1)
            for i in range(SN):
                r = slice(32 * (i % 4), 32 * (i % 4) + 32)
                c = i // 4
                for part in range(2):
                    mm = pe.matmul(bank[6][r, NB * c:NB * c + NB], CT[:, i, part, :], hlast[:, i, part, 1:],
                                   start=(part == 0), stop=(part == 1), tile_position=(0, r.start))
            mm.then_inc(ys_done, 1)
            pe.wait_ge(gelu_ready, ST + 1)
            pe.wait_ge(z_ready, NZ + 1)
            for n in range(ST):
                if n == 1:
                    pe.wait_ge(vt_ready, 2)
                if n >= 2:
                    pe.wait_ge(glu_sig, n - 1)
                for k in range(ST):
                    for c, (a, b) in enumerate(CHUNKS):
                        mm = pe.matmul(bank[2 + 2 * (n % 2) + c][:, 0:HALF], w_glu[:, k, n * P:(n + 1) * P],
                                       Z[:, k, a:b], start=(k == 0), stop=(k == ST - 1))
                mm.then_inc(glu_done, 1)

            pe.wait_ge(glu_sig, ST)
            pe.matmul(bank[3][:, 0:P], cc("rep_c", 16), vcp[:], start=True, stop=True).then_inc(vb_rep, 1)

            def scores(n):
                qt, br, pos, L = unit(n)
                m, g = divmod(pos, 2)
                r = slice(g * HD, g * HD + HD)
                if n >= 2:
                    pe.wait_ge(sb_ready, n - 1)
                pe.matmul(bank[n % 2][:, 0:L], Z[r, Z_Q + m, qt * P:(qt + 1) * P], Z[r, Z_KV + 2 + 2 * br, 0:L],
                          start=True, stop=True, tile_position=(g * HD, 0)).then_inc(s_done, 1)

            def turn(n):
                L = unit(n)[3]
                pe.wait_ge(e_ready, n + 1)
                if n >= 2:
                    pe.wait_ge(pt_ready, n - 1)
                for k in range(L // P):
                    mm = pe.transpose(bank[2 + n % 2][:, k * P:(k + 1) * P], Ex[n % 2][:, k * P:(k + 1) * P], identity)
                mm.then_inc(t_done, 1)

            def pv(n):
                qt, br, pos, L = unit(n)
                g = pos % 2
                pe.wait_ge(pt_ready, n + 1)
                if n == 0:
                    pe.wait_ge(vt_ready, 2)
                if n % 16 == 0 and qt:
                    pe.wait_ge(y_nat, qt)
                for k in range(L // P):
                    mm = pe.matmul(bank[4 + br][:, pos * HD:pos * HD + HD], PT[n % 2][:, k * P:(k + 1) * P],
                                   VN[:, br, k, g * HD:g * HD + HD], start=(k == 0), stop=(k == L // P - 1))
                mm.then_inc(pv_done, 1)

            def out_c(qt):
                pe.wait_ge(kc_ready, 4 + 4 * qt)
                pe.matmul(bank[6][:, :], PTC[:, qt * P:(qt + 1) * P], VB, start=True, stop=True).then_inc(oc_done, 1)

            def y_turn(qt):
                pe.wait_ge(y_nat, qt + 1)
                pe.wait_ge(kc_ready, 2 + 4 * (qt + 1))
                for m in range(GRP):
                    mm = pe.transpose(bank[7][:, m * P:(m + 1) * P], YN[:, m * P:(m + 1) * P], identity)
                mm.then_inc(yt_done, 1)

            pe.wait_ge(sc_ready, 1)
            scores(0)
            pe.wait_ge(ecm_ready, 1)
            pe.wait_ge(gt_ready, 1)
            for qt in range(4):
                mm = pe.transpose(bank[7][:, qt * P:(qt + 1) * P], SCc[:, qt * P:(qt + 1) * P], identity)
            mm.then_inc(ptc_done, 1)
            pe.wait_ge(ptc_ready, 1)
            pe.wait_ge(vb_ready, 1)
            pe.wait_ge(yconv_ready, 1)

            def hidden_part(smp, part, parts):
                b = smp % 2
                if part == 0:
                    pe.wait_ge(pages_in[b], 8 * PAGES * (smp // 2 + 1))
                    pe.wait_ge(odd_pages_in[b], 8 * PAGES * (smp // 2 + 1))
                    if smp >= 2:
                        pe.wait_ge(kc_ready, 2 * smp)
                    if b == 1 and smp > 1:
                        pe.wait_ge(yt_ready, smp // 2)
                    if b == 0 and smp:
                        pe.wait_ge(y_nat, smp // 2)
                for at in range(32 * part // parts, 32 * (part + 1) // parts):
                    v, r = divmod(at, 16)
                    mm = pe.matmul(bank[6 + b][v * HD:v * HD + HD, 0:2 * NCB], w1[:, v, r, :],
                                   page[b][:, :, v, :, r, :].rearrange("p g h c -> p h g c"), start=(r == 0),
                                   stop=(r == 15), tile_position=(0, v * HD))
                if part == parts - 1:
                    mm.then_inc(hid_done, 1)

            def second_layer(smp):
                pe.wait_ge(hid_ready, smp + 2)
                b = smp % 2
                second(HID[:, b], NCB, bank[6 + b][:, 2 * NCB:3 * NCB], bank[6 + b][:, 3 * NCB:4 * NCB])

            for n in range(N_UNITS):
                qt, at = divmod(n, 16)
                if n + 1 < N_UNITS:
                    scores(n + 1)
                if qt and at == 1:
                    hidden_part(2 * qt - 1, 8, 9)
                turn(n)
                if n >= 1:
                    pv(n - 1)
                if qt and at == 0:
                    hidden_part(2 * qt - 1, 7, 9)
                if qt and at == 3:
                    second_layer(2 * qt - 1)
                if qt and at == 4:
                    y_turn(qt - 1)
                if 2 <= at < 9:
                    hidden_part(2 * qt, at - 2, 7)
                if at >= 9:
                    hidden_part(2 * qt + 1, at - 9, 9)
                if at == 10:
                    second_layer(2 * qt)
                if at == 14:
                    out_c(qt)
            pv(N_UNITS - 1)
            for part in (7, 8):
                hidden_part(NB - 1, part, 9)
            second_layer(NB - 1)
            y_turn(3)

            for m in range(GRP):
                mm = pe.transpose(bank[6][0:NB, m * P:(m + 1) * P], Z[:, Z_Q + m, SEQ:T], identity)
            mm.then_inc(qn_done, 1)
            pe.wait_ge(yt_ready, 4)
            for j in range(4):
                mm = pe.transpose(bank[7][0:NB, j * P:(j + 1) * P], Z[:, Z_KV + 2 + j, SEQ:T], identity)
            mm.then_inc(kn_done, 1)
            pe.wait_ge(qn_ready, 1)
            pe.matmul(bank[5][:, :], cc("rep8", NB), QN, start=True, stop=True).then_inc(qr_done, 1)
            pe.wait_ge(gm_ready, 1)
            pe.matmul(bank[4][:, 0:96], cc("gate_g", 24), gmask[:].rearrange("p a b -> p (a b)"), start=True,
                      stop=True).then_inc(gb_done, 1)
            pe.wait_ge(qr_ready, 1)

            def merge(br, y0, first=0, last=4):
                nk = BRANCH_K[br]
                with pe.Fori(first, last) as i:
                    for b in range(2):
                        q = 8 * br + 2 * i + b
                        pe.wait_ge(w_in[b], 16 * (NZ // 2 + 4 * br + i + 1))
                        pe.wait_ge(mz_ready, q + 1)
                        for k in range(KD):
                            for c, (lo, hi_) in enumerate(CHUNKS):
                                mm = pe.matmul(bank[c][:, 0:HALF], W_RING[:, b, k, :], H[:, k, lo:hi_], start=(k == 0),
                                               stop=(k == KD - 1))
                        mm.then_inc(mz_done, 1)
                        pe.wait_ge(wb_in[b], 16 * (4 * br + i + 1))
                        pe.wait_ge(mb_ready, q + 1)
                        for k in range(nk):
                            for c, (lo, hi_) in enumerate(CHUNKS):
                                mm = pe.matmul(bank[2 + c][:, 0:HALF], WB[:, b, k, :], Z[:, y0 + k, lo:hi_],
                                               start=(k == 0), stop=(k == nk - 1))
                        mm.then_inc(mb_done, 1)

            pe.wait_ge(kc_ready, 2 + 2 * NB)
            for g in range(KVH):
                r = slice(g * HD, g * HD + HD)
                for b in range(NB):
                    mm = pe.matmul(bank[6 + g][:, GRP * b:GRP * b + GRP], KCT[r, b, :], Z[r, Z_Q:Z_Q + GRP, SEQ + b],
                                   start=True, stop=True, tile_position=(g * HD, 0))
            mm.then_inc(qs_done, 1)
            pe.wait_ge(qs_copied, 1)
            pe.transpose(bank[4][0:64, 0:P], sm[:, 0:64], identity).then_inc(st_done, 1)
            merge(0, Z_U, 0, 1)
            pe.wait_ge(p_ready, 1)
            pe.transpose(bank[4][:, 0:64], sm[0:64, 64:192], identity[0:64, 0:64])
            pe.matmul(bank[5][0:16, 0:P], cc("sum_g", 64), sm[0:64, 64:192], start=True, stop=True)\
                .then_inc(imp_done, 1)
            merge(0, Z_U, 1, 2)
            pe.wait_ge(idx_ready, 1)
            pe.matmul(bank[7][:, 0:8], cc("rep16", 16), small[0:16, 16:24], start=True, stop=True)
            pe.matmul(bank[7][:, 8:40], cc("rep8", NB), pt8f[:], start=True, stop=True).then_inc(idx_done, 1)
            pe.wait_ge(pts_ready, 1)
            for b in range(NB):
                mm = pe.matmul(bank[5][:, P + HEADS * b:P + HEADS * b + HEADS], VC[:, b, :],
                               sm[:, 256 + HEADS * b:256 + HEADS * b + HEADS], start=True, stop=True)
            mm.then_inc(ocs_done, 1)

            merge(0, Z_U, 2, 4)
            merge(1, Z_CB)
            pe.wait_ge(o2_ready, 2)
            for a in range(2):
                mm = pe.transpose(bank[6][0:8, a * P:(a + 1) * P], stat[:, a, :], identity)
            mm.then_inc(stt_done, 1)
            pe.wait_ge(wn_ready, 1)
            pe.transpose(bank[6][:, 256:264], stT[:, 0, :], identity[0:8, 0:8]).then_inc(wn_done, 1)
            pe.wait_ge(o2_scaled, 1)
            for br in range(2):
                for m in range(GRP):
                    for g in range(KVH):
                        at = 64 + (GRP * br + m) * NB
                        mm = pe.matmul(bank[7][g * HD:g * HD + HD, at:at + NB], O2[:, br, m, :],
                                       cc("sel_g").rearrange("p (g b) -> p g b", g=KVH)[:, g, :], start=True, stop=True,
                                       tile_position=(0, g * HD))
            mm.then_inc(ot_done, 1)
            pe.wait_ge(ya_ready, 1)
            merge(2, Z_CC)
            pe.wait_ge(mm_ready, 26)
            pe.wait_ge(mb_ready, 25)
            with pe.Fori(0, 4) as i:
                for b in range(2):
                    pe.wait_ge(w_in[b], 16 * (NZ // 2 + 12 + i + 1))
                    pe.wait_ge(mo_ready, 2 * i + b + 1)
                    for k in range(KD):
                        for c, (lo, hi_) in enumerate(CHUNKS):
                            mm = pe.matmul(bank[2 * b + c][:, 0:HALF], W_RING[:, b, k, :], M[:, k, lo:hi_],
                                           start=(k == 0), stop=(k == KD - 1))
                    mm.then_inc(mo_done, 1)

            rms_tensor(pe, 1)
            pe.wait_ge(x_again, 48)
            for k in range(KD):
                pe.wait_ge(norm_ready, KD + k + 1)
                for c, (lo, hi_) in enumerate(CHUNKS):
                    mm = pe.matmul(bank[6 + c][0:20, 0:HALF], rw[:, k, :], H[:, k, lo:hi_], start=(k == 0),
                                   stop=(k == KD - 1))
            mm.then_inc(lt_done, 1)
            pe.wait_ge(lt_ready, 1)
            for j in range(5):
                mm = pe.transpose(bank[6][0:104, 20 * j:20 * j + 20], lgT[:, 104 * j:104 * j + 104],
                                  identity[0:20, 0:20])
            mm.then_inc(lg_done, 1)
            def gate_up(e, b):
                pe.wait_ge(gl_ready, 2 * e + 2)
                for f in range(2):
                    if f == 1:
                        pe.wait_ge(dn_ready, 8 * e + 1)
                    elif not (isinstance(e, int) and e == 0):
                        pe.wait_ge(up_ready, 2 * e)
                    for w in range(2):
                        for j, (wt, h) in enumerate(((GH[b][w], HH), (GL[b][:, w], HH), (GH[b][w], HL))):
                            for k in range(KD):
                                if isinstance(e, int) and e == f == w == 0 and j != 1:
                                    pe.wait_ge((hh_ready, None, hl_ready)[j], k + 1)
                                for c, (lo, hi_) in enumerate(CHUNKS):
                                    mm = pe.matmul(bank[4 * ((b + f) % 2) + 2 * w + c][:, 0:HALF],
                                                   wt[:, k, f * P:(f + 1) * P], h[:, k, lo:hi_],
                                                   start=(k == j == 0), stop=(k == KD - 1 and j == 2))
                    mm.then_inc(gu_done, 1)

            def down(e, b):
                pe.wait_ge(wl_ready, 2 * e + 2)
                pe.wait_ge(al_ready, 2 * e + 2)
                for n in range(KD):
                    if n >= 2:
                        pe.wait_ge(dn_ready, 8 * e + n - 1 + 9)
                    for f in range(2):
                        high, low = (x[:, n * P:(n + 1) * P] for x in (WH[b][f], WL[b][:, f]))
                        for j, (wt, a) in enumerate(((high, AH[b]), (high, AL[b]), (low, AH[b]))):
                            for c, (lo, hi_) in enumerate(CHUNKS):
                                mm = pe.matmul(bank[4 * (1 - b) + 2 * (n % 2) + c][:, 0:HALF], wt,
                                               a[:, f, lo:hi_], start=(f == j == 0), stop=(f == 1 and j == 2))
                    mm.then_inc(dn_done, 1)

            gate_up(0, 0)
            pe.wait_ge(silu_ready, 1)
            pe.wait_ge(comb_ready, 1)
            for j in range(5):
                out = bank[0][0:N_EXP, 104 * j:104 * j + 104] if j < 4 else bank[1][0:N_EXP, 0:104]
                mm = pe.transpose(out, comb[:, j, :], identity[0:104, 0:104])
            mm.then_inc(ct_done, 1)
            with pe.Fori(0, N_EXP // 2 - 1) as i:
                gate_up(2 * i + 1, 1)
                pe.wait_ge(up_ready, 4 * i + 3)
                down(2 * i, 0)
                gate_up(2 * i + 2, 0)
                pe.wait_ge(up_ready, 4 * i + 5)
                down(2 * i + 1, 1)
            gate_up(N_EXP - 1, 1)
            pe.wait_ge(up_ready, 2 * N_EXP - 1)
            down(N_EXP - 2, 0)
            pe.wait_ge(up_ready, 2 * N_EXP)
            down(N_EXP - 1, 1)
            rms_tensor(pe, 2)


def tiles(w):
    k, n = w.shape
    return w.reshape(k // P, P, n // P, P).transpose(2, 1, 0, 3)


def rows(v):
    return np.moveaxis(v.reshape(*v.shape[:-1], v.shape[-1] // P, P), -1, 0)


def lay_out(i):
    x = np.concatenate([i["x_prompt"][0], i["x_sample"][:, 0]])
    w = i["w_in"][0]
    qcols = [384 + h * HD + d for j in range(GRP) for h in (j, j + GRP) for d in range(HD)]
    cols = np.concatenate([np.arange(0, 384), qcols, np.arange(896, 1664), np.arange(1688, 2840)])
    BT = np.zeros((ST, 4, 2, SC, 2, 2, 64), np.float32)
    CT = np.zeros((SN, 2, 64, 2, 2, SC), np.float32)
    for part, (b, c) in enumerate((("ssm_b_re", "ssm_c_re"), ("ssm_b_im", "ssm_c_im"))):
        b, c = i[b][0].reshape(ST, 4, 2, 64, SC), i[c][0].reshape(SN, 2, SC, 64)
        for g in range(2):
            BT[:, :, g, :, part, g, :] = b[:, :, g].transpose(0, 1, 3, 2)
            CT[:, g, :, part, g, :] = c[:, g].transpose(0, 2, 1)

    def state(v):
        return v.reshape(SN, 2, 64).transpose(1, 2, 0).reshape(P, SN)

    ldt = np.repeat(i["ssm_log_dt"][0], 64)
    return {
        "xT": x.T.reshape(KD, P, T).transpose(1, 0, 2),
        "gains": rows(np.stack([i["norm_attn_g"][0], i["norm_ffn_g"][0], i["norm_final_g"]])),
        "w_z": tiles(w[:, cols])[Z_ORDER],
        "w_gates": w[:, 1664:1688].reshape(KD, P, 24).transpose(1, 0, 2),
        "prm": np.stack([state(i["ssm_a_re"][0]), state(i["ssm_a_im"][0]), state(ldt)], 1),
        "BT": BT.transpose(1, 2, 3, 0, 4, 5, 6).reshape(P, ST, 2, P),
        "CT": CT.transpose(1, 2, 0, 3, 4, 5).reshape(P, SN, 2, 32),
        "h0": i["state_ssm"][0].reshape(NB, SN, 2, 64, 2).transpose(2, 3, 1, 4, 0).reshape(P, SN, 2, NB),
        "sdb": rows(np.stack([i["ssm_d"][0], i["ssm_b_glu"][0]])),
        "w_glu": i["ssm_w_glu"][0].reshape(ST, P, SG * SC).transpose(1, 0, 2),
        "cw": i["conv_w"][0].reshape(3, ST, P).transpose(2, 1, 0),
        "cst": CST_ARRAY,
        "ptab": i["page_table"].reshape(1, -1),
        "pt8": i["page_table"],
        "cmp": i["cache_kv"][0][:, :, 0:2].reshape(N_POOL, 4, 16, 2, 2, KVH, HD).transpose(0, 3, 6, 4, 5, 2, 1)
        .reshape(N_POOL, P, 256),
        "w1": i["cmp_w1"][0].reshape(2, 16, 2, HD, HD).transpose(2, 3, 0, 1, 4).reshape(P, 2, 16, HD),
        "w2": np.stack([np.pad(i["cmp_w2"][0][v], ((HD * v, HD - HD * v), (0, 0))) for v in range(2)], 1),
        "pe": i["cmp_pe"][0].reshape(2, 16, 2, HD).transpose(2, 3, 0, 1).reshape(P, 2, 16),
        "win": i["cache_win"][0].transpose(2, 0, 3, 1, 4).reshape(2, -1),
        "kslc": i["cache_kv"][0][:, :, 2].reshape(N_POOL, 2, SELB, KVH, HD).transpose(0, 1, 3, 2, 4)
        .reshape(-1, SELB * HD),
        "vslc": i["cache_kv"][0][:, :, 3].reshape(N_POOL, 2, SELB, KVH, HD).transpose(0, 1, 3, 2, 4)
        .reshape(-1, SELB * HD),
        "w_m": np.concatenate([tiles(w[:, 2840 + j * D:2840 + (j + 1) * D]) for j in (0, 2, 1)]),
        "w_b0": tiles(i["w_br_ssm"][0]),
        "w_b1": tiles(i["w_br_conv"][0]),
        "w_b2": tiles(i["w_br_attn"][0][np.array(qcols) - 384]),
        "w_o": tiles(i["w_out"][0]),
        "w_r": np.concatenate([i["w_router_group"][0], i["w_router_expert"][0]], 1).reshape(KD, P, 20)
        .transpose(1, 0, 2),
        "b_r": np.concatenate([i["b_router_group"][0], i["b_router_expert"][0]])[:, None],
        "w_gu": np.stack([i["moe_w_gate"][0], i["moe_w_up"][0]], 1).reshape(N_EXP, 2, KD, P, FF)
        .transpose(0, 3, 1, 2, 4),
        "w_d": i["moe_w_down"][0].reshape(N_EXP, 2, P, D).transpose(0, 2, 1, 3),
        "cprev": i["state_conv"][0].reshape(NB, 2, ST, P).transpose(3, 2, 1, 0),
    }


OUTS = {
    "o_yT": (P, KD, T),
    "o_win": (2, P, SELB * HD),
    "o_kvT": (6, P, T),
    "o_clast": (P, ST, 2, NB + 1),
    "o_hlast": (P, SN, 2, NB + 1),
}


def give_back(r):
    kv = r["o_kvT"].reshape(6, KVH, HD, T)
    hl = r["o_hlast"].reshape(2, 64, SN, 2, NB + 1).transpose(4, 2, 0, 1, 3).reshape(NB + 1, SG, 64, 2)
    cl = r["o_clast"].transpose(3, 2, 1, 0).reshape(NB + 1, 2, SG * SC)
    kv_rows = kv[:4].transpose(3, 0, 1, 2)
    y = r["o_yT"].transpose(2, 1, 0).reshape(T, D)
    win_p = kv[4:].transpose(3, 0, 1, 2)
    win_s = r["o_win"].reshape(2, NB, KVH, WINDOW, HD).transpose(1, 3, 0, 2, 4)
    return tuple(np.ascontiguousarray(a) for a in (
        y[None, :SEQ], y[SEQ:, None], kv_rows[None, None, :SEQ], kv_rows[None, SEQ:, None], win_p[None, None, :SEQ],
        win_s[None], hl[None, :1], hl[None, 1:], cl[None, :1], cl[None, 1:]))


def kernel(**inputs):
    import concourse.bacc as bacc
    from concourse.bass_utils import run_bass_kernel_spmd

    arrays = {k: np.ascontiguousarray(v) for k, v in lay_out({k: np.asarray(v) for k, v in inputs.items()}).items()}
    nc = bacc.Bacc("TRN2", target_bir_lowering=False, num_devices=1)
    io = {k: nc.dram_tensor("in_" + k, v.shape, mybir.dt.from_np(v.dtype), kind="ExternalInput").ap()
          for k, v in arrays.items()}
    io |= {k: nc.dram_tensor(k, s, F32, kind="ExternalOutput").ap() for k, s in OUTS.items()}
    io["comb"] = nc.dram_tensor("comb", (N_EXP, T), F32, kind="Internal").ap()
    build(nc, io)
    r = run_bass_kernel_spmd(nc, [{"in_" + k: v for k, v in arrays.items()}], core_ids=[0]).results[0]
    return give_back(r)
```
